# Optimizing a Trainium2 kernel written in Bass

```python
import jax, jax.numpy as jnp
from jax import lax
import numpy as np

D_MODEL = 1024
BATCH = 1
SEQ = 1024
DEPTH = 1

N_ATTN_HEADS = 8
HEAD_DIM = 64
ATTN_WIDTH = N_ATTN_HEADS * HEAD_DIM
CONV_GROUPS = 8
CONV_WIDTH = 512
CONV_K = 3
D_FF = 4 * D_MODEL
PLE_DIM = 256
Q_BLOCK = 128
EPS = 1e-6
SPLIT_SIZES = (ATTN_WIDTH, ATTN_WIDTH, ATTN_WIDTH, CONV_WIDTH, CONV_WIDTH, CONV_WIDTH, D_MODEL, D_MODEL)
SPLIT_POINTS = tuple(int(v) for v in np.cumsum(SPLIT_SIZES)[:-1])
D_IN = sum(SPLIT_SIZES)


def rms_norm(x, g):
    xf = x.astype(jnp.float32)
    var = jnp.mean(xf * xf, axis=-1, keepdims=True)
    return (xf * lax.rsqrt(var + EPS) * g.astype(jnp.float32)).astype(x.dtype)

def stick_breaking_attention(q, k, v):
    b, h, s, dh = q.shape
    nblk = s // Q_BLOCK
    scale = dh ** -0.5
    kf = k.astype(jnp.float32)
    vf = v.astype(jnp.float32)
    q_blocks = q.reshape(b, h, nblk, Q_BLOCK, dh).transpose(2, 0, 1, 3, 4)
    key_pos = jnp.arange(s, dtype=jnp.int32)
    starts = jnp.arange(nblk, dtype=jnp.int32) * Q_BLOCK

    def block(args):
        qb, start = args
        z = jnp.einsum('bhqd,bhkd->bhqk', qb.astype(jnp.float32), kf) * scale
        q_pos = start + jnp.arange(Q_BLOCK, dtype=jnp.int32)
        causal = key_pos[None, :] < q_pos[:, None]
        log_beta = jax.nn.log_sigmoid(z)
        log_keep = jnp.where(causal, log_beta - z, 0.0)
        between = lax.cumsum(log_keep, axis=3, reverse=True) - log_keep
        w = jnp.where(causal, jnp.exp(log_beta + between), 0.0)
        return jnp.einsum('bhqk,bhkd->bhqd', w, vf)

    out = lax.map(block, (q_blocks, starts))
    return out.transpose(1, 2, 0, 3, 4).reshape(b, h, s, dh).astype(q.dtype)

def causal_depthwise_conv(u, w):
    c = u.shape[-1]
    return lax.conv_general_dilated(
        u, w[:, None, :].astype(u.dtype), window_strides=(1,),
        padding=((CONV_K - 1, 0),), dimension_numbers=('NWC', 'WIO', 'NWC'),
        feature_group_count=c)

def first_inputs(seed: int = 0) -> dict:
    key = jax.random.key(seed)
    ks = jax.random.split(key, 20)
    f32 = jnp.float32

    def nrm(k, shape, fan_in):
        return jax.random.normal(k, shape, f32) * (fan_in ** -0.5)

    def gain(k, shape):
        return jnp.ones(shape, f32) + 0.05 * jax.random.normal(k, shape, f32)

    return {
        'x': jax.random.normal(ks[0], (BATCH, SEQ, D_MODEL), f32),
        'p': jax.random.normal(ks[1], (DEPTH, BATCH, SEQ, PLE_DIM), f32),
        'g_pre_mix': gain(ks[2], (DEPTH, D_MODEL)),
        'w_in': nrm(ks[3], (DEPTH, D_MODEL, D_IN), D_MODEL),
        'b_gate': 0.1 * jax.random.normal(ks[4], (DEPTH, 2 * D_MODEL), f32),
        'w_conv': nrm(ks[5], (DEPTH, CONV_K, CONV_WIDTH), CONV_K),
        'w_attn_out': nrm(ks[6], (DEPTH, ATTN_WIDTH, D_MODEL), ATTN_WIDTH),
        'w_conv_out': nrm(ks[7], (DEPTH, CONV_WIDTH, D_MODEL), CONV_WIDTH),
        'w_o': nrm(ks[8], (DEPTH, D_MODEL, D_MODEL), D_MODEL),
        'g_post_mix': gain(ks[9], (DEPTH, D_MODEL)),
        'g_pre_mlp': gain(ks[10], (DEPTH, D_MODEL)),
        'w_up': nrm(ks[11], (DEPTH, D_MODEL, D_FF), D_MODEL),
        'w_down': nrm(ks[12], (DEPTH, D_FF, D_MODEL), D_FF),
        'g_post_mlp': gain(ks[13], (DEPTH, D_MODEL)),
        'g_ple': gain(ks[14], (DEPTH, D_MODEL)),
        'w_ple_gate': nrm(ks[15], (DEPTH, D_MODEL, D_MODEL), D_MODEL),
        'w_ple_proj': nrm(ks[16], (DEPTH, PLE_DIM, D_MODEL), PLE_DIM),
    }

def first_block(x, p, g_pre_mix, w_in, b_gate, w_conv, w_attn_out, w_conv_out, w_o,
              g_post_mix, g_pre_mlp, w_up, w_down, g_post_mlp, g_ple, w_ple_gate, w_ple_proj):
    bsz, seq, _ = x.shape
    for i in range(DEPTH):
        h = rms_norm(x, g_pre_mix[i])
        proj = h @ w_in[i]
        q, k, v, cb, cc, cu, ga, gc = jnp.split(proj, SPLIT_POINTS, axis=-1)

        def heads(t):
            return t.reshape(bsz, seq, N_ATTN_HEADS, HEAD_DIM).transpose(0, 2, 1, 3)

        o = stick_breaking_attention(heads(q), heads(k), heads(v))
        o = o.transpose(0, 2, 1, 3).reshape(bsz, seq, ATTN_WIDTH)
        y_attn = o @ w_attn_out[i]

        y_conv = (cb * causal_depthwise_conv(cc * cu, w_conv[i])) @ w_conv_out[i]

        gates = jax.nn.sigmoid(jnp.concatenate([ga, gc], axis=-1) + b_gate[i])
        gate_attn, gate_conv = jnp.split(gates, 2, axis=-1)
        mixed = (gate_attn * y_attn + gate_conv * y_conv) @ w_o[i]
        x = x + rms_norm(mixed, g_post_mix[i])

        h = rms_norm(x, g_pre_mlp[i])
        f = jnp.square(jax.nn.relu(h @ w_up[i])) @ w_down[i]
        x = x + rms_norm(f, g_post_mlp[i])

        ple_gate = jax.nn.sigmoid(rms_norm(x, g_ple[i]) @ w_ple_gate[i])
        x = x + ple_gate * (p[i] @ w_ple_proj[i])
    return x


NSA_HEADS = 8
NSA_KV = 2
NSA_REP = NSA_HEADS // NSA_KV
RWKV_HEADS = 8
NSA_WIDTH = NSA_HEADS * HEAD_DIM
RWKV_WIDTH = RWKV_HEADS * HEAD_DIM
MIX_WIDTH = NSA_WIDTH + RWKV_WIDTH
KV_WIDTH = NSA_KV * HEAD_DIM
ROPE_DIM = HEAD_DIM // 4
ROPE_THETA = 500000.0
CMP_BLOCK = 32
CMP_STRIDE = 16
CMP_HIDDEN = 256
SEL_BLOCK = 64
SEL_TOPK = 8
WINDOW = 512
DECAY_RANK = 64
ICLR_RANK = 64
RWKV_SHIFT_WIDTH = 3 * RWKV_WIDTH + DECAY_RANK + ICLR_RANK
IN_SIZES = (NSA_WIDTH, KV_WIDTH, KV_WIDTH, KV_WIDTH, KV_WIDTH, KV_WIDTH, KV_WIDTH,
            3 * NSA_HEADS, NSA_WIDTH, RWKV_SHIFT_WIDTH, RWKV_WIDTH)
IN_WIDTH = sum(IN_SIZES)
SCALE = HEAD_DIM ** -0.5
RMS_EPS = 1e-6
GN_EPS = 64e-5
NEG_INF = -1e30
FORCE_BONUS = 1e3


def _split(h, sizes):
    idx = np.cumsum(sizes)[:-1].tolist()
    return jnp.split(h, idx, axis=-1)

def rms_norm_2(x, g):
    xf = x.astype(jnp.float32)
    y = xf * lax.rsqrt(jnp.mean(xf * xf, axis=-1, keepdims=True) + RMS_EPS)
    return (y * g.astype(jnp.float32)).astype(x.dtype)

def partial_rope(t, pos):
    half = ROPE_DIM // 2
    inv = ROPE_THETA ** (-jnp.arange(half, dtype=jnp.float32) / half)
    ang = pos.astype(jnp.float32)[:, None] * inv[None, :]
    cos, sin = jnp.cos(ang), jnp.sin(ang)
    tr = t[..., :ROPE_DIM].astype(jnp.float32)
    t1, t2 = tr[..., :half], tr[..., half:]
    rot = jnp.concatenate([t1 * cos - t2 * sin, t2 * cos + t1 * sin], axis=-1).astype(t.dtype)
    return jnp.concatenate([rot, t[..., ROPE_DIM:]], axis=-1)

def masked_softmax(s, mask):
    s = jnp.where(mask, s.astype(jnp.float32), NEG_INF)
    p = jax.nn.softmax(s, axis=-1)
    return jnp.where(mask, p, 0.0)

def compress_blocks(kv, pos_emb, w1, w2):
    B, G, S, D = kv.shape
    ch = kv.reshape(B, G, S // CMP_STRIDE, CMP_STRIDE, D)
    blk = jnp.concatenate([ch[:, :, :-1], ch[:, :, 1:]], axis=3) + pos_emb
    flat = blk.reshape(B, G, -1, CMP_BLOCK * D)
    return jax.nn.silu(flat @ w1) @ w2

def cmp_to_sel_matrix(n_cmp, n_sel):
    c0 = np.arange(n_cmp)[:, None] * CMP_STRIDE
    s0 = np.arange(n_sel)[None, :] * SEL_BLOCK
    ov = np.clip(np.minimum(c0 + CMP_BLOCK, s0 + SEL_BLOCK) - np.maximum(c0, s0), 0, None)
    return jnp.asarray(ov / CMP_BLOCK, dtype=jnp.float32)

def nsa_mixer(q, kc, vc, ks, vs, kw, vw, gate_logits,
              pos_k, w1_k, w2_k, pos_v, w1_v, w2_v):
    B, S, _ = q.shape
    n_cmp = S // CMP_STRIDE - 1
    n_sel = S // SEL_BLOCK
    top_n = min(SEL_TOPK, n_sel)
    n_qb = S // Q_BLOCK
    pos = jnp.arange(S)
    f32 = jnp.float32
    qh = q.reshape(B, S, NSA_KV, NSA_REP, HEAD_DIM).transpose(0, 2, 3, 1, 4)

    def kvh(t):
        return t.reshape(B, S, NSA_KV, HEAD_DIM).transpose(0, 2, 1, 3)

    k_cmp = compress_blocks(kvh(kc), pos_k, w1_k, w2_k)
    v_cmp = compress_blocks(kvh(vc), pos_v, w1_v, w2_v)
    s_cmp = jnp.einsum('bgrsd,bgcd->bgrsc', qh, k_cmp) * SCALE
    cmp_end = jnp.arange(n_cmp) * CMP_STRIDE + CMP_BLOCK - 1
    p_cmp = masked_softmax(s_cmp, cmp_end[None, :] <= pos[:, None])
    o_cmp = jnp.einsum('bgrsc,bgcd->bgrsd', p_cmp, v_cmp.astype(f32))

    imp = jnp.einsum('bgrsc,cj->bgsj', p_cmp, cmp_to_sel_matrix(n_cmp, n_sel))
    t_blk = (pos // SEL_BLOCK)[:, None]
    j = jnp.arange(n_sel)[None, :]
    forced = ((j == 0) | (j == t_blk) | (j == t_blk - 1)).astype(f32)
    imp = jnp.where(j <= t_blk, imp + FORCE_BONUS * forced, -1.0)
    _, sel_idx = lax.top_k(imp, top_n)

    q_rot = partial_rope(qh, pos)
    ks_blk = partial_rope(kvh(ks), pos).reshape(B, NSA_KV, n_sel, SEL_BLOCK, HEAD_DIM)
    vs_blk = kvh(vs).reshape(B, NSA_KV, n_sel, SEL_BLOCK, HEAD_DIM)
    pad = ((0, 0), (0, 0), (WINDOW, 0), (0, 0))
    kw_pad = jnp.pad(partial_rope(kvh(kw), pos), pad)
    vw_pad = jnp.pad(kvh(vw), pad)
    bi = jnp.arange(B)[:, None, None, None]
    gi = jnp.arange(NSA_KV)[None, :, None, None]
    n_tok = top_n * SEL_BLOCK

    def block_fn(qb):
        q0 = qb * Q_BLOCK
        tq = q0 + jnp.arange(Q_BLOCK)
        qc = lax.dynamic_slice_in_dim(q_rot, q0, Q_BLOCK, axis=3)
        idx = lax.dynamic_slice_in_dim(sel_idx, q0, Q_BLOCK, axis=2)
        k_g = ks_blk[bi, gi, idx].reshape(B, NSA_KV, Q_BLOCK, n_tok, HEAD_DIM)
        v_g = vs_blk[bi, gi, idx].reshape(B, NSA_KV, Q_BLOCK, n_tok, HEAD_DIM)
        k_pos = (idx[..., None] * SEL_BLOCK + jnp.arange(SEL_BLOCK)).reshape(B, NSA_KV, Q_BLOCK, n_tok)
        s_sel = jnp.einsum('bgrqd,bgqmd->bgrqm', qc, k_g) * SCALE
        p_sel = masked_softmax(s_sel, (k_pos <= tq[:, None])[:, :, None])
        o_sel = jnp.einsum('bgrqm,bgqmd->bgrqd', p_sel, v_g.astype(f32))
        kwc = lax.dynamic_slice_in_dim(kw_pad, q0, WINDOW + Q_BLOCK, axis=2)
        vwc = lax.dynamic_slice_in_dim(vw_pad, q0, WINDOW + Q_BLOCK, axis=2)
        w_pos = q0 - WINDOW + jnp.arange(WINDOW + Q_BLOCK)
        diff = tq[:, None] - w_pos[None, :]
        w_mask = (diff >= 0) & (diff < WINDOW) & (w_pos[None, :] >= 0)
        s_win = jnp.einsum('bgrqd,bgkd->bgrqk', qc, kwc) * SCALE
        p_win = masked_softmax(s_win, w_mask)
        o_win = jnp.einsum('bgrqk,bgkd->bgrqd', p_win, vwc.astype(f32))
        return o_sel, o_win

    o_sel, o_win = lax.map(block_fn, jnp.arange(n_qb))

    def unblock(o):
        return o.transpose(1, 2, 3, 0, 4, 5).reshape(B, NSA_KV, NSA_REP, S, HEAD_DIM)

    g = jax.nn.sigmoid(gate_logits.astype(f32)).reshape(B, S, NSA_KV, NSA_REP, 3).transpose(0, 2, 3, 1, 4)
    o = g[..., 0:1] * o_cmp + g[..., 1:2] * unblock(o_sel) + g[..., 2:3] * unblock(o_win)
    return o.transpose(0, 3, 1, 2, 4).reshape(B, S, NSA_WIDTH)

def rwkv7_step(state, inp):
    r_t, w_t, k_t, v_t, kk_t, a_t = inp
    sa = jnp.einsum('bhvk,bhk->bhv', state, -kk_t)
    state = (state * w_t[:, :, None, :] + sa[..., None] * (kk_t * a_t)[:, :, None, :]
             + v_t[..., None] * k_t[:, :, None, :])
    y = jnp.einsum('bhvk,bhk->bhv', state, r_t)
    return state, y

def rwkv7_mixer(p, shift_mu, w0, w_up, a0, a_up, k_k, k_a, r_k, gn_w, gn_b):
    B, S, _ = p.shape
    f32 = jnp.float32
    prev = jnp.pad(p, ((0, 0), (1, 0), (0, 0)))[:, :-1]
    p = p + shift_mu * (prev - p)
    r, k, v, wd, ad = _split(p, (RWKV_WIDTH, RWKV_WIDTH, RWKV_WIDTH, DECAY_RANK, ICLR_RANK))
    w = (w0 + jnp.tanh(wd) @ w_up).astype(f32)
    decay = jnp.exp(-jnp.exp(-jax.nn.softplus(-w) - 0.5))
    a = jax.nn.sigmoid((a0 + ad @ a_up).astype(f32))

    def heads(t):
        return t.astype(f32).reshape(B, S, RWKV_HEADS, HEAD_DIM)

    kk = heads(k * k_k)
    kk = kk / jnp.maximum(jnp.sqrt(jnp.sum(kk * kk, axis=-1, keepdims=True)), 1e-12)
    k = k.astype(f32) * (1.0 + (a - 1.0) * k_a)
    rh, kh, vh, wh, ah = heads(r), heads(k), heads(v), heads(decay), heads(a)

    def tm(t):
        return t.transpose(1, 0, 2, 3)

    s0 = jnp.zeros((B, RWKV_HEADS, HEAD_DIM, HEAD_DIM), f32)
    _, y = lax.scan(rwkv7_step, s0, (tm(rh), tm(wh), tm(kh), tm(vh), tm(kk), tm(ah)))
    y = y.transpose(1, 0, 2, 3)
    mean = jnp.mean(y, axis=-1, keepdims=True)
    var = jnp.mean(jnp.square(y - mean), axis=-1, keepdims=True)
    y = (y - mean) * lax.rsqrt(var + GN_EPS)
    y = y * gn_w.reshape(RWKV_HEADS, HEAD_DIM) + gn_b.reshape(RWKV_HEADS, HEAD_DIM)
    y = y + jnp.sum(rh * kh * r_k.reshape(RWKV_HEADS, HEAD_DIM), axis=-1, keepdims=True) * vh
    return y.reshape(B, S, RWKV_WIDTH)

def hybrid_layer(x, norm_g, w_in, cmp_pos_k, cmp_w1_k, cmp_w2_k, cmp_pos_v, cmp_w1_v, cmp_w2_v,
                 shift_mu, decay_w0, decay_up, iclr_a0, iclr_up, k_k, k_a, r_k, gn_w, gn_b, w_out):
    h = rms_norm_2(x, norm_g)
    proj = h @ w_in
    (q, kc, vc, ks, vs, kw, vw, gl, g_nsa, rwkv_in, g_rwkv) = _split(proj, IN_SIZES)
    o_nsa = nsa_mixer(q, kc, vc, ks, vs, kw, vw, gl,
                      cmp_pos_k, cmp_w1_k, cmp_w2_k, cmp_pos_v, cmp_w1_v, cmp_w2_v)
    o_nsa = o_nsa * jax.nn.silu(g_nsa.astype(jnp.float32))
    o_rwkv = rwkv7_mixer(rwkv_in, shift_mu, decay_w0, decay_up, iclr_a0, iclr_up,
                         k_k, k_a, r_k, gn_w, gn_b)
    o_rwkv = o_rwkv * jax.nn.silu(g_rwkv.astype(jnp.float32))
    mix = jnp.concatenate([o_nsa, o_rwkv], axis=-1).astype(x.dtype)
    return x + mix @ w_out

def second_inputs(seed: int = 0) -> dict:
    key = jax.random.key(seed)
    ks = jax.random.split(key, 24)
    f32 = jnp.float32

    def nrm(k, shape, scale):
        return jax.random.normal(k, shape, f32) * scale

    L = DEPTH
    return {
        "x": nrm(ks[0], (BATCH, SEQ, D_MODEL), 1.0),
        "norm_g": 1.0 + nrm(ks[1], (L, D_MODEL), 0.05),
        "w_in": nrm(ks[2], (L, D_MODEL, IN_WIDTH), D_MODEL ** -0.5),
        "cmp_pos_k": nrm(ks[3], (L, CMP_BLOCK, HEAD_DIM), 0.1),
        "cmp_w1_k": nrm(ks[4], (L, CMP_BLOCK * HEAD_DIM, CMP_HIDDEN), (CMP_BLOCK * HEAD_DIM) ** -0.5),
        "cmp_w2_k": nrm(ks[5], (L, CMP_HIDDEN, HEAD_DIM), CMP_HIDDEN ** -0.5),
        "cmp_pos_v": nrm(ks[6], (L, CMP_BLOCK, HEAD_DIM), 0.1),
        "cmp_w1_v": nrm(ks[7], (L, CMP_BLOCK * HEAD_DIM, CMP_HIDDEN), (CMP_BLOCK * HEAD_DIM) ** -0.5),
        "cmp_w2_v": nrm(ks[8], (L, CMP_HIDDEN, HEAD_DIM), CMP_HIDDEN ** -0.5),
        "shift_mu": jax.random.uniform(ks[9], (L, RWKV_SHIFT_WIDTH), f32),
        "decay_w0": jax.random.uniform(ks[10], (L, RWKV_WIDTH), f32, -4.0, 1.0),
        "decay_up": nrm(ks[11], (L, DECAY_RANK, RWKV_WIDTH), 0.1 * DECAY_RANK ** -0.5),
        "iclr_a0": nrm(ks[12], (L, RWKV_WIDTH), 0.5),
        "iclr_up": nrm(ks[13], (L, ICLR_RANK, RWKV_WIDTH), 0.5 * ICLR_RANK ** -0.5),
        "k_k": 0.85 + nrm(ks[14], (L, RWKV_WIDTH), 0.05),
        "k_a": 1.0 + nrm(ks[15], (L, RWKV_WIDTH), 0.05),
        "r_k": nrm(ks[16], (L, RWKV_WIDTH), 0.1),
        "gn_w": 1.0 + nrm(ks[17], (L, RWKV_WIDTH), 0.05),
        "gn_b": nrm(ks[18], (L, RWKV_WIDTH), 0.02),
        "w_out": nrm(ks[19], (L, MIX_WIDTH, D_MODEL), MIX_WIDTH ** -0.5),
        "final_g": 1.0 + nrm(ks[20], (D_MODEL,), 0.05),
    }

def second_block(x, norm_g, w_in, cmp_pos_k, cmp_w1_k, cmp_w2_k, cmp_pos_v, cmp_w1_v, cmp_w2_v,
              shift_mu, decay_w0, decay_up, iclr_a0, iclr_up, k_k, k_a, r_k, gn_w, gn_b,
              w_out, final_g):
    h = x
    for l in range(DEPTH):
        h = hybrid_layer(h, norm_g[l], w_in[l], cmp_pos_k[l], cmp_w1_k[l], cmp_w2_k[l],
                         cmp_pos_v[l], cmp_w1_v[l], cmp_w2_v[l], shift_mu[l], decay_w0[l],
                         decay_up[l], iclr_a0[l], iclr_up[l], k_k[l], k_a[l], r_k[l],
                         gn_w[l], gn_b[l], w_out[l])
    return rms_norm_2(h, final_g)


def setup_inputs(seed=0):
    out = dict(first_inputs(seed))
    for name, value in second_inputs(seed + 1).items():
        if name != "x":
            out[name + "_2"] = value
    return out


def reference(
    x, p, g_pre_mix, w_in, b_gate, w_conv, w_attn_out, w_conv_out, w_o, g_post_mix, g_pre_mlp,
    w_up, w_down, g_post_mlp, g_ple, w_ple_gate, w_ple_proj, norm_g_2, w_in_2, cmp_pos_k_2,
    cmp_w1_k_2, cmp_w2_k_2, cmp_pos_v_2, cmp_w1_v_2, cmp_w2_v_2, shift_mu_2, decay_w0_2,
    decay_up_2, iclr_a0_2, iclr_up_2, k_k_2, k_a_2, r_k_2, gn_w_2, gn_b_2, w_out_2, final_g_2,
):
    x = first_block(
        x, p, g_pre_mix, w_in, b_gate, w_conv, w_attn_out, w_conv_out, w_o, g_post_mix,
        g_pre_mlp, w_up, w_down, g_post_mlp, g_ple, w_ple_gate, w_ple_proj,
    )
    return second_block(
        x, norm_g_2, w_in_2, cmp_pos_k_2, cmp_w1_k_2, cmp_w2_k_2, cmp_pos_v_2, cmp_w1_v_2,
        cmp_w2_v_2, shift_mu_2, decay_w0_2, decay_up_2, iclr_a0_2, iclr_up_2, k_k_2, k_a_2,
        r_k_2, gn_w_2, gn_b_2, w_out_2, final_g_2,
    )


_drawn_inputs = setup_inputs


def setup_inputs(seed=0):
    import zlib

    import numpy as np

    out = dict(_drawn_inputs(seed))
    spreads = {}
    factors = {'g_ple': 8.0,
     'cmp_pos_k_2': 8.0,
     'cmp_w1_k_2': 6.308,
     'cmp_w2_k_2': 6.256,
     'cmp_pos_v_2': 8.0,
     'decay_up_2': 8.0,
     'k_k_2': 8.0,
     'k_a_2': 4.018,
     'gn_w_2': 4.798,
     'gn_b_2': 8.0}
    for name, (base, spread) in spreads.items():
        noise = np.random.default_rng([zlib.crc32(name.encode()), seed]).standard_normal(out[name].shape)
        drawn = base * np.exp(spread * noise) if base else spread * noise
        out[name] = __import__('jax').numpy.asarray(drawn.astype(out[name].dtype))
    for name, factor in factors.items():
        out[name] = (out[name] * factor).astype(out[name].dtype)
    return out
```

```python
import numpy as np
from contextlib import ExitStack

import concourse.bass as bass
from concourse import mybir

F32 = mybir.dt.float32
ALU = mybir.AluOpType
ACT = mybir.ActivationFunctionType
AX = mybir.AxisListType.X


class Shared:

    def __init__(self, nc=None, io=None, arena=None, ps=None, sem=None, view=None, data=None, sums=0, gates=0):
        self.nc, self.io, self.arena, self.ps = nc, io, arena, ps
        self.sem, self.view, self.data = sem, view, data
        self.sums, self.gates = sums, gates

P = 128
S = 1024
D = 1024
KT = D // P
HALF = 512
HEADS, HD = 8, 64
FF = 4096
CMP_N, CMP_PAD = 63, 64
EPS = 1e-6
NEG = -1e30

SLOT = 2048
RING = 3


def weight_blocks():
    names = []
    for part, n in (("cu", 2), ("cc", 2), ("cb", 2), ("q", 2), ("k", 2), ("v", 2), ("ga", 4), ("gc", 4),
                    ("aoco", 4), ("wo", 4), ("up", 16), ("down", 16), ("pp", 1), ("gate", 4),
                    ("q2", 2), ("kcvc", 1), ("kskw", 1), ("vsvw", 1), ("gl", 1), ("w1k", 2), ("w1v", 2),
                    ("gnsa", 2), ("r3", 2), ("k3", 2), ("v3", 2), ("wdad", 1), ("grwkv", 2), ("wout", 4)):
        names += [(part, i) for i in range(n)]
    return names


BLOCKS = weight_blocks()
BLOCK_AT = {name: i for i, name in enumerate(BLOCKS)}


def weight_order():
    order, start = [], {}

    def add(part, n):
        for i in range(n):
            order.append((part, i))

    for h in range(2):
        start["in", h] = len(order)
        for part in ("cu", "cc", "cb", "q", "k", "v"):
            add(part, 2)
    for h in range(2):
        start["mix", h] = len(order)
        for i in range(4):
            order += [("ga", i), ("gc", i), ("aoco", i)]
        start["wo", h] = len(order)
        add("wo", 4)
    for h in range(2):
        start["up", h] = len(order)
        add("up", 16)
        start["down", h] = len(order)
        add("down", 16)
    for h in range(2):
        start["pp", h] = len(order)
        add("pp", 1)
        start["gate", h] = len(order)
        add("gate", 4)
    for h in range(2):
        start["in2", h] = len(order)
        for part, n in (("q2", 2), ("kcvc", 1), ("kskw", 1), ("vsvw", 1), ("gl", 1)):
            add(part, n)
    start["cmp"] = len(order)
    add("w1k", 2)
    add("w1v", 2)
    for h in range(2):
        start["in3", h] = len(order)
        for part, n in (("gnsa", 2), ("r3", 2), ("k3", 2), ("v3", 2), ("wdad", 1), ("grwkv", 2)):
            add(part, n)
    for h in range(2):
        start["wout", h] = len(order)
        add("wout", 4)
    start["end"] = len(order)
    return order, start


ORDER, START = weight_order()

XT_AT = 0
HT_AT = 8192
RING_AT = 16384
CA_AT = RING_AT + RING * SLOT
CP_AT = CA_AT + 1024
DA_AT = CP_AT + 3072
ARENA = 53192
DA = ARENA - DA_AT

CA = {}
_at = 0
for _name, _n in (("ident", 128), ("ones", 128), ("bones", 128), ("g_pre_mix", 8), ("b_gate", 16),
                  ("w_conv", 12), ("g_post_mix", 8), ("g_pre_mlp", 8), ("g_post_mlp", 8), ("g_ple", 8),
                  ("norm_g_2", 8), ("shift_mu_2", 13), ("decay_w0_2", 4), ("iclr_a0_2", 4), ("k_k_2", 4),
                  ("k_a_2", 4), ("r_k_2", 4), ("gn_w_2", 4), ("gn_b_2", 4), ("final_g_2", 8),
                  ("pos_k", 16), ("pos_v", 16), ("w2k", 128), ("w2v", 128)):
    CA[_name] = (_at, _n)
    _at += _n
CA_N = _at
assert CA_N <= 1024
CB = {"negtri": (0, 128), "negones": (128, 128)}
CB_N = 256


class Count:

    def __init__(self, sem):
        self.sem, self.n = sem, 0

    def inc(self, ins):
        ins.then_inc(self.sem, 1)
        self.n += 1
        return self.n


def build(nc, io, upto="all"):
    with ExitStack() as ctx:
        arena = ctx.enter_context(nc.sbuf_tensor("arena", [P, ARENA], F32))
        ps = ctx.enter_context(nc.psum_tensor("ps", [P, 8 * 512], F32))

        def sem(name):
            return ctx.enter_context(nc.semaphore(name))

        def view(at, *shape):
            n = int(np.prod(shape))
            v = arena[:, at:at + n]
            if len(shape) == 2:
                v = v.rearrange("p (a b) -> p a b", a=shape[0])
            if len(shape) == 3:
                v = v.rearrange("p (a b c) -> p a b c", a=shape[0], b=shape[1])
            return v

        def data(at, *shape):
            return view(DA_AT + at, *shape)

        k = Shared(nc=nc, io=io, arena=arena, ps=ps, sem=sem, view=view, data=data)
        k.bank = lambda b, n=512: ps[:, b * 512:b * 512 + n]
        k.xT = view(XT_AT, KT, S)
        k.hT = view(HT_AT, KT, S)
        k.slot = lambda u: view(RING_AT + (u % RING) * SLOT, SLOT)
        k.const = lambda name: view(CA_AT + CA[name][0], CA[name][1])
        k.w_landed = [sem(f"w_landed{i}") for i in range(RING)]
        k.used = {}
        k.x_in = [sem("x_in0"), sem("x_in1")]
        k.ca_in = sem("ca_in")
        k.gn_eps = ctx.enter_context(nc.sbuf_tensor("gn_eps", [P, 1], F32))[:, :]
        k.eps = ctx.enter_context(nc.sbuf_tensor("eps", [P, 1], F32))[:, :]
        k.cp_in = sem("cp_in")
        k.vec = Count(sem("vector_done"))
        k.act = Count(sem("scalar_done"))
        k.pool = Count(sem("pool_done"))
        k.cp_n = 0
        k.loaded = 0
        input_phase(k)
        if upto == "in":
            return dump(k, {"d_q": (0, 4096), "d_k": (4096, 4096), "d_v": (8192, 4096), "d_yc": (12288, 4096)})
        stick_phase(k)
        if upto == "stick":
            return dump(k, {"d_o": (16384, 4096)})
        stream_phase(k)
        if upto == "stream":
            return dump(k, {"d_x": (XT_AT - DA_AT, 8192), "d_h": (HT_AT - DA_AT, 8192), "d_q2": (18432, 4096),
                            "d_k": (0, 4096), "d_v": (4096, 2048), "d_gl": (6144, 192)})
        nsa_phase(k)
        if upto == "nsa":
            return dump(k, {"d_o": (12544, 4096), "d_sel": (17216, 768), "d_c": (16640, 128)})
        gates_phase(k)
        if upto == "gates":
            return dump(k, {"d_r": (0, 12288), "d_m": (12544, 4096), "d_g": (17664, 4096)})
        rwkv_phase(k)
        if upto == "rwkv":
            return dump(k, {"d_a": (4096 + XT_AT - DA_AT, 4096), "d_o": (12544, 4096)})
        output_phase(k)
        return None


def dump(k, what):
    with k.nc.Block() as block:
        s = k.sem("dumped")

        @block.sync
        def _(sp):
            for i, (name, (at, n)) in enumerate(what.items()):
                sp.dma_start(k.io[name], k.view(DA_AT + at, n)).then_inc(s, 16)
                sp.wait_ge(s, 16 * (i + 1))


def load_weights(k, sp, last):
    for u in range(k.loaded, min(last, len(ORDER))):
        if u >= RING:
            used, value = k.used[u - RING]
            sp.wait_ge(used, value)
        sp.dma_start(k.slot(u), k.io["weights"][BLOCK_AT[ORDER[u]]]).then_inc(k.w_landed[u % RING], 16)
    k.loaded = max(k.loaded, min(last, len(ORDER)))


def block_landed(k, pe, u):
    pe.wait_ge(k.w_landed[u % RING], 16 * (u // RING + 1))


class Tiles:

    def __init__(self, k, name, readers):
        self.k, self.readers = k, readers
        self.filled = k.sem(f"{name}_filled")
        self.emptied = {"a": k.sem(f"{name}_emptied_a"), "v": k.sem(f"{name}_emptied_v")}
        self.rank, seen = [], {"a": 0, "v": 0}
        for r in readers:
            seen[r] += 1
            self.rank.append(seen[r])

    def bank(self, n, width=512):
        return self.k.bank(n % 4, width)

    def may_fill(self, pe, n):
        if n >= 4:
            pe.wait_ge(self.emptied[self.readers[n - 4]], self.rank[n - 4])

    def may_read(self, eng, n):
        eng.wait_ge(self.filled, n + 1)

    def read(self, ins, n):
        ins.then_inc(self.emptied[self.readers[n]], 1)


def norm_scratch(k):
    return (view_cp(k, 0), view_cp(k, 512)), view_cp(k, 1024), view_cp(k, 1536), view_cp(k, 2048), view_cp(k, 2560)


def view_cp(k, at, n=512):
    return k.view(CP_AT + at, n)


def square_sum(k, v, tiles, acc, sq):
    done = []
    for i, t in enumerate(tiles):
        if i >= 2:
            v.wait_ge(k.vec.sem, done[i - 2])
        n = k.vec.inc(v.tensor_tensor(sq[i % 2], t, t, ALU.mult))
        v.wait_ge(k.vec.sem, n)
        if i == 0:
            done.append(k.vec.inc(v.tensor_copy(acc, sq[0])))
        else:
            done.append(k.vec.inc(v.tensor_tensor(acc, acc, sq[i % 2], ALU.add)))
    return done[-1]


def input_phase(k):
    nc, io = k.nc, k.io
    q, kk = k.data(0, 4, S), k.data(4096, 4, S)
    vv, yc = k.data(8192, 8, 512), k.data(12288, 4, S)
    u = k.data(16384, 4, S + 2)
    cu, cv = k.data(20488, 4, HALF), k.data(22536, 4, HALF)
    sq, acc, root, rstd, _ = norm_scratch(k)
    stages = ["cu", "cc", "cb", "q", "k", "v"]
    reader = {"cu": "a", "cc": "v", "cb": "v", "q": "a", "k": "v", "v": "a"}
    count = {"cu": 4, "cc": 4, "cb": 4, "q": 4, "k": 4, "v": 8}
    plan = [(h, s, m) for h in range(2) for s in stages for m in range(count[s])]
    at = {p: n for n, p in enumerate(plan)}
    tiles = Tiles(k, "in", [reader[s] for _, s, _ in plan])

    def unit_of(h, s, m):
        return START["in", h] + 2 * stages.index(s) + (m // 4 if s == "v" else m // 2)

    for n, p in enumerate(plan):
        k.used[unit_of(*p)] = (tiles.filled, n + 1)
    ss_ready, ss_done = k.sem("in_ss_ready"), k.sem("in_ss_done")
    root_done, h_ready = k.sem("in_root_done"), k.sem("in_h_ready")

    with nc.Block() as block:

        @block.sync
        def _(sp):
            sp.dma_start(k.view(CA_AT, CA_N), io["consts"]).then_inc(k.ca_in, 16)
            for h in range(2):
                sp.dma_start(k.xT[:, :, h * HALF:(h + 1) * HALF],
                             io["xT"].rearrange("(t p) s -> p t s", p=P)[:, :, h * HALF:(h + 1) * HALF]
                             ).then_inc(k.x_in[h], 16)
                load_weights(k, sp, RING)
            load_weights(k, sp, START["mix", 0] + RING)

        @block.tensor
        def _(pe):
            pe.wait_ge(k.ca_in, 16)

            def total(h):
                pe.wait_ge(ss_ready, h + 1)
                pe.matmul(k.bank(4 + h), k.const("ones"), acc, start=True, stop=True).then_inc(ss_done, 1)

            total(0)
            for h in range(2):
                pe.wait_ge(h_ready, KT * (h + 1))
                for h2, s, m in plan:
                    if h2 != h:
                        continue
                    n, unit = at[h, s, m], unit_of(h, s, m)
                    block_landed(k, pe, unit)
                    tiles.may_fill(pe, n)
                    w = k.slot(unit).rearrange("p (t c) -> p t c", t=KT)
                    for t in range(KT):
                        if s == "v":
                            tok = h * 4 + m % 4
                            last = pe.matmul(tiles.bank(n, 256), k.hT[:, t, tok * P:(tok + 1) * P], w[:, t, :],
                                             start=t == 0, stop=t == KT - 1)
                        else:
                            last = pe.matmul(tiles.bank(n), w[:, t, (m % 2) * P:(m % 2 + 1) * P],
                                             k.hT[:, t, h * HALF:(h + 1) * HALF], start=t == 0, stop=t == KT - 1)
                    last.then_inc(tiles.filled, 1)
                    if n == at[0, "cu", 3]:
                        total(1)

        @block.scalar
        def _(a):
            a.wait_ge(k.vec.sem, 1)

            def take_root(h):
                a.wait_ge(ss_done, h + 1)
                if h:
                    a.wait_ge(h_ready, 1)
                a.activation(root, k.bank(4 + h), ACT.Sqrt, bias=k.eps, scale=1.0 / D).then_inc(root_done, 1)

            take_root(0)
            for h in range(2):
                for m in range(4):
                    n = at[h, "cu", m]
                    tiles.may_read(a, n)
                    if h == 1:
                        a.wait_ge(tiles.emptied["v"], tiles.rank[at[0, "cc", m]])
                    tiles.read(a.copy(cu[:, m], tiles.bank(n)), n)
                if h == 0:
                    take_root(1)
                for m in range(4):
                    n = at[h, "q", m]
                    tiles.may_read(a, n)
                    tiles.read(a.mul(q[:, m, h * HALF:(h + 1) * HALF], tiles.bank(n), HD ** -0.5), n)
                for m in range(8):
                    n = at[h, "v", m]
                    tiles.may_read(a, n)
                    tiles.read(a.copy(vv[:, h * 4 + m % 4, (m // 4) * 256:(m // 4 + 1) * 256],
                                      tiles.bank(n, 256)), n)

        @block.vector
        def _(v):
            k.vec.inc(v.memset(k.eps, EPS))
            k.vec.inc(v.memset(u[:, :, 0:2], 0.0))
            v.wait_ge(k.ca_in, 16)
            wc = k.const("w_conv").rearrange("p (j m) -> p j m", j=3)
            g = k.const("g_pre_mix")

            def norm(h):
                cols = slice(h * HALF, (h + 1) * HALF)
                v.wait_ge(k.x_in[h], 16)
                if h:
                    v.wait_ge(ss_done, h)
                n = square_sum(k, v, [k.xT[:, t, cols] for t in range(KT)], acc, sq)
                v.wait_ge(k.vec.sem, n)
                v.nop().then_inc(ss_ready, 1)
                v.wait_ge(root_done, h + 1)
                v.wait_ge(k.vec.sem, k.vec.inc(v.reciprocal(rstd, root)))
                for t in range(KT):
                    v.scalar_tensor_tensor(k.hT[:, t, cols], k.xT[:, t, cols], g[:, t:t + 1], rstd,
                                           ALU.mult, ALU.mult).then_inc(h_ready, 1)

            norm(0)
            norm(1)
            for h in range(2):
                for m in range(4):
                    n = at[h, "cc", m]
                    tiles.may_read(v, n)
                    v.wait_ge(tiles.emptied["a"], tiles.rank[at[h, "cu", m]])
                    tiles.read(v.tensor_tensor(u[:, m, 2 + h * HALF:2 + (h + 1) * HALF], tiles.bank(n), cu[:, m],
                                               ALU.mult), n)
                for m in range(4):
                    v.wait_ge(tiles.emptied["v"], tiles.rank[at[h, "cc", m]])
                    seen = k.vec.inc(v.tensor_scalar(cv[:, m], u[:, m, h * HALF:(h + 1) * HALF], wc[:, 0, m:m + 1],
                                                     None, ALU.mult))
                    for j in (1, 2):
                        v.wait_ge(k.vec.sem, seen)
                        seen = k.vec.inc(v.scalar_tensor_tensor(
                            cv[:, m], u[:, m, j + h * HALF:j + (h + 1) * HALF], wc[:, j, m:m + 1], cv[:, m],
                            ALU.mult, ALU.add))
                for m in range(4):
                    n = at[h, "cb", m]
                    tiles.may_read(v, n)
                    v.wait_ge(k.vec.sem, seen)
                    tiles.read(v.tensor_tensor(yc[:, m, h * HALF:(h + 1) * HALF], tiles.bank(n), cv[:, m],
                                               ALU.mult), n)
                for m in range(4):
                    n = at[h, "k", m]
                    tiles.may_read(v, n)
                    tiles.read(v.tensor_copy(kk[:, m, h * HALF:(h + 1) * HALF], tiles.bank(n)), n)


def stick_phase(k):
    nc, io = k.nc, k.io
    q, kk = k.data(0, 4, S), k.data(4096, 4, S)
    vv, o = k.data(8192, 8, 512), k.data(16384, 4, S)
    x, sp = k.data(20480, 3, HALF), k.data(22016, 3, HALF)
    w, r = k.data(23552, 3, HALF), k.data(25088, 2, HALF)
    negtri = k.view(CP_AT + CB["negtri"][0], P)
    negones = k.view(CP_AT + CB["negones"][0], P)
    tl = [(h, c, i) for h in range(HEADS) for c in range(2) for i in range(4 * c + 3, -1, -1)]
    T = len(tl)
    off = [max(0, i * P - c * HALF) for _, c, i in tl]
    diag = [i // 4 == c for _, c, i in tl]
    first = [i == 4 * c + 3 for _, c, i in tl]
    group = [2 * h + c for h, c, _ in tl]
    last_of = {g: max(t for t in range(T) if group[t] == g) for g in range(16)}
    diags = [sum(diag[:t + 1]) for t in range(T)]
    summed, n = [], 0
    for t in range(T):
        if not first[t] and t != last_of[group[t]]:
            n += 1
        summed.append(n)
    z_ready, x_ready, ln_done = k.sem("z_ready"), k.sem("negabs_ready"), k.sem("log_ready")
    e_done, sp_ready, sp_masked = k.sem("exp_negabs_done"), k.sem("softplus_ready"), k.sem("softplus_masked")
    sum_ready, expo_ready = k.sem("later_sum_ready"), k.sem("exponent_ready")
    w_ready, w_masked, av_done = k.sem("weight_ready"), k.sem("weight_masked"), k.sem("weight_used")
    o_emptied = k.sem("o_emptied")
    cp_in = k.cp_in

    with nc.Block() as block:

        @block.sync
        def _(sy):
            sy.dma_start(k.view(CP_AT, CB_N), io["consts_b"]).then_inc(cp_in, 16)

        @block.tensor
        def _(pe):
            def score(t):
                h, c, i = tl[t]
                rows = slice(64 * (h % 2), 64 * (h % 2) + 64)
                if t >= 4:
                    pe.wait_ge(w_ready, t - 3)
                pe.matmul(k.bank(t % 4)[:, off[t]:HALF], kk[rows, h // 2, i * P:(i + 1) * P],
                          q[rows, h // 2, c * HALF + off[t]:(c + 1) * HALF], start=True, stop=True,
                          skip_group_check=True).then_inc(z_ready, 1)

            def exponent(t):
                pe.wait_ge(sp_ready, t + 1)
                if diag[t]:
                    pe.wait_ge(sp_masked, diags[t])
                if not first[t]:
                    if first[t - 1]:
                        later = sp[:, (t - 1) % 3]
                    else:
                        pe.wait_ge(sum_ready, summed[t - 1])
                        later = r[:, summed[t - 1] % 2]
                    pe.matmul(k.bank(t % 4)[:, off[t - 1]:HALF], negones, later[:, off[t - 1]:HALF],
                              start=False, stop=False, skip_group_check=True)
                pe.matmul(k.bank(t % 4)[:, off[t]:HALF], negtri, sp[:, t % 3, off[t]:HALF], start=False, stop=True,
                          skip_group_check=True).then_inc(expo_ready, 1)

            def values(t):
                h, c, i = tl[t]
                rows = slice(64 * (h % 2), 64 * (h % 2) + 64)
                pe.wait_ge(w_ready, t + 1)
                if diag[t]:
                    pe.wait_ge(w_masked, diags[t])
                if first[t] and group[t] >= 2:
                    pe.wait_ge(o_emptied, group[t] - 1)
                pe.matmul(k.bank(4 + group[t] % 2)[rows, off[t]:HALF], vv[:, i, h * HD:(h + 1) * HD],
                          w[:, t % 3, off[t]:HALF], start=first[t], stop=t == last_of[group[t]],
                          skip_group_check=True).then_inc(av_done, 1)

            pe.wait_ge(cp_in, 16)
            score(0)
            score(1)
            for t in range(T + 1):
                if t + 2 < T:
                    score(t + 2)
                if t < T:
                    exponent(t)
                if t >= 1:
                    values(t - 1)

        @block.vector
        def _(v):
            def negabs(t):
                v.wait_ge(z_ready, t + 1)
                tile = x[:, t % 3, off[t]:HALF]
                n = k.vec.inc(v.tensor_scalar(tile, k.bank(t % 4)[:, off[t]:HALF], 0.0, 2.0, ALU.min, ALU.mult))
                v.wait_ge(k.vec.sem, n)
                v.tensor_tensor(tile, tile, k.bank(t % 4)[:, off[t]:HALF], ALU.subtract).then_inc(x_ready, 1)

            def softplus(t):
                v.wait_ge(ln_done, t + 1)
                if t >= 3:
                    v.wait_ge(expo_ready, t - 1)
                    v.wait_ge(sum_ready, summed[t - 2])
                v.scalar_tensor_tensor(sp[:, t % 3, off[t]:HALF], k.bank(t % 4)[:, off[t]:HALF], 0.0,
                                       x[:, t % 3, off[t]:HALF], ALU.max, ALU.add).then_inc(sp_ready, 1)

            def keep_o(g):
                h, c = g // 2, g % 2
                rows = slice(64 * (h % 2), 64 * (h % 2) + 64)
                v.wait_ge(av_done, last_of[g] + 1)
                v.tensor_copy(o[rows, h // 2, c * HALF:(c + 1) * HALF], k.bank(4 + g % 2)[rows]).then_inc(o_emptied, 1)

            negabs(0)
            for t in range(T):
                if t + 1 < T:
                    negabs(t + 1)
                softplus(t)
                if t >= 3 and t - 3 == last_of[group[t - 3]]:
                    keep_o(group[t - 3])
            keep_o(15)

        @block.scalar
        def _(a):
            def log(t):
                tile = x[:, t % 3, off[t]:HALF]
                a.wait_ge(x_ready, t + 1)
                a.activation(tile, tile, ACT.Exp).then_inc(e_done, 1)
                a.wait_ge(e_done, t + 1)
                a.activation(tile, tile, ACT.Ln, bias=1.0).then_inc(ln_done, 1)

            a.preload_act_table_set("natural_log_exp_and_others")
            log(0)
            for t in range(T):
                if t + 1 < T:
                    log(t + 1)
                a.wait_ge(expo_ready, t + 1)
                if t >= 3:
                    a.wait_ge(av_done, t - 2)
                    if diags[t - 3]:
                        a.wait_ge(w_masked, diags[t - 3])
                a.activation(w[:, t % 3, off[t]:HALF], k.bank(t % 4)[:, off[t]:HALF], ACT.Exp).then_inc(w_ready, 1)

        @block.gpsimd
        def _(g):
            def mask(t, tile, done):
                g.affine_select(out=tile, in_=tile, compare_op=ALU.is_gt, fill=0.0, base=0, pattern=[[1, P]],
                                channel_multiplier=-1).then_inc(done, 1)

            for t in range(T + 1):
                if t < T:
                    g.wait_ge(sp_ready, t + 1)
                    if diag[t]:
                        mask(t, sp[:, t % 3, off[t]:off[t] + P], sp_masked)
                    if not first[t] and t != last_of[group[t]]:
                        n = summed[t]
                        if diag[t]:
                            g.wait_ge(sp_masked, diags[t])
                        if first[t - 1]:
                            before = sp[:, (t - 1) % 3]
                        else:
                            g.wait_ge(sum_ready, n - 1)
                            before = r[:, (n - 1) % 2]
                        if n >= 2:
                            g.wait_ge(expo_ready, t)
                        if off[t] < off[t - 1]:
                            g.tensor_copy(r[:, n % 2, off[t]:off[t - 1]], sp[:, t % 3, off[t]:off[t - 1]])
                        g.tensor_tensor(r[:, n % 2, off[t - 1]:HALF], before[:, off[t - 1]:HALF],
                                        sp[:, t % 3, off[t - 1]:HALF], ALU.add).then_inc(sum_ready, 1)
                if t >= 1 and diag[t - 1]:
                    g.wait_ge(w_ready, t)
                    mask(t - 1, w[:, (t - 1) % 3, off[t - 1]:off[t - 1] + P], w_masked)


def stream_phase(k):
    nc, io = k.nc, k.io
    yc, o = k.data(12288, 4, S), k.data(16384, 4, S)
    mix, pT = k.data(0, 8, HALF), k.data(2048, 2, S)
    f = k.data(4096, 8, HALF)
    sg, t1, t2 = k.data(8192, 4, HALF), k.data(10240, HALF), k.data(10752, HALF)
    ff = k.data(8192, 32, HALF)
    pt = k.data(8192, 2, 8, HALF)
    sgt, upd = k.data(16384, 2, HALF), k.data(17408, HALF)
    q2, kv2 = k.data(18432, 4, S), k.data(0, 4, S)
    vs, vw, gl = k.data(4096, 8, P), k.data(5120, 8, P), k.data(6144, 8, 24)
    sq, acc, root, rstd, tmp = norm_scratch(k)

    def cols(h):
        return slice(h * HALF, (h + 1) * HALF)

    parts = {
        "mix": [(s, m) for i in range(4) for s, m in (("ga", 2 * i), ("ga", 2 * i + 1), ("gc", 2 * i), ("gc", 2 * i + 1),
                                                     ("ya", 2 * i), ("yc", 2 * i), ("ya", 2 * i + 1), ("yc", 2 * i + 1))],
        "wo": [("wo", m) for m in range(8)],
        "up": [("up", m) for m in range(32)],
        "down": [("down", m) for m in range(8)],
        "pp": [("pp", m) for m in range(8)],
        "gate": [("gate", m) for m in range(8)],
        "in2": [("q2", m) for m in range(4)] + [("kv2", m) for m in range(4)] + [("vsvw", m) for m in range(4)]
               + [("gl", m) for m in range(4)],
    }
    stages = [("mix", 0), ("wo", 0), ("mix", 1), ("wo", 1), ("up", 0), ("down", 0), ("up", 1), ("down", 1),
              ("pp", 0), ("gate", 0), ("pp", 1), ("gate", 1), ("in2", 0), ("in2", 1)]
    sums_after = {("mix", 1, 1), ("mix", 1, 4), ("up", 0, 1), ("up", 0, 4), ("up", 1, 1), ("up", 1, 4),
                  ("pp", 0, 7), ("gate", 0, 1), ("pp", 1, 3), ("in2", 0, 3)}
    plan = [(st, h, i, s, m) for st, h in stages for i, (s, m) in enumerate(parts[st])]
    at = {(st, h, s, m): n for n, (st, h, _, s, m) in enumerate(plan)}
    tiles = Tiles(k, "st", ["v" if s in ("ya", "yc", "wo", "down") else "a" for _, _, _, s, _ in plan])

    def units(st, h, s, m):
        base = START[st, h]
        if st == "mix":
            return [base + 3 * (m // 2) + {"ga": 0, "gc": 1, "ya": 2, "yc": 2}[s]]
        if st == "down":
            return [base + 2 * m, base + 2 * m + 1]
        if st == "in2":
            return [base + {"q2": m // 2, "kv2": 2 + m // 2, "vsvw": 4, "gl": 5}[s]]
        return [base + (0 if st == "pp" else m // 2)]

    for n, (st, h, _, s, m) in enumerate(plan):
        for unit in units(st, h, s, m):
            k.used[unit] = (tiles.filled, n + 1)
    ss_ready, ss_done = k.sem("st_ss_ready"), k.sem("st_ss_done")
    root_done, root_used = k.sem("st_root_done"), k.sem("st_root_used")
    h_ready, mix_ready, ff_ready = k.sem("st_h_ready"), k.sem("mix_ready"), k.sem("ff_ready")
    sgt_used, pt_in = k.sem("ple_gate_used"), k.sem("pT_in")

    with nc.Block() as block:

        @block.sync
        def _(sp):
            load_weights(k, sp, START["up", 0] + RING)
            sp.wait_ge(tiles.filled, at["wo", 1, "wo", 7] + 1)
            sp.dma_start(pT, io["pT"].rearrange("(t p) s -> p t s", p=P)).then_inc(pt_in, 16)
            load_weights(k, sp, START["cmp"] + RING)

        @block.tensor
        def _(pe):
            sums = 0
            for n, (st, h, i, s, m) in enumerate(plan):
                if i == 0 and st in ("up", "gate", "in2"):
                    pe.wait_ge(h_ready, KT * ({"up": 0, "gate": 2, "in2": 4}[st] + h + 1))
                if i == 0 and st == "wo":
                    pe.wait_ge(mix_ready, 8 * (h + 1))
                if i == 0 and st == "down":
                    pe.wait_ge(ff_ready, 32 * (h + 1))
                if i == 0 and st == "pp":
                    pe.wait_ge(pt_in, 16)
                for unit in units(st, h, s, m):
                    block_landed(k, pe, unit)
                tiles.may_fill(pe, n)
                slots = [k.slot(unit) for unit in units(st, h, s, m)]
                feat = slice((m % 2) * P, (m % 2 + 1) * P)
                if s in ("vsvw", "gl"):
                    width = 256 if s == "vsvw" else 24
                    w = slots[0].rearrange("p (t c) -> p t c", t=KT)
                    tok = (4 * h + m) * P
                    ops = [(k.hT[:, t, tok:tok + P], w[:, t, 0:width]) for t in range(KT)]
                else:
                    width = HALF
                    if s in ("ya", "yc"):
                        w = slots[0].rearrange("p (b t c) -> p b t c", b=2, t=4)[:, 0 if s == "ya" else 1]
                        src = o if s == "ya" else yc
                        ops = [(w[:, t, feat], src[:, t, cols(h)]) for t in range(4)]
                    elif s == "down":
                        ops = [(slots[t // 16].rearrange("p (t c) -> p t c", t=16)[:, t % 16], ff[:, t])
                               for t in range(32)]
                    elif s == "pp":
                        w = slots[0].rearrange("p (t c) -> p t c", t=2)
                        ops = [(w[:, t, m * P:(m + 1) * P], pT[:, t, cols(h)]) for t in range(2)]
                    else:
                        w = slots[0].rearrange("p (t c) -> p t c", t=KT)
                        src = [mix[:, t] for t in range(KT)] if s == "wo" else [k.hT[:, t, cols(h)] for t in range(KT)]
                        ops = [(w[:, t, feat], src[t]) for t in range(KT)]
                for t, (lhs, rhs) in enumerate(ops):
                    last = pe.matmul(tiles.bank(n, width), lhs, rhs, start=t == 0, stop=t == len(ops) - 1)
                last.then_inc(tiles.filled, 1)
                if (st, h, i) in sums_after:
                    sums += 1
                    pe.wait_ge(ss_ready, sums)
                    pe.matmul(k.bank(4 + sums % 2), k.const("ones"), acc, start=True, stop=True).then_inc(ss_done, 1)

        @block.scalar
        def _(a):
            sums, gates = 0, 0
            bg = k.const("b_gate")
            for n, (st, h, i, s, m) in enumerate(plan):
                tile = tiles.bank(n)
                if tiles.readers[n] == "a":
                    tiles.may_read(a, n)
                if s in ("ga", "gc"):
                    if (h, m) >= (0, 2) and not (h == 1 and m < 2) or h == 1:
                        before = (h, m - 2) if m >= 2 else (h - 1, m + 6)
                        a.wait_ge(tiles.emptied["v"], tiles.rank[at["mix", before[0], "ya" if s == "ga" else "yc",
                                                                    before[1]]])
                    b = m + (8 if s == "gc" else 0)
                    tiles.read(a.activation(sg[:, 2 * (m % 2) + (s == "gc")], tile, ACT.Sigmoid, bias=bg[:, b:b + 1]), n)
                elif s == "up":
                    tiles.read(a.activation(ff[:, m], tile, ACT.Relu), n)
                elif s == "pp":
                    tiles.read(a.copy(pt[:, h, m], tile), n)
                elif s == "gate":
                    if gates >= 2:
                        a.wait_ge(sgt_used, gates - 1)
                    tiles.read(a.activation(sgt[:, gates % 2], tile, ACT.Sigmoid), n)
                    gates += 1
                elif s == "q2":
                    tiles.read(a.mul(q2[:, m, cols(h)], tile, HD ** -0.5), n)
                elif s == "kv2":
                    tiles.read(a.copy(kv2[:, m, cols(h)], tile), n)
                elif s == "vsvw":
                    both = k.data(4096, 2, 8, P)[:, :, 4 * h + m]
                    tiles.read(a.copy(both, tiles.bank(n, 256).rearrange("p (b c) -> p b c", b=2)), n)
                elif s == "gl":
                    tiles.read(a.activation(gl[:, 4 * h + m], tiles.bank(n, 24), ACT.Sigmoid), n)
                if (st, h, i) in sums_after:
                    sums += 1
                    a.wait_ge(ss_done, sums)
                    if sums > 1:
                        a.wait_ge(root_used, sums - 1)
                    a.activation(root, k.bank(4 + sums % 2), ACT.Sqrt, bias=k.eps, scale=1.0 / D).then_inc(root_done, 1)

        @block.vector
        def _(v):
            state = Shared(sums=0, gates=0)

            def finish_sum(n):
                v.wait_ge(k.vec.sem, n)
                v.nop().then_inc(ss_ready, 1)
                state.sums += 1
                v.wait_ge(root_done, state.sums)
                v.reciprocal(rstd, root).then_inc(root_used, 1)
                v.wait_ge(root_used, state.sums)

            def normed(h, g):
                for t in range(KT):
                    v.scalar_tensor_tensor(k.hT[:, t, cols(h)], k.xT[:, t, cols(h)], k.const(g)[:, t:t + 1], rstd,
                                           ALU.mult, ALU.mult).then_inc(h_ready, 1)

            def add_square(i, tile):
                n = k.vec.inc(v.tensor_tensor(sq[i % 2], tile, tile, ALU.mult))
                v.wait_ge(k.vec.sem, n)
                if i == 0:
                    return k.vec.inc(v.tensor_copy(acc, sq[0]))
                return k.vec.inc(v.tensor_tensor(acc, acc, sq[i % 2], ALU.add))

            def add_to_x(t, h, term):
                n = k.vec.inc(v.tensor_tensor(k.xT[:, t, cols(h)], k.xT[:, t, cols(h)], term, ALU.add))
                v.wait_ge(k.vec.sem, n)

            def residual(h, n, post, pre):
                finish_sum(n)
                for t in range(KT):
                    n = k.vec.inc(v.scalar_tensor_tensor(tmp, f[:, t], k.const(post)[:, t:t + 1], rstd, ALU.mult,
                                                         ALU.mult))
                    v.wait_ge(k.vec.sem, n)
                    add_to_x(t, h, tmp)
                    n = add_square(t, k.xT[:, t, cols(h)])
                finish_sum(n)
                normed(h, pre)

            for n, (st, h, i, s, m) in enumerate(plan):
                tile = tiles.bank(n)
                if s in ("ya", "yc"):
                    gate = at["mix", h, "ga" if s == "ya" else "gc", m]
                    tiles.may_read(v, n)
                    v.wait_ge(tiles.emptied["a"], tiles.rank[gate])
                    if (h, m) > (0, 0):
                        v.wait_ge(mix_ready, 8 * h + m)
                    tiles.read(v.tensor_tensor(t1 if s == "ya" else t2, tile, sg[:, 2 * (m % 2) + (s == "yc")],
                                               ALU.mult), n)
                    if s == "yc":
                        v.wait_ge(tiles.emptied["v"], tiles.rank[n])
                        v.tensor_tensor(mix[:, m], t1, t2, ALU.add).then_inc(mix_ready, 1)
                elif s in ("wo", "down"):
                    tiles.may_read(v, n)
                    tiles.read(v.tensor_copy(f[:, m], tile), n)
                    v.wait_ge(tiles.emptied["v"], tiles.rank[n])
                    done = add_square(m, f[:, m])
                    if m == 7:
                        residual(h, done, *(("g_post_mix", "g_pre_mlp") if s == "wo" else ("g_post_mlp", "g_ple")))
                elif s == "up":
                    v.wait_ge(tiles.emptied["a"], tiles.rank[n])
                    v.tensor_tensor(ff[:, m], ff[:, m], ff[:, m], ALU.mult).then_inc(ff_ready, 1)
                elif s == "gate":
                    v.wait_ge(tiles.emptied["a"], tiles.rank[n])
                    v.tensor_tensor(upd, sgt[:, state.gates % 2], pt[:, h, m], ALU.mult).then_inc(sgt_used, 1)
                    state.gates += 1
                    v.wait_ge(sgt_used, state.gates)
                    add_to_x(m, h, upd)
                    done = add_square(m, k.xT[:, m, cols(h)])
                    if m == 7:
                        finish_sum(done)
                        normed(h, "norm_g_2")


CC = {}
_at = 0
for _name, _n in (("causal", 128), ("window", 640), ("cmp_add", 512), ("cmp_keep", 512), ("imp_add", 64),
                  ("imp_keep", 64), ("overlap", 64), ("earlier", 256), ("swap", 128)):
    CC[_name] = (_at, _n)
    _at += _n
CC_N = _at
assert CC_N <= 3072


def nsa_phase(k):
    nc, io = k.nc, k.io
    nt = S // P
    q2 = k.data(18432, 4, S)
    kc_vc, kskw = k.data(0, 2, S), k.data(2048, 2, S)
    vsvw, gl = k.data(4096, 2, nt, P), k.data(6144, nt, 3, 8)
    rope = k.data(6400, 2, S)
    acc, mixn = k.data(8448, nt, 512), k.data(12544, 4, S)
    kcmp, vcmp = k.data(16640, 64), k.data(16704, 64)
    st_max, st_sum, st_inv = k.data(16768, nt, 8), k.data(16832, nt, 8), k.data(16896, nt, 8)
    pg, pw, imp = k.data(16960, 2, 64), k.data(17088, 2, 64), k.data(17216, 8, 16)
    neg_max, sums = k.data(17344, 2 * 64), k.data(17472, 2 * 64)
    coef, rank, sel = k.data(17600, 16, 8), k.data(17728, 8, 16), k.data(17856, 8, 16)
    cs, pc, ptc = k.data(22528, 2, 512), k.data(23552, 2, 512), k.data(24576, 2, 512)
    rt = k.data(25600, 512)
    greater = k.data(22528, 8, 256)
    hv = lambda at, *shape: k.view(HT_AT + at, *shape)
    shifted, win_in = hv(0, 2, S), hv(2048, 16, P)
    hid, sig = hv(4096, 2, P), hv(4352, 2, P)
    ss, pp, pts = hv(0, 2, 1024), hv(2048, 2, 1024), hv(4096, 4, 512)
    equal = hv(6144, 8, 256)
    bias_at = (k.data(0, 2, 1024), k.data(6400, 2, 1024))
    o_tmp = rt

    def cst(name, *shape):
        return k.view(CP_AT + CC[name][0], *(shape or (CC[name][1],)))

    causal, window = cst("causal"), cst("window")

    def rows(g):
        return slice(64 * g, 64 * g + 64)

    passes = [(b, t, j, g) for b in (2, 1) for t in range(nt) for j in range(4) for g in range(2)]
    N = len(passes)

    def span(n):
        b, t, _, _ = passes[n]
        first = max(0, t - 4) if b == 2 else 0
        return first, t + 1 - first

    chunks = [(n, c) for n in range(N) for c in range((span(n)[1] + 3) // 4)]
    chunk_at = {nc_: i for i, nc_ in enumerate(chunks)}
    copier = ["a" if i % 2 else "v" for i in range(len(chunks))]
    copied_rank = [copier[:i + 1].count(copier[i]) for i in range(len(chunks))]

    def of(n):
        return [min(4, span(n)[1] - 4 * c) for c in range((span(n)[1] + 3) // 4)]

    sem = k.sem
    rope_in = sem("rope_in")
    swapped, swap_read, roped, scaled = sem("swapped"), sem("swap_read"), sem("roped"), sem("cos_scaled")
    sh_ready, wi_ready, hid_mm, sig_ready, hid_ready = (sem("shifted_ready"), sem("windows_ready"), sem("hidden_done"),
                                                        sem("sigmoid_ready"), sem("hidden_ready"))
    cmp_mm, cmp_ready = sem("cmp_done"), sem("cmp_ready")
    cs_mm, cs_ready, ce_ready, pc_ready = sem("cmp_scores"), sem("cmp_shifted"), sem("cmp_exp"), sem("cmp_probs")
    ct_mm, ct_ready, co_mm, co_read = sem("cmp_turned"), sem("cmp_turned_copied"), sem("cmp_out"), sem("cmp_out_read")
    s_mm, s_read, e_ready = sem("scores"), sem("scores_read"), sem("probs_ready")
    t_mm, t_copied = sem("turned"), {"a": sem("turned_copied_a"), "v": sem("turned_copied_v")}
    av_mm, o_mm, o_read = sem("attended"), sem("attended_tile"), sem("attended_read")
    bias_ready, sel_ready = sem("bias_ready"), sem("selection_ready")
    m_mm, m_read = sem("mix_turned"), sem("mix_copied")
    swaps = [(kskw, i, h) for i in range(2) for h in range(2)] + [(q2, j, h) for j in range(4) for h in range(2)]

    with nc.Block() as block:

        def copy_turned(eng, n, who):
            for c, w in enumerate(of(n)):
                i = chunk_at[n, c]
                if copier[i] != who:
                    continue
                eng.wait_ge(t_mm, i + 1)
                if i >= 4:
                    eng.wait_ge(av_mm, chunks[i - 4][0] + 1)
                copy = eng.copy if who == "a" else eng.tensor_copy
                copy(pts[:, i % 4, 0:w * P], k.bank(4 + i % 2, w * P)).then_inc(t_copied[who], 1)

        @block.sync
        def _(sp):
            sp.dma_start(k.view(CP_AT, CC_N), io["consts_c"]).then_inc(k.cp_in, 16)
            sp.dma_start(rope, io["rope"].rearrange("p (b s) -> p b s", b=2)).then_inc(rope_in, 16)
            for i, unit in enumerate(range(START["cmp"], START["in3", 0])):
                k.used[unit] = (hid_mm, i + 1)
            load_weights(k, sp, START["in3", 0] + RING)

        @block.tensor
        def _(pe):
            pe.wait_ge(k.cp_in, 32)
            ident = k.const("ident")

            def swap(i):
                x, j, h = swaps[i]
                if i >= 2:
                    pe.wait_ge(swap_read, i - 1)
                pe.matmul(k.bank(6 + i % 2), cst("swap"), x[:, j, h * HALF:(h + 1) * HALF], start=True,
                          stop=True).then_inc(swapped, 1)

            for i in range(4):
                swap(i)
            for x in range(2):
                pe.wait_ge(wi_ready, 4 * (x + 1))
                for b in range(2):
                    unit = START["cmp"] + 2 * x + b
                    block_landed(k, pe, unit)
                    w = k.slot(unit).rearrange("p (l c) -> p l c", l=8)
                    for ht in range(2):
                        for l in range(8):
                            last = pe.matmul(k.bank(2 * x + ht, P), w[:, l, ht * P:(ht + 1) * P], win_in[:, 8 * b + l],
                                             start=b == 0 and l == 0, stop=b == 1 and l == 7)
                    last.then_inc(hid_mm, 1)
                pe.wait_ge(hid_ready, 2 * (x + 1))
                w2 = k.const("w2k" if x == 0 else "w2v").rearrange("p (t c) -> p t c", t=2)
                for g in range(2):
                    for ht in range(2):
                        a_, b_ = (w2[:, ht], hid[:, ht, rows(g)]) if x == 0 else (hid[:, ht, rows(g)], w2[:, ht])
                        last = pe.matmul(k.bank(4 + x, 64)[rows(g)], a_, b_, start=ht == 0, stop=ht == 1)
                last.then_inc(cmp_mm, 1)
            pe.wait_ge(cmp_ready, 2)
            for t in range(nt + 1):
                if t < nt:
                    if t >= 2:
                        pe.wait_ge(cs_ready, t - 1)
                    for j in range(4):
                        for g in range(2):
                            last = pe.matmul(k.bank(2 * (t % 2) + g)[:, j * 64:(j + 1) * 64],
                                             q2[rows(g), j, t * P:(t + 1) * P], kcmp[rows(g)], start=True, stop=True)
                    last.then_inc(cs_mm, 1)
                if t >= 1:
                    u = t - 1
                    pe.wait_ge(pc_ready, u + 1)
                    if u >= 2:
                        pe.wait_ge(ct_ready, u - 1)
                    for j in range(4):
                        last = pe.transpose(k.bank(4 + u % 2)[:, j * P:(j + 1) * P], pc[:, u % 2, j * P:(j + 1) * P], ident)
                    last.then_inc(ct_mm, 1)
                    pe.wait_ge(ct_ready, u + 1)
                    if u >= 1:
                        pe.wait_ge(co_read, u)
                    for j in range(4):
                        for g in range(2):
                            last = pe.matmul(k.bank(6 + g)[:, j * 64:(j + 1) * 64], ptc[rows(g), u % 2, j * P:(j + 1) * P],
                                             vcmp[rows(g)], start=True, stop=True)
                    last.then_inc(co_mm, 1)
            pe.wait_ge(co_read, nt)
            for i in range(4, len(swaps)):
                swap(i)

            def score(n):
                b, t, j, g = passes[n]
                first, width = span(n)
                if n >= 2:
                    pe.wait_ge(s_read, n - 1)
                keys = kskw[rows(g), 0 if b == 1 else 1]
                for c in range(0, width, 4):
                    w = min(4, width - c)
                    last = pe.matmul(k.bank(2 * (n % 2) + c // 4, w * P), q2[rows(g), j, t * P:(t + 1) * P],
                                     keys[:, (first + c) * P:(first + c + w) * P], start=True, stop=True)
                last.then_inc(s_mm, 1)

            def turn(n):
                pe.wait_ge(e_ready, n + 1)
                for c, w in enumerate(of(n)):
                    i = chunk_at[n, c]
                    if i >= 2:
                        pe.wait_ge(t_copied[copier[i - 2]], copied_rank[i - 2])
                    for x in range(w):
                        at = (4 * c + x) * P
                        last = pe.transpose(k.bank(4 + i % 2)[:, x * P:(x + 1) * P], pp[:, n % 2, at:at + P], ident)
                    last.then_inc(t_mm, 1)

            def attend(n):
                b, t, j, g = passes[n]
                first, width = span(n)
                tile = n // 8
                if n % 8 == 0 and tile >= 2:
                    pe.wait_ge(o_read, tile - 1)
                for c, w in enumerate(of(n)):
                    i = chunk_at[n, c]
                    pe.wait_ge(t_copied[copier[i]], copied_rank[i])
                    for x in range(w):
                        kt = first + 4 * c + x
                        last = pe.matmul(k.bank(6 + tile % 2)[:, (n % 8) * 64:(n % 8) * 64 + 64],
                                         pts[:, i % 4, x * P:(x + 1) * P], vsvw[:, 0 if b == 1 else 1, kt, rows(g)],
                                         start=4 * c + x == 0, stop=4 * c + x == width - 1)
                last.then_inc(av_mm, 1)

            pe.wait_ge(roped, len(swaps))
            score(0)
            for n in range(N + 1):
                if n + 1 < N:
                    score(n + 1)
                if n < N:
                    turn(n)
                if n >= 1:
                    attend(n - 1)
            pe.wait_ge(o_read, N // 8)
            for i in range(8):
                j, h = i // 2, i % 2
                if i >= 2:
                    pe.wait_ge(m_read, i - 1)
                for x in range(4):
                    last = pe.transpose(k.bank(i % 2)[:, x * P:(x + 1) * P], acc[:, 4 * h + x, j * P:(j + 1) * P], ident)
                last.then_inc(m_mm, 1)

        @block.scalar
        def _(a):
            for x in range(2):
                if x == 1:
                    a.wait_ge(wi_ready, 4)
                for g in range(2):
                    a.copy(shifted[0:64, g], kc_vc[rows(g), x]).then_inc(sh_ready, 1)
                    a.copy(shifted[64:128, g, 0:S - 1], kc_vc[rows(g), x, 1:S]).then_inc(sh_ready, 1)
                a.wait_ge(hid_mm, 2 * (x + 1))
                if x == 1:
                    a.wait_ge(hid_ready, 2)
                for ht in range(2):
                    a.activation(sig[:, ht], k.bank(2 * x + ht, P), ACT.Sigmoid).then_inc(sig_ready, 1)
            for t in range(nt + 1):
                if t < nt:
                    a.wait_ge(cs_ready, 2 * t + 2)
                    a.activation(cs[:, t % 2], cs[:, t % 2], ACT.Exp).then_inc(ce_ready, 1)
                if t >= 1:
                    u = t - 1
                    a.wait_ge(ct_mm, u + 1)
                    if u >= 2:
                        a.wait_ge(co_mm, u - 1)
                    a.copy(ptc[:, u % 2], k.bank(4 + u % 2)).then_inc(ct_ready, 1)

            def probs(n):
                width = span(n)[1] * P
                a.wait_ge(s_read, n + 1)
                if n >= 2:
                    a.wait_ge(t_mm, chunk_at[n - 1, 0])
                a.activation(pp[:, n % 2, 0:width], ss[:, n % 2, 0:width], ACT.Exp, bias=neg_max[:, n:n + 1],
                             scale=-1.0, accum_out=sums[:, n:n + 1]).then_inc(e_ready, 1)

            probs(0)
            for n in range(N):
                if n + 1 < N:
                    probs(n + 1)
                copy_turned(a, n, "a")
            for i in range(8):
                j, h = i // 2, i % 2
                a.wait_ge(m_mm, i + 1)
                a.copy(mixn[:, j, h * HALF:(h + 1) * HALF], k.bank(i % 2)).then_inc(m_read, 1)

        @block.vector
        def _(v):
            v.wait_ge(k.cp_in, 32)
            v.wait_ge(rope_in, 16)

            def times_sin(i):
                h = swaps[i][2]
                v.wait_ge(swapped, i + 1)
                if i >= 1:
                    v.wait_ge(roped, i)
                v.tensor_tensor(rt, k.bank(6 + i % 2), rope[:, 1, h * HALF:(h + 1) * HALF], ALU.mult).then_inc(swap_read, 1)

            n = k.vec.inc(v.memset(win_in.rearrange("p l (g c) -> p l g c", g=2)[:, :, :, CMP_N:CMP_PAD], 0.0))
            for i in range(4):
                times_sin(i)
            for x in range(2):
                pos = k.const("pos_k" if x == 0 else "pos_v")
                if x == 1:
                    v.wait_ge(hid_mm, 2)
                for g in range(2):
                    v.wait_ge(sh_ready, 4 * x + 2 * g + 2)
                    src = shifted[:, g].rearrange("p (c l two) -> p l c two", l=8, two=2)[:, :, :, 0]
                    for b in range(2):
                        out = win_in.rearrange("p l (g c) -> p l g c", g=2)[:, 8 * b:8 * b + 8, g, 0:CMP_N]
                        v.tensor_tensor(out, src[:, :, b:b + CMP_N],
                                        pos[:, 8 * b:8 * b + 8].unsqueeze(2).to_broadcast((P, 8, CMP_N)),
                                        ALU.add).then_inc(wi_ready, 1)
                for ht in range(2):
                    v.wait_ge(sig_ready, 2 * x + ht + 1)
                    if x == 1:
                        v.wait_ge(cmp_mm, 1)
                    v.tensor_tensor(hid[:, ht], k.bank(2 * x + ht, P), sig[:, ht], ALU.mult).then_inc(hid_ready, 1)
                v.wait_ge(cmp_mm, x + 1)
                v.tensor_copy(kcmp if x == 0 else vcmp, k.bank(4 + x, 64)).then_inc(cmp_ready, 1)
            add = cst("cmp_add", nt, 64)
            keep = cst("cmp_keep", nt, 64)

            def per_head(tile):
                return tile.rearrange("p (h c) -> p h c", h=8)

            def by_group(tile):
                return tile.rearrange("p (j g c) -> p g j c", j=4, g=2)

            def two_banks(b):
                return k.ps[:, b * 512:(b + 2) * 512].rearrange("p (g j c) -> p g j c", g=2, c=64)[:, :, 0:4]

            def wide(cols, w=64):
                return cols.unsqueeze(2).to_broadcast((P, 8, w))

            def step(ins):
                v.wait_ge(k.vec.sem, k.vec.inc(ins))

            def cmp_scores(t):
                v.wait_ge(cs_mm, t + 1)
                tile = per_head(cs[:, t % 2])
                v.tensor_tensor(by_group(cs[:, t % 2]), two_banks(2 * (t % 2)),
                                add[:, t].unsqueeze(1).unsqueeze(1).to_broadcast((P, 2, 4, 64)),
                                ALU.add).then_inc(cs_ready, 1)
                v.wait_ge(cs_ready, 2 * t + 1)
                step(v.tensor_reduce(st_max[:, t], tile, AX, ALU.max))
                v.tensor_tensor(tile, tile, wide(st_max[:, t]), ALU.subtract).then_inc(cs_ready, 1)

            def cmp_probs(t):
                tile, out = per_head(cs[:, t % 2]), per_head(pc[:, t % 2])
                v.wait_ge(ce_ready, t + 1)
                step(v.tensor_reduce(st_sum[:, t], tile, AX, ALU.add))
                step(v.reciprocal(st_inv[:, t], st_sum[:, t]))
                if t >= 2:
                    v.wait_ge(ct_mm, t - 1)
                step(v.tensor_tensor(out, tile, keep[:, t].unsqueeze(1).to_broadcast((P, 8, 64)), ALU.mult))
                v.tensor_tensor(out, out, wide(st_inv[:, t]), ALU.mult).then_inc(pc_ready, 1)
                if t < 4:
                    return
                v.wait_ge(pc_ready, t + 1)
                step(v.tensor_reduce(pg, pc[:, t % 2].rearrange("p (j g c) -> p g c j", j=4, g=2), AX, ALU.add))
                step(v.tensor_tensor(pw, pg, cst("overlap").unsqueeze(1).to_broadcast((P, 2, 64)), ALU.mult))
                im = imp[:, 2 * (t - 4):2 * (t - 3)]
                four = pw.rearrange("p g (b f) -> p g b f", f=4)
                step(v.tensor_reduce(im, four, AX, ALU.add))
                step(v.tensor_tensor(im[:, :, 1:16], im[:, :, 1:16], four[:, :, 0:15, 3], ALU.add))
                step(v.tensor_tensor(im, im, cst("imp_keep", 4, 16)[:, t - 4].unsqueeze(1).to_broadcast((P, 2, 16)),
                                     ALU.mult))
                step(v.tensor_tensor(im, im, cst("imp_add", 4, 16)[:, t - 4].unsqueeze(1).to_broadcast((P, 2, 16)),
                                     ALU.add))

            def cmp_out(t):
                v.wait_ge(co_mm, t + 1)
                v.tensor_tensor(by_group(acc[:, t]), two_banks(6),
                                gl[:, t, 0].rearrange("p (j g) -> p g j", g=2).unsqueeze(3).to_broadcast((P, 2, 4, 64)),
                                ALU.mult).then_inc(co_read, 1)

            for t in range(nt + 2):
                if t < nt:
                    cmp_scores(t)
                if 1 <= t <= nt:
                    cmp_probs(t - 1)
                if t >= 2:
                    cmp_out(t - 2)
            for i in range(4, len(swaps)):
                times_sin(i)
            bj, bi = imp.unsqueeze(3).to_broadcast((P, 8, 16, 16)), imp.unsqueeze(2).to_broadcast((P, 8, 16, 16))
            four_d = lambda x: x.rearrange("p a (j i) -> p a j i", j=16)
            v.wait_ge(roped, 4)
            step(v.tensor_tensor(four_d(greater), bi, bj, ALU.is_gt))
            v.wait_ge(ct_ready, nt)
            step(v.tensor_tensor(four_d(equal), bi, bj, ALU.is_equal))
            step(v.tensor_tensor(equal, equal, cst("earlier").unsqueeze(1).to_broadcast((P, 8, 256)), ALU.mult))
            step(v.tensor_tensor(greater, greater, equal, ALU.add))
            step(v.tensor_reduce(rank, four_d(greater), AX, ALU.add))
            v.tensor_scalar(sel, rank, 7.5, NEG, ALU.is_gt, ALU.mult).then_inc(sel_ready, 1)

            def mask_scores(n):
                b, t, j, g = passes[n]
                width = span(n)[1] * P
                v.wait_ge(s_mm, n + 1)
                if n >= 2:
                    v.wait_ge(e_ready, n - 1)
                if b == 2:
                    bias = window[:, 640 - width:640]
                else:
                    v.wait_ge(bias_ready, t + 1)
                    bias = bias_at[t % 2][:, g, 0:width]
                v.tensor_tensor_reduce(ss[:, n % 2, 0:width], k.ps[:, 1024 * (n % 2):1024 * (n % 2) + width], bias,
                                       -1.0, 3e38, ALU.add, ALU.min, neg_max[:, n:n + 1]).then_inc(s_read, 1)

            def gather(tile):
                b, t = passes[8 * tile][:2]
                v.wait_ge(e_ready, 8 * tile + 8)
                step(v.reciprocal(coef[:, tile], sums[:, 8 * tile:8 * tile + 8]))
                step(v.tensor_tensor(coef[:, tile], coef[:, tile], gl[:, t, b], ALU.mult))
                v.wait_ge(av_mm, 8 * tile + 8)
                step(v.tensor_tensor(per_head(o_tmp), per_head(k.bank(6 + tile % 2)), wide(coef[:, tile]), ALU.mult))
                step(v.tensor_tensor(acc[:, t], acc[:, t], o_tmp, ALU.add))
                v.nop().then_inc(o_read, 1)

            mask_scores(0)
            for n in range(N):
                if n + 1 < N:
                    mask_scores(n + 1)
                if n % 8 == 1 and n > 8:
                    gather(n // 8 - 1)
                copy_turned(v, n, "v")
            gather(N // 8 - 1)

        @block.gpsimd
        def _(g_):
            g_.wait_ge(rope_in, 16)
            g_.wait_ge(k.cp_in, 32)
            for i, (x, j, h) in enumerate(swaps):
                tile = x[:, j, h * HALF:(h + 1) * HALF]
                g_.wait_ge(swapped, i + 1)
                if i >= 4:
                    g_.wait_ge(cs_mm, nt)
                g_.tensor_tensor(tile, tile, rope[:, 0, h * HALF:(h + 1) * HALF], ALU.mult).then_inc(scaled, 1)
                g_.wait_ge(scaled, i + 1)
                g_.wait_ge(swap_read, i + 1)
                g_.tensor_tensor(tile, tile, rt, ALU.add).then_inc(roped, 1)
            for t in range(nt):
                if t >= 2:
                    g_.wait_ge(s_read, 64 + 8 * (t - 1))
                else:
                    g_.wait_ge(roped, len(swaps))
                    g_.wait_ge(sh_ready, 8)
                for g in range(2):
                    tile = bias_at[t % 2][:, g, 0:(t + 1) * P]
                    if t < 4:
                        n = k.pool.inc(g_.memset(tile, 0.0))
                    else:
                        g_.wait_ge(sel_ready, 1)
                        n = k.pool.inc(g_.tensor_copy(
                            tile.rearrange("p (b c) -> p b c", c=64),
                            sel[:, 2 * (t - 4) + g, 0:2 * (t + 1)].unsqueeze(2).to_broadcast((P, 2 * (t + 1), 64))))
                    g_.wait_ge(k.pool.sem, n)
                    last = g_.tensor_tensor(tile[:, t * P:], tile[:, t * P:], causal, ALU.add)
                    if g == 0:
                        k.pool.inc(last)
                last.then_inc(bias_ready, 1)


CHUNK = 64
NCHUNK = S // CHUNK
LEVELS = 6
GN_EPS = 64e-5
DECAY = float(np.exp(-0.5))
CD = {}
_at = 0
for _name, _n in (("mask", 128), ("level", LEVELS * CHUNK), ("eye", CHUNK), ("up", 512), ("resets", 1024)):
    CD[_name] = (_at, _n)
    _at += _n
CD_N = _at - 1024
assert _at <= 3072


def gates_phase(k):
    nc, io = k.nc, k.io
    r3, k3, v3 = k.data(0, 4, S), k.data(4096, 4, S), k.data(8192, 4, S)
    mixn, wdad, gr = k.data(12544, 4, S), k.data(16640, 1, S), k.data(17664, 4, S)
    xb, sb = k.data(21760, 2, HALF), k.data(22784, 2, HALF)
    sq, acc, root, rstd, _ = norm_scratch(k)
    count = {"gnsa": 4, "r3": 4, "k3": 4, "v3": 4, "wdad": 1, "grwkv": 4}
    first = {"gnsa": 0, "r3": 2, "k3": 4, "v3": 6, "wdad": 8, "grwkv": 9}
    dest = {"r3": r3, "k3": k3, "v3": v3, "wdad": wdad}
    plan = [(h, s, m) for h in range(2) for s in count for m in range(count[s])]
    tiles = Tiles(k, "g", ["a"] * len(plan))
    for n, (h, s, m) in enumerate(plan):
        k.used[START["in3", h] + first[s] + m // 2] = (tiles.filled, n + 1)
    ss_ready, ss_done = k.sem("g_ss_ready"), k.sem("g_ss_done")
    root_done, h_ready = k.sem("g_root_done"), k.sem("g_h_ready")
    copied, gated = k.sem("gate_in_copied"), k.sem("gate_used")
    k.spilled = k.sem("spilled")

    with nc.Block() as block:

        @block.sync
        def _(sp):
            sp.dma_start(io["x_keep"], k.view(XT_AT, 8192)).then_inc(k.spilled, 16)
            load_weights(k, sp, START["wout", 0] + RING)
            sp.wait_ge(gated, 16)
            sp.dma_start(io["mix_keep"], k.data(12544, 4096)).then_inc(k.spilled, 16)
            sp.dma_start(io["gate_keep"], k.data(17664, 4096)).then_inc(k.spilled, 16)

        @block.tensor
        def _(pe):
            def total(h):
                pe.wait_ge(ss_ready, h + 1)
                pe.matmul(k.bank(4 + h), k.const("ones"), acc, start=True, stop=True).then_inc(ss_done, 1)

            total(0)
            for n, (h, s, m) in enumerate(plan):
                if (s, m) == ("gnsa", 0):
                    pe.wait_ge(h_ready, KT * (h + 1))
                unit = START["in3", h] + first[s] + m // 2
                block_landed(k, pe, unit)
                tiles.may_fill(pe, n)
                w = k.slot(unit).rearrange("p (t c) -> p t c", t=KT)
                for t in range(KT):
                    last = pe.matmul(tiles.bank(n), w[:, t, (m % 2) * P:(m % 2 + 1) * P],
                                     k.hT[:, t, h * HALF:(h + 1) * HALF], start=t == 0, stop=t == KT - 1)
                last.then_inc(tiles.filled, 1)
                if n == 1:
                    total(1)

        @block.scalar
        def _(a):
            def take_root(h):
                a.wait_ge(ss_done, h + 1)
                if h:
                    a.wait_ge(h_ready, 1)
                a.activation(root, k.bank(4 + h), ACT.Sqrt, bias=k.eps, scale=1.0 / D).then_inc(root_done, 1)

            take_root(0)
            gates = 0
            for n, (h, s, m) in enumerate(plan):
                cols = slice(h * HALF, (h + 1) * HALF)
                tiles.may_read(a, n)
                if s in ("gnsa", "grwkv"):
                    if gates >= 2:
                        a.wait_ge(gated, gates - 1)
                    a.copy(xb[:, gates % 2], tiles.bank(n)).then_inc(copied, 1)
                    tiles.read(a.activation(sb[:, gates % 2], tiles.bank(n), ACT.Sigmoid), n)
                    gates += 1
                else:
                    tiles.read(a.copy(dest[s][:, m, cols], tiles.bank(n)), n)
                if n == 1:
                    take_root(1)

        @block.vector
        def _(v):
            for h in range(2):
                cols = slice(h * HALF, (h + 1) * HALF)
                if h:
                    v.wait_ge(ss_done, h)
                n = square_sum(k, v, [k.xT[:, t, cols] for t in range(KT)], acc, sq)
                v.wait_ge(k.vec.sem, n)
                v.nop().then_inc(ss_ready, 1)
                v.wait_ge(root_done, h + 1)
                v.wait_ge(k.vec.sem, k.vec.inc(v.reciprocal(rstd, root)))
                for t in range(KT):
                    v.scalar_tensor_tensor(k.hT[:, t, cols], k.xT[:, t, cols], k.const("norm_g_2")[:, t:t + 1], rstd,
                                           ALU.mult, ALU.mult).then_inc(h_ready, 1)
            gates = 0
            for n, (h, s, m) in enumerate(plan):
                if s not in ("gnsa", "grwkv"):
                    continue
                cols = slice(h * HALF, (h + 1) * HALF)
                v.wait_ge(copied, gates + 1)
                v.wait_ge(tiles.emptied["a"], tiles.rank[n])
                x_, s_ = xb[:, gates % 2], sb[:, gates % 2]
                if s == "gnsa":
                    v.wait_ge(k.vec.sem, k.vec.inc(v.tensor_tensor(x_, x_, s_, ALU.mult)))
                    v.tensor_tensor(mixn[:, m, cols], mixn[:, m, cols], x_, ALU.mult).then_inc(gated, 1)
                else:
                    v.tensor_tensor(gr[:, m, cols], x_, s_, ALU.mult).then_inc(gated, 1)
                gates += 1


def rwkv_phase(k):
    nc, io = k.nc, k.io
    r3, k3, v3 = k.data(0, 4, S), k.data(4096, 4, S), k.data(8192, 4, S)
    wdad = k.data(16640, S)
    low = lambda at, *shape: k.view(XT_AT + at, *shape)
    L, A, KK = low(0, 4, S), low(4096, 4, S), low(8192, 4, S)
    dd, t0, t1, t2, t3 = low(12288, 2, S), low(14336, HALF), low(14848, HALF), low(15360, HALF), low(15872, HALF)
    mask, level = k.view(CP_AT + CD["mask"][0], P), k.view(CP_AT + CD["level"][0], LEVELS, CHUNK)
    eye, up = k.view(CP_AT + CD["eye"][0], CHUNK), k.view(CP_AT + CD["up"][0], 512)
    resets = k.view(CP_AT + CD["resets"][0], S)
    place = [12544]

    def buf(*shape):
        at = place[0]
        place[0] += int(np.prod(shape))
        assert place[0] <= DA
        if len(shape) == 4:
            return k.data(at, shape[0] * shape[1], shape[2] * shape[3]).rearrange(
                "p (a b) (c d) -> p a b c d", a=shape[0], c=shape[2])
        return k.data(at, *shape)

    ra, bk = buf(2, 4, P), buf(2, 4, P)
    er, ek = buf(2, 4, CHUNK), buf(2, 4, CHUNK)
    mm = buf(2, 2, 4, P)
    mab = buf(2, 4, CHUNK)
    off = buf(2, LEVELS, 4, CHUNK)
    tt, gg = buf(1, 4, CHUNK), buf(2, 4, CHUNK)
    xx = buf(2, 4, CHUNK)
    bkt, uv = buf(2, 4, P), buf(2, 4, P)
    zv, zz, st = buf(2, 4, CHUNK), buf(1, 4, CHUNK), buf(1, 4, CHUNK)
    sem = k.sem
    shifts = [wdad] + [x[:, m] for x in (r3, k3, v3) for m in range(4)]
    mu_at = [12] + list(range(12))
    mt = [(m, h) for m in range(4) for h in range(2)]

    diff_ready, shifted = sem("token_diff"), sem("token_shifted")
    tanh_done, wa_mm, wa_read = sem("tanh_done"), sem("decay_iclr_mm"), sem("decay_iclr_read")
    kq_ready, kn_mm, kn_root, kn_read = sem("kk_squares"), sem("kk_norm_mm"), sem("kk_norm_root"), sem("kk_norm_read")
    prep_done, resets_ready = sem("prep_done"), sem("resets_ready")

    def rows(e):
        return slice(64 * e, 64 * e + 64)

    with nc.Block() as block:

        @block.sync
        def _(sp):
            sp.wait_ge(k.spilled, 48)
            sp.dma_start(k.view(CP_AT, CD_N), io["consts_d"]).then_inc(k.cp_in, 16)

        @block.gpsimd
        def _(g):
            n = k.pool.inc(g.memset(resets, 1.0))
            g.wait_ge(k.pool.sem, n)
            g.memset(resets.rearrange("p (c t) -> p c t", t=CHUNK)[:, :, 0:1], 0.0).then_inc(resets_ready, 1)
            for i, x in enumerate(shifts):
                if i >= 2:
                    g.wait_ge(shifted, i - 1)
                d = dd[:, i % 2]
                g.tensor_tensor(d[:, 1:S], x[:, 0:S - 1], x[:, 1:S], ALU.subtract)
                g.tensor_scalar(d[:, 0:1], x[:, 0:1], -1.0, None, ALU.mult).then_inc(diff_ready, 1)

        @block.tensor
        def _(pe):
            pe.wait_ge(k.cp_in, 48)
            pe.wait_ge(tanh_done, 1)
            for i, (m, h) in enumerate(mt):
                cols = slice(h * HALF, (h + 1) * HALF)
                if i >= 2:
                    pe.wait_ge(wa_read, 2 * i - 2)
                pe.matmul(k.bank(2 * (i % 2)), up[0:64, m * P:(m + 1) * P], wdad[0:64, cols], start=True, stop=True)
                pe.matmul(k.bank(2 * (i % 2) + 1), up[64:128, m * P:(m + 1) * P], wdad[64:128, cols], start=True,
                          stop=True).then_inc(wa_mm, 1)
            for i in range(8):
                pe.wait_ge(kq_ready, i + 1)
                pe.matmul(k.bank(4 + i % 2), k.const("bones"), (t0, t1)[i % 2], start=True, stop=True).then_inc(kn_mm, 1)

        @block.scalar
        def _(a):
            a.wait_ge(shifted, 1)
            a.activation(wdad[0:64], wdad[0:64], ACT.Tanh).then_inc(tanh_done, 1)
            w0, a0 = k.const("decay_w0_2"), k.const("iclr_a0_2")
            for i, (m, h) in enumerate(mt):
                cols = slice(h * HALF, (h + 1) * HALF)
                a.wait_ge(wa_mm, i + 1)
                a.activation(L[:, m, cols], k.bank(2 * (i % 2)), ACT.Sigmoid, bias=w0[:, m:m + 1]).then_inc(wa_read, 1)
                a.activation(A[:, m, cols], k.bank(2 * (i % 2) + 1), ACT.Sigmoid,
                             bias=a0[:, m:m + 1]).then_inc(wa_read, 1)
            for i in range(8):
                a.wait_ge(kn_mm, i + 1)
                if i >= 2:
                    a.wait_ge(kn_read, i - 1)
                a.activation((t2, t3)[i % 2], k.bank(4 + i % 2), ACT.Sqrt).then_inc(kn_root, 1)

        @block.vector
        def _(v):
            def step(ins):
                v.wait_ge(k.vec.sem, k.vec.inc(ins))

            mu = k.const("shift_mu_2")
            for i, x in enumerate(shifts):
                v.wait_ge(diff_ready, i + 1)
                v.scalar_tensor_tensor(x, dd[:, i % 2], mu[:, mu_at[i]:mu_at[i] + 1], x, ALU.mult,
                                       ALU.add).then_inc(shifted, 1)
            kk_, ka = k.const("k_k_2"), k.const("k_a_2")
            v.wait_ge(shifted, 13)

            def normalise(i):
                m, h = mt[i]
                tile = KK[:, m, h * HALF:(h + 1) * HALF]
                v.wait_ge(kn_root, i + 1)
                root = (t2, t3)[i % 2]
                step(v.tensor_scalar(root, root, 1e-12, None, ALU.max))
                step(v.reciprocal(root, root))
                v.tensor_tensor(tile, tile, root, ALU.mult).then_inc(kn_read, 1)

            for i, (m, h) in enumerate(mt):
                cols = slice(h * HALF, (h + 1) * HALF)
                step(v.tensor_scalar(KK[:, m, cols], k3[:, m, cols], kk_[:, m:m + 1], None, ALU.mult))
                if i >= 2:
                    v.wait_ge(kn_mm, i - 1)
                v.tensor_tensor((t0, t1)[i % 2], KK[:, m, cols], KK[:, m, cols], ALU.mult).then_inc(kq_ready, 1)
                if i >= 1:
                    normalise(i - 1)
            normalise(7)
            v.wait_ge(resets_ready, 1)
            for m in range(4):
                v.wait_ge(wa_read, 4 * m + 4)
                v.tensor_tensor_scan(L[:, m], resets, L[:, m], 0.0, ALU.mult, ALU.add).then_inc(prep_done, 1)
            for i, (m, h) in enumerate(mt):
                cols = slice(h * HALF, (h + 1) * HALF)
                v.wait_ge(kn_read, 8)
                step(v.tensor_scalar(t0, A[:, m, cols], 1.0, ka[:, m:m + 1], ALU.subtract, ALU.mult))
                step(v.scalar_tensor_tensor(k3[:, m, cols], t0, 1.0, k3[:, m, cols], ALU.add, ALU.mult))
                step(v.tensor_tensor(A[:, m, cols], A[:, m, cols], KK[:, m, cols], ALU.mult))
            v.nop().then_inc(prep_done, 1)

    exp_ready, ops_ready, raw_mm, mm_ready, mab_ready = (sem("chunk_exp"), sem("chunk_operands"), sem("chunk_raw"),
                                                         sem("chunk_masked"), sem("chunk_mab"))
    off_ready, turn_mm, turn_read, zv_mm, zv_ready = (sem("chunk_levels"), sem("chunk_turned"), sem("chunk_turned_read"),
                                                      sem("chunk_zv_mm"), sem("chunk_zv"))
    x_mm, x_ready, w_mm, g_mm, t_ready, g_ready = (sem("inv_x_mm"), sem("inv_x"), sem("inv_w_mm"), sem("inv_g_mm"),
                                                   sem("inv_t"), sem("inv_g"))
    zs_mm, z_ready, u_mm, u_ready, y_mm, y_read, s_mm, s_ready = (
        sem("chunk_zs_mm"), sem("chunk_z"), sem("chunk_u_mm"), sem("chunk_u"), sem("chunk_y_mm"), sem("chunk_y"),
        sem("chunk_s_mm"), sem("chunk_state"))
    C = NCHUNK

    def at(c):
        return slice(c * CHUNK, (c + 1) * CHUNK)

    def four(b, width=CHUNK):
        return k.bank(b, 4 * width).rearrange("p (m c) -> p m c", m=4)

    def bc(x, n=4):
        return x.unsqueeze(1).to_broadcast((x.shape[0], n, x.shape[1]))

    with nc.Block() as block:

        @block.tensor
        def _(pe):
            ident = k.const("ident")

            def pairs(bank, lhs, rhs):
                for m in range(4):
                    for e in range(2):
                        last = pe.matmul(four(bank)[rows(e), m], lhs(m, e), rhs(m, e), start=True, stop=True)
                return last

            def raw(c):
                pe.wait_ge(ops_ready, c + 1)
                if c >= 1:
                    pe.wait_ge(zv_ready, c)
                    pe.wait_ge(turn_read, 2 * c)
                for e in range(2):
                    for m in range(4):
                        last = pe.matmul(four(e, P)[:, m], bk[rows(e), c % 2, m], ra[rows(e), c % 2, m], start=True,
                                         stop=True)
                last.then_inc(raw_mm, 1)

            def turn(c):
                pe.wait_ge(mm_ready, 2 * c + 2)
                for m in range(4):
                    last = pe.transpose(four(0, P)[:, m], bk[:, c % 2, m], ident)
                last.then_inc(turn_mm, 1)
                for m in range(4):
                    vt = k.data(8192 + m * S + c * CHUNK - CHUNK, P)
                    last = pe.transpose(four(1, P)[:, m], vt, ident)
                last.then_inc(turn_mm, 1)

            def value_part(c):
                pe.wait_ge(turn_read, 2 * c + 2)
                pairs(0, lambda m, e: mm[64:128, c % 2, e, m, 64:128],
                      lambda m, e: uv[64:128, c % 2, m, 64 * e:64 * e + 64]).then_inc(zv_mm, 1)

            def inv_x(c, l):
                pe.wait_ge(off_ready, LEVELS * c + l + 1)
                if l == 0:
                    pairs(2, lambda m, e: off[rows(e), c % 2, 0, m], lambda m, e: eye[rows(e)]).then_inc(x_mm, 1)
                else:
                    pe.wait_ge(t_ready, (LEVELS - 1) * c + l)
                    pairs(2, lambda m, e: off[rows(e), c % 2, l, m], lambda m, e: tt[rows(e), 0, m]).then_inc(x_mm, 1)

            def inv_w(c, l):
                pe.wait_ge(x_ready, (LEVELS - 1) * c + l)
                pe.wait_ge(g_ready, LEVELS * c + l)
                if l < LEVELS - 1:
                    pairs(3, lambda m, e: gg[rows(e), c % 2, m], lambda m, e: xx[rows(e), l % 2, m]).then_inc(w_mm, 1)
                pairs(4, lambda m, e: xx[rows(e), l % 2, m], lambda m, e: gg[rows(e), c % 2, m]).then_inc(g_mm, 1)

            def state_part(c):
                if c >= 1:
                    pe.wait_ge(s_ready, c)
                pairs(5, lambda m, e: ra[rows(e), c % 2, m, 64:128], lambda m, e: st[rows(e), 0, m]).then_inc(zs_mm, 1)

            def solve(c):
                pe.wait_ge(z_ready, c + 1)
                pe.wait_ge(g_ready, LEVELS * (c + 1))
                pairs(6, lambda m, e: gg[rows(e), c % 2, m], lambda m, e: zz[rows(e), 0, m]).then_inc(u_mm, 1)

            def outputs(c):
                pe.wait_ge(u_ready, 2 * c + 2)
                for m in range(4):
                    for e in range(2):
                        last = pe.matmul(four(5)[rows(e), m], bkt[:, c % 2, m, rows(e)], uv[:, c % 2, m, rows(e)],
                                         start=True, stop=True)
                last.then_inc(s_mm, 1)
                if c >= 1:
                    pe.wait_ge(y_read, c)
                for m in range(4):
                    for e in range(2):
                        pe.matmul(four(7)[rows(e), m], st[rows(e), 0, m], ra[rows(e), c % 2, m, 0:64], start=True,
                                  stop=False)
                        last = pe.matmul(four(7)[rows(e), m], uv[:, c % 2, m, rows(e)], mm[:, c % 2, e, m, 0:64],
                                         start=False, stop=True)
                last.then_inc(y_mm, 1)

            for c in range(C + 1):
                if c < C:
                    raw(c)
                if c >= 1:
                    state_part(c - 1)
                if c < C:
                    inv_x(c, 0)
                    turn(c)
                if c >= 1:
                    solve(c - 1)
                if c < C:
                    inv_x(c, 1)
                    value_part(c)
                    inv_w(c, 1)
                if c >= 1:
                    outputs(c - 1)
                if c < C:
                    for l in range(2, LEVELS):
                        inv_x(c, l)
                        inv_w(c, l)

        @block.scalar
        def _(a):
            a.wait_ge(prep_done, 5)

            def exps(c):
                if c >= 2:
                    a.wait_ge(ops_ready, c - 1)
                    a.wait_ge(s_ready, c - 1)
                a.activation(er[:, c % 2], L[:, :, at(c)], ACT.Exp, scale=-DECAY)
                a.activation(ek[:, c % 2], L[:, :, at(c)], ACT.Exp, scale=DECAY).then_inc(exp_ready, 1)

            exps(0)
            for c in range(C + 1):
                if c < C:
                    a.wait_ge(mm_ready, 2 * c + 2)
                    if c >= 2:
                        a.wait_ge(off_ready, LEVELS * (c - 1))
                    a.copy(mab[0:64, c % 2], mm[0:64, c % 2, 0, :, 64:128])
                    a.copy(mab[64:128, c % 2], mm[0:64, c % 2, 1, :, 64:128]).then_inc(mab_ready, 1)
                    a.wait_ge(turn_mm, 2 * c + 1)
                    if c >= 2:
                        a.wait_ge(y_mm, c - 1)
                    a.copy(bkt[:, c % 2], four(0, P)).then_inc(turn_read, 1)
                    a.wait_ge(turn_mm, 2 * c + 2)
                    a.copy(uv[64:128, c % 2], four(1, P)[64:128]).then_inc(turn_read, 1)
                if c >= 1:
                    a.wait_ge(u_mm, c)
                    for e in range(2):
                        a.copy(uv[0:64, (c - 1) % 2, :, rows(e)], four(6)[rows(e)]).then_inc(u_ready, 1)
                if c < C:
                    for l in range(1, LEVELS):
                        a.wait_ge(x_mm, LEVELS * c + l + 1)
                        n = (LEVELS - 1) * c + l
                        if n > 2:
                            a.wait_ge(g_mm, n - 2)
                        a.copy(xx[:, l % 2], four(2)).then_inc(x_ready, 1)
                        if l == 2 and c >= 1:
                            a.wait_ge(y_mm, c)
                            a.copy(A[:, :, at(c - 1)], four(7)).then_inc(y_read, 1)
                        if l == 2 and c + 1 < C:
                            exps(c + 1)
                else:
                    a.wait_ge(y_mm, c)
                    a.copy(A[:, :, at(c - 1)], four(7)).then_inc(y_read, 1)

        @block.vector
        def _(v):
            def step(ins):
                v.wait_ge(k.vec.sem, k.vec.inc(ins))

            step(v.memset(st, 0.0))

            def combine(c):
                v.wait_ge(zs_mm, c + 1)
                v.wait_ge(zv_ready, c + 1)
                if c >= 1:
                    v.wait_ge(u_mm, c)
                v.tensor_tensor(zz[:, 0], four(5), zv[:, c % 2], ALU.add).then_inc(z_ready, 1)

            def next_state(c):
                v.wait_ge(s_mm, c + 1)
                v.wait_ge(y_mm, c + 1)
                step(v.tensor_tensor(st[:, 0], st[:, 0], four(5), ALU.add))
                v.tensor_tensor(st[:, 0], st[:, 0], er[:, c % 2, :, CHUNK - 1:CHUNK].to_broadcast((P, 4, CHUNK)),
                                ALU.mult).then_inc(s_ready, 1)

            for c in range(C + 1):
                if c < C:
                    v.wait_ge(raw_mm, c + 1)
                    if c >= 2:
                        v.wait_ge(y_mm, c - 1)
                    for e in range(2):
                        v.tensor_tensor(mm[:, c % 2, e], four(e, P), bc(mask), ALU.mult).then_inc(mm_ready, 1)
                if c >= 1:
                    combine(c - 1)
                if c < C:
                    v.wait_ge(off_ready, LEVELS * c + 1)
                    v.tensor_tensor(gg[:, c % 2], off[:, c % 2, 0], bc(eye), ALU.add).then_inc(g_ready, 1)
                    v.wait_ge(x_mm, LEVELS * c + 1)
                    v.tensor_tensor(tt[:, 0], four(2), bc(eye), ALU.add).then_inc(t_ready, 1)
                    v.wait_ge(zv_mm, c + 1)
                    v.tensor_copy(zv[:, c % 2], four(0)).then_inc(zv_ready, 1)
                    for l in range(1, LEVELS):
                        if l < LEVELS - 1:
                            v.wait_ge(w_mm, (LEVELS - 2) * c + l)
                            v.wait_ge(t_ready, (LEVELS - 1) * c + l)
                            v.tensor_tensor(tt[:, 0], tt[:, 0], four(3), ALU.add).then_inc(t_ready, 1)
                        v.wait_ge(g_mm, (LEVELS - 1) * c + l)
                        v.wait_ge(g_ready, LEVELS * c + l)
                        v.tensor_tensor(gg[:, c % 2], gg[:, c % 2], four(4), ALU.add).then_inc(g_ready, 1)
                        if l == 1 and c >= 1:
                            next_state(c - 1)
                else:
                    next_state(c - 1)

        @block.gpsimd
        def _(g):
            def operands(c):
                g.wait_ge(exp_ready, c + 1)
                if c >= 2:
                    g.wait_ge(y_mm, c - 1)
                    g.wait_ge(turn_read, 2 * c - 3)
                o = ra[:, c % 2]
                g.tensor_tensor(o[:, :, 0:64], r3[:, :, at(c)], er[:, c % 2], ALU.mult)
                g.tensor_scalar(o[:, :, 64:65], KK[:, :, c * CHUNK:c * CHUNK + 1], -1.0, None, ALU.mult)
                n = k.pool.inc(g.tensor_scalar(er_neg, er[:, c % 2], -1.0, None, ALU.mult))
                g.wait_ge(k.pool.sem, n)
                k.pool.inc(g.tensor_tensor(o[:, :, 65:128], KK[:, :, c * CHUNK + 1:(c + 1) * CHUNK],
                                           er_neg[:, :, 0:63], ALU.mult))
                o = bk[:, c % 2]
                g.tensor_tensor(o[:, :, 0:64], A[:, :, at(c)], ek[:, c % 2], ALU.mult)
                g.tensor_tensor(o[:, :, 64:128], k3[:, :, at(c)], ek[:, c % 2], ALU.mult).then_inc(ops_ready, 1)
                g.wait_ge(k.pool.sem, k.pool.n)

            er_neg = low(12288, 4, CHUNK)
            operands(0)
            for c in range(C):
                g.wait_ge(mab_ready, c + 1)
                for l in range(LEVELS):
                    if c >= 2:
                        g.wait_ge(x_mm, LEVELS * (c - 1))
                    g.tensor_tensor(off[:, c % 2, l], mab[:, c % 2], bc(level[:, l]), ALU.mult).then_inc(off_ready, 1)
                if c + 1 < C:
                    operands(c + 1)

    gate_in, back = sem("gate_in"), sem("restored")
    q1_ready, mean_mm, d_ready, q2_ready, var_mm, root2 = (sem("y_mean_in"), sem("y_mean_mm"), sem("y_centred"),
                                                           sem("y_var_in"), sem("y_var_mm"), sem("y_root"))
    bo_in, bo_mm, done = sem("bonus_in"), sem("bonus_mm"), sem("recurrent_done")
    gn_eps_ready = sem("gn_eps_ready")
    gr, sq2, bon = k.data(12544, 4, S), k.data(16640, 2, HALF), k.data(17664, 2, HALF)
    rr, cc = k.data(18688, 2, HALF), k.data(19712, 2, HALF)
    k.recurrent_done = done
    k.restored = back

    with nc.Block() as block:

        @block.sync
        def _(sp):
            sp.dma_start(k.data(12544, 4096), io["gate_keep"]).then_inc(gate_in, 16)

        @block.tensor
        def _(pe):
            def mean(i):
                m, h = mt[i]
                if i >= 2:
                    pe.wait_ge(d_ready, i - 1)
                pe.matmul(k.bank(i % 2), k.const("bones"), A[:, m, h * HALF:(h + 1) * HALF], start=True,
                          stop=True).then_inc(mean_mm, 1)
                pe.wait_ge(bo_in, i + 1)
                if i >= 2:
                    pe.wait_ge(done, i - 1)
                pe.matmul(k.bank(4 + i % 2), k.const("bones"), bon[:, i % 2], start=True, stop=True).then_inc(bo_mm, 1)

            mean(0)
            for i in range(8):
                if i + 1 < 8:
                    mean(i + 1)
                pe.wait_ge(q2_ready, i + 1)
                if i >= 2:
                    pe.wait_ge(root2, i - 1)
                pe.matmul(k.bank(2 + i % 2), k.const("bones"), sq2[:, i % 2], start=True, stop=True).then_inc(var_mm, 1)

        @block.scalar
        def _(a):
            for i in range(8):
                a.wait_ge(var_mm, i + 1)
                if i == 0:
                    a.wait_ge(gn_eps_ready, 1)
                if i >= 2:
                    a.wait_ge(done, i - 1)
                a.activation(rr[:, i % 2], k.bank(2 + i % 2), ACT.Sqrt, bias=k.gn_eps, scale=1.0 / HD).then_inc(root2, 1)

        @block.gpsimd
        def _(g):
            g.memset(k.gn_eps, GN_EPS).then_inc(gn_eps_ready, 1)
            rk = k.const("r_k_2")
            for i, (m, h) in enumerate(mt):
                cols = slice(h * HALF, (h + 1) * HALF)
                if i >= 2:
                    g.wait_ge(bo_mm, i - 1)
                n = k.pool.inc(g.tensor_tensor(bon[:, i % 2], r3[:, m, cols], k3[:, m, cols], ALU.mult))
                g.wait_ge(k.pool.sem, n)
                g.tensor_scalar(bon[:, i % 2], bon[:, i % 2], rk[:, m:m + 1], None, ALU.mult).then_inc(bo_in, 1)
                g.wait_ge(d_ready, i + 1)
                if i >= 2:
                    g.wait_ge(var_mm, i - 1)
                g.wait_ge(bo_in, i + 1)
                g.tensor_tensor(sq2[:, i % 2], cc[:, i % 2], cc[:, i % 2], ALU.mult).then_inc(q2_ready, 1)

        @block.vector
        def _(v):
            def step(ins):
                v.wait_ge(k.vec.sem, k.vec.inc(ins))

            gw, gb = k.const("gn_w_2"), k.const("gn_b_2")

            def centre(i):
                m, h = mt[i]
                v.wait_ge(mean_mm, i + 1)
                if i >= 2:
                    v.wait_ge(done, i - 1)
                    v.wait_ge(q2_ready, i - 1)
                v.scalar_tensor_tensor(cc[:, i % 2], k.bank(i % 2), -1.0 / HD, A[:, m, h * HALF:(h + 1) * HALF],
                                       ALU.mult, ALU.add).then_inc(d_ready, 1)

            centre(0)
            v.wait_ge(gate_in, 16)
            for i, (m, h) in enumerate(mt):
                cols = slice(h * HALF, (h + 1) * HALF)
                if i + 1 < 8:
                    centre(i + 1)
                v.wait_ge(root2, i + 1)
                x, c_ = rr[:, i % 2], cc[:, i % 2]
                step(v.reciprocal(x, x))
                step(v.tensor_tensor(c_, c_, x, ALU.mult))
                step(v.tensor_scalar(c_, c_, gw[:, m:m + 1], gb[:, m:m + 1], ALU.mult, ALU.add))
                v.wait_ge(bo_mm, i + 1)
                step(v.tensor_tensor(x, k.bank(4 + i % 2), v3[:, m, cols], ALU.mult))
                step(v.tensor_tensor(c_, c_, x, ALU.add))
                v.tensor_tensor(gr[:, m, cols], gr[:, m, cols], c_, ALU.mult).then_inc(done, 1)


def output_phase(k):
    nc, io = k.nc, k.io
    mixr, mixn = k.data(12544, 4, S), k.data(0, 4, S)
    sq, acc, root, rstd, _ = norm_scratch(k)
    plan = [(h, m) for h in range(2) for m in range(8)]
    tiles = Tiles(k, "out", ["v"] * 16)
    for n, (h, m) in enumerate(plan):
        k.used[START["wout", h] + m // 2] = (tiles.filled, n + 1)
    ss_ready, ss_done, root_done = k.sem("out_ss_ready"), k.sem("out_ss_done"), k.sem("out_root_done")
    mix_in, x_in, out_ready, stored = k.sem("mix_in"), k.sem("x_back"), k.sem("out_ready"), k.sem("stored")

    with nc.Block() as block:

        @block.sync
        def _(sp):
            sp.dma_start(k.data(0, 4096), io["mix_keep"]).then_inc(mix_in, 16)
            sp.dma_start(k.view(XT_AT, 8192), io["x_keep"]).then_inc(x_in, 16)
            load_weights(k, sp, START["end"])
            for h in range(2):
                sp.wait_ge(out_ready, h + 1)
                sp.dma_start(io["out"].rearrange("(t p) s -> p t s", p=P)[:, :, h * HALF:(h + 1) * HALF],
                             k.hT[:, :, h * HALF:(h + 1) * HALF]).then_inc(stored, 16)
            sp.wait_ge(stored, 32)

        @block.tensor
        def _(pe):
            pe.wait_ge(mix_in, 16)
            for n, (h, m) in enumerate(plan):
                unit = START["wout", h] + m // 2
                block_landed(k, pe, unit)
                tiles.may_fill(pe, n)
                w = k.slot(unit).rearrange("p (t c) -> p t c", t=KT)
                for t in range(KT):
                    src = (mixn if t < 4 else mixr)[:, t % 4, h * HALF:(h + 1) * HALF]
                    last = pe.matmul(tiles.bank(n), w[:, t, (m % 2) * P:(m % 2 + 1) * P], src, start=t == 0,
                                     stop=t == KT - 1)
                last.then_inc(tiles.filled, 1)
                if n in (9, 15):
                    pe.wait_ge(ss_ready, 1 if n == 9 else 2)
                    pe.matmul(k.bank(4 + n % 2), k.const("ones"), acc, start=True, stop=True).then_inc(ss_done, 1)

        @block.scalar
        def _(a):
            for h in range(2):
                a.wait_ge(ss_done, h + 1)
                if h:
                    a.wait_ge(out_ready, 1)
                a.activation(root, k.bank(5), ACT.Sqrt, bias=k.eps, scale=1.0 / D).then_inc(root_done, 1)

        @block.vector
        def _(v):
            g = k.const("final_g_2")
            v.wait_ge(x_in, 16)
            for n, (h, m) in enumerate(plan):
                cols = slice(h * HALF, (h + 1) * HALF)
                x = k.xT[:, m, cols]
                tiles.may_read(v, n)
                tiles.read(v.tensor_tensor(x, x, tiles.bank(n), ALU.add), n)
                v.wait_ge(tiles.emptied["v"], n + 1)
                last = k.vec.inc(v.tensor_tensor(sq[m % 2], x, x, ALU.mult))
                v.wait_ge(k.vec.sem, last)
                if m == 0:
                    last = k.vec.inc(v.tensor_copy(acc, sq[0]))
                else:
                    last = k.vec.inc(v.tensor_tensor(acc, acc, sq[m % 2], ALU.add))
                if m == 7:
                    v.wait_ge(k.vec.sem, last)
                    v.nop().then_inc(ss_ready, 1)
                    v.wait_ge(root_done, h + 1)
                    v.wait_ge(k.vec.sem, k.vec.inc(v.reciprocal(rstd, root)))
                    for t in range(KT):
                        last = k.vec.inc(v.scalar_tensor_tensor(k.hT[:, t, cols], k.xT[:, t, cols], g[:, t:t + 1], rstd,
                                                                ALU.mult, ALU.mult))
                    v.wait_ge(k.vec.sem, last)
                    v.nop().then_inc(out_ready, 1)


KEPT = {"x_keep": 8192, "mix_keep": 4096, "gate_keep": 4096}

def pack(inputs):
    f = {n: np.asarray(a) for n, a in inputs.items()}
    z = np.float32

    def cols(w, c0, n=256):
        b = np.zeros((w.shape[0], 256), z)
        b[:, :n] = w[:, c0:c0 + n]
        return b.reshape(-1, P, 256).transpose(1, 0, 2).reshape(P, -1)

    w = f["w_in"][0]
    blocks = {}
    for i, part in enumerate(("q", "k", "v", "cb", "cc", "cu")):
        for j in range(2):
            blocks[part, j] = cols(w, i * 512 + j * 256)
    for j in range(4):
        blocks["ga", j] = cols(w, 3072 + j * 256)
        blocks["gc", j] = cols(w, 4096 + j * 256)
        blocks["aoco", j] = np.concatenate([cols(f["w_attn_out"][0], j * 256), cols(f["w_conv_out"][0], j * 256)], 1)
        blocks["wo", j] = cols(f["w_o"][0], j * 256)
        blocks["gate", j] = cols(f["w_ple_gate"][0], j * 256)
    for j in range(16):
        blocks["up", j] = cols(f["w_up"][0], j * 256)
    wd = f["w_down"][0].reshape(2, 16, P, 8, P)
    for m in range(8):
        for j in range(2):
            blocks["down", 2 * m + j] = wd[j, :, :, m, :].transpose(1, 0, 2).reshape(P, -1)
    blocks["pp", 0] = f["w_ple_proj"][0].reshape(2, P, D).transpose(1, 0, 2).reshape(P, -1)

    order = np.concatenate([np.r_[j * 64:(j + 1) * 64, (4 + j) * 64:(5 + j) * 64] for j in range(4)])
    w = f["w_in_2"][0]
    w2 = {"q": w[:, 0:512][:, order], "kc": w[:, 512:640], "vc": w[:, 640:768], "ks": w[:, 768:896],
          "vs": w[:, 896:1024], "kw": w[:, 1024:1152], "vw": w[:, 1152:1280], "gl": w[:, 1280:1304],
          "gnsa": w[:, 1304:1816][:, order], "r": w[:, 1816:2328], "k": w[:, 2328:2840], "v": w[:, 2840:3352],
          "wdad": w[:, 3352:3480], "grwkv": w[:, 3480:3992]}
    for j in range(2):
        blocks["q2", j] = cols(w2["q"], j * 256)
        blocks["gnsa", j] = cols(w2["gnsa"], j * 256)
        blocks["grwkv", j] = cols(w2["grwkv"], j * 256)
        for part in "rkv":
            blocks[part + "3", j] = cols(w2[part], j * 256)
    blocks["kcvc", 0] = cols(np.concatenate([w2["kc"], w2["vc"]], 1), 0)
    blocks["kskw", 0] = cols(np.concatenate([w2["ks"], w2["kw"]], 1), 0)
    blocks["vsvw", 0] = cols(np.concatenate([w2["vs"], w2["vw"]], 1), 0)
    gl = w2["gl"].reshape(D, 2, 4, 3).transpose(0, 3, 2, 1).reshape(D, 24)
    blocks["gl", 0] = cols(gl, 0, 24)
    blocks["wdad", 0] = cols(w2["wdad"], 0, 128)
    for name in "kv":
        w1 = f[f"cmp_w1_{name}_2"][0].reshape(16, P, 256)
        for j in range(2):
            blocks["w1" + name, j] = w1[8 * j:8 * j + 8].transpose(1, 0, 2).reshape(P, -1)
    wout = f["w_out_2"][0]
    wout = np.concatenate([wout[:512][order], wout[512:]], 0)
    for j in range(4):
        blocks["wout", j] = cols(wout, j * 256)
    weights = np.stack([blocks[n] for n in BLOCKS])

    def col(a):
        return np.asarray(a).reshape(-1, P).T

    c = np.zeros((P, CA_N), z)

    def put(name, a):
        at, n = CA[name]
        c[:, at:at + n] = a

    put("ident", np.eye(P, dtype=z))
    put("ones", np.ones((P, P), z))
    put("bones", np.kron(np.eye(2, dtype=z), np.ones((64, 64), z)))
    for name in ("g_pre_mix", "b_gate", "g_post_mix", "g_pre_mlp", "g_post_mlp", "g_ple", "norm_g_2", "shift_mu_2",
                 "decay_w0_2", "iclr_a0_2", "k_k_2", "k_a_2", "r_k_2", "gn_w_2", "gn_b_2"):
        put(name, col(f[name][0]))
    put("final_g_2", col(f["final_g_2"]))
    put("w_conv", f["w_conv"][0].reshape(3, 4, P).transpose(2, 0, 1).reshape(P, 12))
    for name in "kv":
        put("pos_" + name, f[f"cmp_pos_{name}_2"][0].reshape(16, P).T)
        put("w2" + name, f[f"cmp_w2_{name}_2"][0].reshape(2, P, 64).transpose(1, 0, 2).reshape(P, 128))
    tri = np.zeros((P, CB_N), z)
    tri[:, :P] = -np.tril(np.ones((P, P), z))
    tri[:, P:] = -1.0
    pos, blk = np.arange(S), np.arange(16)
    cc = np.zeros((P, CC_N), z)

    def put_c(name, a):
        at, n = CC[name]
        cc[:, at:at + n] = np.asarray(a, z).reshape(-1, n)

    qi, ki = np.arange(P)[:, None], np.arange(P)[None, :]
    put_c("causal", np.where(ki <= qi, 0.0, NEG))
    wk = np.arange(640)[None, :] - 512
    put_c("window", np.where((qi - wk >= 0) & (qi - wk < 512), 0.0, NEG))
    ends = np.r_[np.arange(CMP_N) * 16 + 31, 1 << 20]
    keep = (ends[None, None, :] <= pos.reshape(8, P).T[:, :, None])
    put_c("cmp_add", np.where(keep, 0.0, NEG))
    put_c("cmp_keep", keep)
    tb = (pos // 64).reshape(8, P).T[:, 4:, None]
    forced = (blk == 0) | (blk == tb) | (blk == tb - 1)
    put_c("imp_keep", blk <= tb)
    put_c("imp_add", np.where(blk <= tb, 1e3 * forced, -1.0))
    put_c("overlap", np.tile(np.array([1, 1, 1, 0.5]), 16))
    put_c("earlier", (blk[None, :] < blk[:, None]).reshape(1, 256))
    swap = np.zeros((P, P), z)
    for base in (0, 64):
        for i in range(8):
            swap[base + i + 8, base + i] = swap[base + i, base + i + 8] = 1.0
    put_c("swap", swap)
    inv = np.float32(500000.0) ** (-np.arange(8, dtype=z) / np.float32(8))
    ang = pos.astype(z)[None, :] * inv.astype(z)[:, None]
    cos, sin = np.ones((64, S), z), np.zeros((64, S), z)
    cos[0:8] = cos[8:16] = np.cos(ang)
    sin[0:8], sin[8:16] = -np.sin(ang), np.sin(ang)
    rope = np.concatenate([np.tile(cos, (2, 1)), np.tile(sin, (2, 1))], 1)
    cd = np.zeros((P, CD_N), z)
    j, t = np.arange(64)[:, None], np.arange(64)[None, :]
    cd[:, :P] = np.tile(np.concatenate([t >= j, t > j], 1), (2, 1))
    at = CD["level"][0]
    for lv in range(LEVELS):
        s2 = 2 << lv
        here = (j // s2 == t // s2) & (j % s2 < s2 // 2) & (t % s2 >= s2 // 2)
        cd[:, at + lv * 64:at + (lv + 1) * 64] = np.tile(here, (2, 1))
    cd[:, CD["eye"][0]:CD["eye"][0] + 64] = np.tile(np.eye(64), (2, 1))
    cd[:, CD["up"][0]:CD["up"][0] + 512] = np.concatenate([f["decay_up_2"][0], f["iclr_up_2"][0]], 0)
    return {
        "consts_d": cd, "consts_c": cc, "rope": rope, "weights": weights, "consts": c, "consts_b": tri,
        "xT": np.ascontiguousarray(f["x"][0].T), "pT": np.ascontiguousarray(f["p"][0, 0].T),
    }


def kernel(**inputs):
    import concourse.bacc as bacc
    from concourse.bass_utils import run_bass_kernel_spmd

    nc = bacc.Bacc("TRN2", target_bir_lowering=False, num_devices=1)
    arrays = {"in_" + name: a for name, a in pack(inputs).items()}
    io = {name[3:]: nc.dram_tensor(name, a.shape, F32, kind="ExternalInput").ap() for name, a in arrays.items()}
    for name, n in KEPT.items():
        io[name] = nc.dram_tensor(name, (P, n), F32, kind="Internal").ap()
    io["out"] = nc.dram_tensor("out_T", (D, S), F32, kind="ExternalOutput").ap()
    build(nc, io)
    result = run_bass_kernel_spmd(nc, [arrays], core_ids=[0])
    return np.ascontiguousarray(result.results[0]["out_T"].T)[None]
```

```python
import numpy as np
from contextlib import ExitStack

import concourse.bass as bass
from concourse import mybir

F32 = mybir.dt.float32
F32R = mybir.dt.float32r
ALU = mybir.AluOpType
ACT = mybir.ActivationFunctionType
AX = mybir.AxisListType.X


class Shared:

    def __init__(self, nc=None, io=None, ps=None, sem=None, view=None, data=None, sums=0, gates=0):
        self.nc, self.io, self.ps = nc, io, ps
        self.sem, self.view, self.data = sem, view, data
        self.sums, self.gates = sums, gates

P = 128
S = 1024
D = 1024
KT = D // P
HALF = 512
HEADS, HD = 8, 64
FF = 4096
FF_PARTS = 4
CMP_N, CMP_PAD = 63, 64
EPS = 1e-6
NEG = -1e30

SLOT = 2048
RING = 3


def weight_blocks():
    names = []
    for part, n in (("cu", 2), ("cc", 2), ("cb", 2), ("q", 2), ("k", 2), ("v", 2), ("ga", 4), ("gc", 4),
                    ("aoco", 4), ("wo", 4), ("up", 16), ("down", 16), ("pp", 1), ("gate", 4),
                    ("q2", 2), ("kcvc", 1), ("kskw", 1), ("vsvw", 1), ("gl", 1), ("w1k", 2), ("w1v", 2),
                    ("gnsa", 2), ("r3", 2), ("k3", 2), ("v3", 2), ("wdad", 1), ("grwkv", 2), ("wout", 4)):
        names += [(part, i) for i in range(n)]
    return names


BLOCKS = weight_blocks()
BLOCK_AT = {name: i for i, name in enumerate(BLOCKS)}


def weight_order():
    order, start = [], {}

    def add(part, n):
        for i in range(n):
            order.append((part, i))

    for h in range(2):
        start["in", h] = len(order)
        for part, n in (("q", 2), ("k", 2), ("v", 2), ("cu", 2), ("cc", 2), ("cb", 2), ("ga", 4), ("gc", 4)):
            add(part, n)
    for h in range(2):
        start["mix", h] = len(order)
        add("aoco", 4)
        start["wo", h] = len(order)
        add("wo", 4)
    for h in range(2):
        start["mlp", h] = len(order)
        for c in range(FF_PARTS):
            order += [("up", 4 * c + i) for i in range(4)] + [("down", 4 * c + i) for i in range(4)]
    for h in range(2):
        start["gate", h] = len(order)
        add("gate", 4)
    for h in range(2):
        start["in2", h] = len(order)
        for part, n in (("q2", 2), ("kcvc", 1), ("kskw", 1), ("vsvw", 1), ("gl", 1)):
            add(part, n)
    start["cmp"] = len(order)
    add("w1k", 2)
    add("w1v", 2)
    for h in range(2):
        start["in3", h] = len(order)
        for part, n in (("gnsa", 2), ("grwkv", 2), ("r3", 2), ("k3", 2), ("v3", 2), ("wdad", 1)):
            add(part, n)
    for h in range(2):
        start["wout", h] = len(order)
        add("wout", 4)
    start["end"] = len(order)
    return order, start


ORDER, START = weight_order()

XT_AT = 0
HT_AT = 8192
RING_AT = 16384
CA_AT = RING_AT + RING * SLOT
CP_AT = CA_AT + 1024
DA_AT = CP_AT + 3072
ARENA = 53192
DA = ARENA - DA_AT
HI_AT = DA - 2 * SLOT

CA = {}
_at = 0
for _name, _n in (("ident", 128), ("ones", 128), ("bones", 128), ("g_pre_mix", 8), ("b_gate", 16),
                  ("w_conv", 12), ("g_post_mix", 8), ("g_pre_mlp", 8), ("g_post_mlp", 8), ("g_ple", 8),
                  ("norm_g_2", 8), ("shift_mu_2", 13), ("decay_w0_2", 4), ("iclr_a0_2", 4), ("k_k_2", 4),
                  ("k_a_2", 4), ("r_k_2", 4), ("gn_w_2", 4), ("gn_b_2", 4), ("final_g_2", 8),
                  ("pos_k", 16), ("pos_v", 16), ("w2k", 128), ("w2v", 128)):
    CA[_name] = (_at, _n)
    _at += _n
CA_N = _at
assert CA_N <= 1024
CB = {"negtri": (0, 128), "negones": (128, 128)}
CB_N = 256


class Count:

    def __init__(self, sem):
        self.sem, self.n = sem, 0

    def inc(self, ins):
        ins.then_inc(self.sem, 1)
        self.n += 1
        return self.n


def build(nc, io):
    with ExitStack() as ctx:
        gn_eps = ctx.enter_context(nc.sbuf_tensor("gn_eps", [P, 1], F32))[:, :]
        eps = ctx.enter_context(nc.sbuf_tensor("eps", [P, 1], F32))[:, :]
        base = -(-nc.sbuf_base // 64) * 64
        ps = ctx.enter_context(nc.psum_tensor("ps", [P, 8 * 512], F32))

        def sem(name):
            return ctx.enter_context(nc.semaphore(name))

        def place(name, at, n, dtype):
            return nc.alloc_sbuf_tensor_at(name, [P, n], dtype, offset=base + 4 * at, align_bytes=4)

        areas = [(at, at + n, place(name, at, n, F32)) for name, at, n in (
            ("stream", XT_AT, KT * S), ("normed", HT_AT, KT * S), ("ring", RING_AT, RING * SLOT),
            ("constants", CA_AT, 1024), ("phase_scratch", CP_AT, 3072), ("phase_data", DA_AT, DA))]
        parts = {}

        def shaped(v, shape):
            if len(shape) == 2:
                v = v.rearrange("p (a b) -> p a b", a=shape[0])
            if len(shape) == 3:
                v = v.rearrange("p (a b c) -> p a b c", a=shape[0], b=shape[1])
            return v

        def view(at, *shape):
            n = int(np.prod(shape))
            start, tensor = [(start, tensor) for start, end, tensor in areas if start <= at and at + n <= end][0]
            return shaped(tensor[:, at - start:at - start + n], shape)

        def part(at, *shape):
            n = int(np.prod(shape))
            if (at, n) not in parts:
                parts[at, n] = place(f"parts_{at}_{n}", at, n, F32R)
            return shaped(parts[at, n][:, 0:n], shape)

        def data(at, *shape):
            return view(DA_AT + at, *shape)

        k = Shared(nc=nc, io=io, ps=ps, sem=sem, view=view, data=data)
        k.part, k.data_part = part, lambda at, *shape: part(DA_AT + at, *shape)
        k.bank = lambda b, n=512: ps[:, b * 512:b * 512 + n]
        k.xT = view(XT_AT, KT, S)
        k.slot = lambda u: view(RING_AT + (u % RING) * SLOT, SLOT)
        k.const = lambda name: view(CA_AT, CA_N)[:, CA[name][0]:sum(CA[name])]
        k.w_landed = [sem(f"w_landed{i}") for i in range(RING)]
        k.used = {}
        k.x_in = [sem(f"x_in{i}") for i in range(3)]
        k.ca_in = sem("ca_in")
        k.gn_eps, k.eps = gn_eps, eps
        k.cp_in = sem("cp_in")
        k.vec = Count(sem("vector_done"))
        k.act = Count(sem("scalar_done"))
        k.pool = Count(sem("pool_done"))
        k.loaded = 0
        k.hi_ready, k.lo_ready = sem("weights_hi_ready"), sem("weights_split")
        k.piece_used = []
        input_phase(k)
        stick_phase(k)
        stream_phase(k)
        nsa_phase(k)
        gates_phase(k)
        rwkv_phase(k)
        output_phase(k)


def load_weights(k, sp, last):
    for u in range(k.loaded, min(last, len(ORDER))):
        if u >= RING:
            used, value = k.used[u - RING]
            sp.wait_ge(used, value)
        sp.dma_start(k.slot(u), k.io["weights"][BLOCK_AT[ORDER[u]]]).then_inc(k.w_landed[u % RING], 16)
    k.loaded = max(k.loaded, min(last, len(ORDER)))


def block_landed(k, pe, u):
    pe.wait_ge(k.w_landed[u % RING], 16 * (u // RING + 1))


class Tiles:

    def __init__(self, k, name, readers):
        self.k, self.readers = k, readers
        self.filled = k.sem(f"{name}_filled")
        self.emptied = {r: k.sem(f"{name}_emptied_{r}") for r in ("a", "v") if r in readers}
        self.rank, seen = [], {"a": 0, "v": 0}
        for r in readers:
            seen[r] += 1
            self.rank.append(seen[r])

    def bank(self, n, width=512):
        return self.k.bank(n % 4, width)

    def may_fill(self, pe, n):
        if n >= 4:
            pe.wait_ge(self.emptied[self.readers[n - 4]], self.rank[n - 4])

    def may_read(self, eng, n):
        eng.wait_ge(self.filled, n + 1)

    def read(self, ins, n):
        ins.then_inc(self.emptied[self.readers[n]], 1)


def norm_scratch(k):
    return (view_cp(k, 0), view_cp(k, 512)), view_cp(k, 1024), view_cp(k, 1536), view_cp(k, 2048), view_cp(k, 2560)


def view_cp(k, at, n=512):
    return k.view(CP_AT + at, n)


class Pieces:

    def __init__(self, k, filled, of_tile):
        self.k, self.base, self.filled = k, len(k.piece_used), filled
        self.what, self.last = [], {}
        index = {}
        self.of_tile = []
        for n, pieces in enumerate(of_tile):
            for piece in pieces:
                if piece not in index:
                    index[piece] = self.base + len(self.what)
                    self.what.append(piece)
                self.last[index[piece]] = n
            self.of_tile.append([index[piece] for piece in pieces])
        for i in range(len(self.what)):
            k.piece_used.append((filled, self.last[self.base + i] + 1))
        self.next = self.base

    def hi(self, p):
        return self.k.data_part(HI_AT + (p % 4) * (SLOT // 2), SLOT // 2)

    def at(self, p):
        unit, half = self.what[p - self.base]
        return RING_AT + (unit % RING) * SLOT + half * (SLOT // 2)

    def whole(self, p):
        return self.k.view(self.at(p), SLOT // 2)

    def lo(self, p):
        return self.k.part(self.at(p), SLOT // 2)

    def split_ahead(self, v, n):
        while self.next < self.base + len(self.what):
            p = self.next
            if p - 4 >= self.base and self.last[p - 4] >= n:
                return
            unit = self.what[p - self.base][0]
            if unit >= RING and self.k.used[unit - RING][0] is self.filled and self.k.used[unit - RING][1] > n:
                return
            if p >= 4:
                v.wait_ge(*self.k.piece_used[p - 4])
            block_landed(self.k, v, unit)
            v.tensor_copy(self.hi(p), self.whole(p)).then_inc(self.k.hi_ready, 1)
            self.next += 1

    def lower(self, g):
        for p in range(self.base, self.base + len(self.what)):
            g.wait_ge(self.k.hi_ready, p + 1)
            g.tensor_tensor(self.lo(p), self.whole(p), self.hi(p).bitcast(F32), ALU.subtract).then_inc(self.k.lo_ready, 1)

    def ready(self, pe, n):
        pe.wait_ge(self.k.lo_ready, max(self.of_tile[n]) + 1)


def split_tile(k, v, hi, lo, whole):
    v.wait_ge(k.vec.sem, k.vec.inc(v.tensor_copy(hi, whole)))
    return v.tensor_tensor(lo, whole, hi.bitcast(F32), ALU.subtract)


def three_passes(pe, out, pairs):
    for i, ((ah, al), (bh, bl), wait) in enumerate(pairs):
        if wait is not None:
            pe.wait_ge(*wait)
        for a, b in ((ah, bh), (ah, bl), (al, bh)):
            last = pe.matmul(out, a, b, start=i == 0 and a is ah and b is bh,
                             stop=i == len(pairs) - 1 and a is al)
    return last


def square_sum(k, v, tiles, acc, sq, arrived):
    done = []
    for i, t in enumerate(tiles):
        if i in arrived:
            v.wait_ge(*arrived[i])
        if i >= 2:
            v.wait_ge(k.vec.sem, done[i - 2])
        n = k.vec.inc(v.tensor_tensor(sq[i % 2], t, t, ALU.mult))
        v.wait_ge(k.vec.sem, n)
        if i == 0:
            done.append(k.vec.inc(v.tensor_copy(acc, sq[0])))
        else:
            done.append(k.vec.inc(v.tensor_tensor(acc, acc, sq[i % 2], ALU.add)))
    return done[-1]



def input_phase(k):
    nc, io = k.nc, k.io
    q, kk = k.data(0, 4, S), k.data(4096, 4, S)
    vv = k.data(8192, 8, 512)
    H = (k.data_part(12288, 16, HALF), k.part(HT_AT, 16, HALF))
    whole = (k.data(12288, 16, HALF), k.view(HT_AT, 16, HALF))
    sg = k.data(20480, 3, HALF)
    yc, u = k.view(XT_AT, 4, S), k.view(XT_AT + 4 * S, 4, S)
    sq, acc, root, rstd, _ = norm_scratch(k)
    stages = ["q", "k", "v", "cu", "cc", "cb", "ga", "gc"]
    count = {"q": 4, "k": 4, "v": 8, "cu": 4, "cc": 4, "cb": 4, "ga": 8, "gc": 8}
    unit_at = {"q": 0, "k": 2, "v": 4, "cu": 6, "cc": 8, "cb": 10, "ga": 12, "gc": 16}
    plan = [(h, s, m) for h in range(2) for s in stages for m in range(count[s])]
    at = {p: n for n, p in enumerate(plan)}
    tiles = Tiles(k, "in", ["v" if s in ("cc", "cb") else "a" for _, s, _ in plan])

    def unit_of(h, s, m):
        return START["in", h] + unit_at[s] + (m // 4 if s == "v" else m // 2)

    pieces = Pieces(k, tiles.filled, [[(unit_of(h, s, m), i) for i in ((0, 1) if s == "v" else (m % 2,))]
                                      for h, s, m in plan])
    for n, p in enumerate(plan):
        k.used[unit_of(*p)] = (tiles.filled, n + 1)
    ss_ready, ss_done = k.sem("in_ss_ready"), k.sem("in_ss_done")
    root_done, h_ready = k.sem("in_root_done"), k.sem("in_h_ready")
    k.kept = [k.sem(f"gates_kept{i}") for i in range(3)]
    gates = [(h, s, m) for h, s, m in plan if s in ("ga", "gc")]

    with nc.Block() as block:

        @block.sync
        def _(sp):
            for h in range(2):
                for i, ts in enumerate((slice(0, 4), slice(4, 8)) if h == 0 else (slice(0, 8),)):
                    part = (slice(None), ts, slice(h * HALF, (h + 1) * HALF))
                    sp.dma_start(k.xT[part], io["xT"].rearrange("(t p) s -> p t s", p=P)[part]
                                 ).then_inc(k.x_in[2 * h + i], 16)
                if h == 0:
                    sp.dma_start(k.view(CA_AT, CA_N), io["consts"]).then_inc(k.ca_in, 16)
                load_weights(k, sp, RING)
            load_weights(k, sp, START["mix", 0] + RING)
            for i in range(3):
                sp.wait_ge(k.kept[i], 16 * len(range(i, len(gates), 3)))

        @block.gpsimd
        def _(g):
            pieces.lower(g)

        @block.tensor
        def _(pe):
            pe.wait_ge(k.ca_in, 16)

            def total(h):
                pe.wait_ge(ss_ready, h + 1)
                pe.matmul(k.bank(4 + h), k.const("ones"), acc, start=True, stop=True).then_inc(ss_done, 1)

            total(0)
            for n, (h, s, m) in enumerate(plan):
                tiles.may_fill(pe, n)
                pieces.ready(pe, n)
                pairs = []
                for t in range(KT):
                    wait = (h_ready, KT * h + t + 1) if (s, m) == ("q", 0) else None
                    if s == "v":
                        p = pieces.of_tile[n][t // 4]
                        w = slice((t % 4) * 256, (t % 4 + 1) * 256)
                        tok = slice((m % 4) * P, (m % 4 + 1) * P)
                        pairs.append(((H[h][:, t, tok], H[h][:, KT + t, tok]),
                                      (pieces.hi(p)[:, w], pieces.lo(p)[:, w]), wait))
                    else:
                        p = pieces.of_tile[n][0]
                        w = slice(t * P, (t + 1) * P)
                        pairs.append(((pieces.hi(p)[:, w], pieces.lo(p)[:, w]), (H[h][:, t], H[h][:, KT + t]), wait))
                three_passes(pe, tiles.bank(n, 256 if s == "v" else HALF), pairs).then_inc(tiles.filled, 1)
                if n == at[0, "q", 3]:
                    total(1)

        @block.scalar
        def _(a):
            a.wait_ge(k.vec.sem, 1)

            def take_root(h):
                a.wait_ge(ss_done, h + 1)
                if h:
                    a.wait_ge(h_ready, 1)
                a.activation(root, k.bank(4 + h), ACT.Sqrt, bias=k.eps, scale=1.0 / D).then_inc(root_done, 1)

            take_root(0)
            bg = k.const("b_gate")
            gated = 0
            for n, (h, s, m) in enumerate(plan):
                if tiles.readers[n] != "a":
                    continue
                tiles.may_read(a, n)
                tile, cols = tiles.bank(n), slice(h * HALF, (h + 1) * HALF)
                if s == "q":
                    tiles.read(a.mul(q[:, m, cols], tile, HD ** -0.5), n)
                    if (h, m) == (0, 3):
                        take_root(1)
                elif s == "k":
                    tiles.read(a.copy(kk[:, m, cols], tile), n)
                elif s == "v":
                    tiles.read(a.copy(vv[:, h * 4 + m % 4, (m // 4) * 256:(m // 4 + 1) * 256],
                                      tiles.bank(n, 256)), n)
                elif s == "cu":
                    a.wait_ge(h_ready, 2 * KT)
                    tiles.read(a.copy(u[:, m, cols], tile), n)
                else:
                    if gated >= 3:
                        a.wait_ge(k.kept[gated % 3], 16 * (gated // 3))
                    b = m + (8 if s == "gc" else 0)
                    tiles.read(a.activation(sg[:, gated % 3], tile, ACT.Sigmoid, bias=bg[:, b:b + 1]), n)
                    a.wait_ge(tiles.emptied["a"], tiles.rank[n])
                    a.dma_start(io["gates_keep"][:, (16 * h + b) * HALF:(16 * h + b + 1) * HALF],
                                sg[:, gated % 3]).then_inc(k.kept[gated % 3], 16)
                    gated += 1

        @block.vector
        def _(v):
            k.vec.inc(v.memset(k.eps, EPS))
            v.memset(k.gn_eps, GN_EPS)

            def sums(h):
                if h:
                    v.wait_ge(ss_done, h)
                arrived = {0: (k.x_in[2], 16)} if h else {0: (k.x_in[0], 16), 4: (k.x_in[1], 16)}
                n = square_sum(k, v, [k.xT[:, t, h * HALF:(h + 1) * HALF] for t in range(KT)], acc, sq, arrived)
                v.wait_ge(k.vec.sem, n)
                v.nop().then_inc(ss_ready, 1)

            def normed(h, t):
                cols = slice(h * HALF, (h + 1) * HALF)
                v.wait_ge(k.vec.sem, k.vec.inc(v.scalar_tensor_tensor(
                    whole[h][:, KT + t], k.xT[:, t, cols], k.const("g_pre_mix")[:, t:t + 1], rstd, ALU.mult, ALU.mult)))
                split_tile(k, v, H[h][:, t], H[h][:, KT + t], whole[h][:, KT + t]).then_inc(h_ready, 1)

            def take_rstd(h):
                v.wait_ge(root_done, h + 1)
                if h:
                    v.wait_ge(h_ready, KT)
                v.wait_ge(k.vec.sem, k.vec.inc(v.reciprocal(rstd, root)))

            sums(0)
            pieces.split_ahead(v, 0)
            v.wait_ge(k.ca_in, 16)
            take_rstd(0)
            for t in range(KT):
                normed(0, t)
            sums(1)
            wc = k.const("w_conv").rearrange("p (j m) -> p j m", j=3)
            for n, (h, s, m) in enumerate(plan):
                pieces.split_ahead(v, n)
                tile, cols = tiles.bank(n), slice(h * HALF, (h + 1) * HALF)
                if h == 0 and at[0, "q", 3] + 2 <= n < at[0, "q", 3] + 2 + KT:
                    t = n - at[0, "q", 3] - 2
                    if t == 0:
                        take_rstd(1)
                    normed(1, t)
                if s == "cc":
                    tiles.may_read(v, n)
                    v.wait_ge(tiles.emptied["a"], tiles.rank[at[h, "cu", m]])
                    tiles.read(v.tensor_tensor(u[:, m, cols], tile, u[:, m, cols], ALU.mult), n)
                    v.wait_ge(tiles.emptied["v"], tiles.rank[n])
                    v.wait_ge(k.vec.sem, k.vec.inc(v.tensor_scalar(yc[:, m, cols], u[:, m, cols], wc[:, 2, m:m + 1],
                                                                   None, ALU.mult)))
                    for back in (1, 2):
                        first = max(back, h * HALF)
                        end = (h + 1) * HALF
                        v.wait_ge(k.vec.sem, k.vec.inc(v.scalar_tensor_tensor(
                            yc[:, m, first:end], u[:, m, first - back:end - back], wc[:, 2 - back, m:m + 1],
                            yc[:, m, first:end], ALU.mult, ALU.add)))
                if s == "cb":
                    tiles.may_read(v, n)
                    tiles.read(v.tensor_tensor(yc[:, m, cols], tile, yc[:, m, cols], ALU.mult), n)

def stick_phase(k):
    nc, io = k.nc, k.io
    q, kk = k.data(0, 4, S), k.data(4096, 4, S)
    vv, o = k.data(8192, 8, 512), k.data(16384, 4, S)
    x, sp = k.data(20480, 3, HALF), k.data(22016, 3, HALF)
    w, r = k.data(23552, 3, HALF), k.data(25088, 2, HALF)
    negtri = k.view(CP_AT + CB["negtri"][0], P)
    negones = k.view(CP_AT + CB["negones"][0], P)
    tl = [(h, c, i) for h in range(HEADS) for c in range(2) for i in range(4 * c + 3, -1, -1)]
    T = len(tl)
    off = [max(0, i * P - c * HALF) for _, c, i in tl]
    diag = [i // 4 == c for _, c, i in tl]
    first = [i == 4 * c + 3 for _, c, i in tl]
    group = [2 * h + c for h, c, _ in tl]
    last_of = {g: max(t for t in range(T) if group[t] == g) for g in range(16)}
    diags = [sum(diag[:t + 1]) for t in range(T)]
    summed, n = [], 0
    for t in range(T):
        if not first[t] and t != last_of[group[t]]:
            n += 1
        summed.append(n)
    z_ready, x_ready, ln_done = k.sem("z_ready"), k.sem("negabs_ready"), k.sem("log_ready")
    e_done, sp_ready, sp_masked = k.sem("exp_negabs_done"), k.sem("softplus_ready"), k.sem("softplus_masked")
    sum_ready, expo_ready = k.sem("later_sum_ready"), k.sem("exponent_ready")
    w_ready, w_masked, av_done = k.sem("weight_ready"), k.sem("weight_masked"), k.sem("weight_used")
    o_emptied = k.sem("o_emptied")
    cp_in = k.cp_in
    yc_moved, k.x_again, k.gates_in = k.sem("yc_moved"), k.sem("x_again"), k.sem("gates_in")

    with nc.Block() as block:

        @block.sync
        def _(sy):
            sy.dma_start(k.view(CP_AT, CB_N), io["consts_b"]).then_inc(cp_in, 16)
            sy.dma_start(k.data(12288, 4096), k.view(XT_AT, 4096)).then_inc(yc_moved, 16)
            sy.dma_start(k.view(HT_AT, 8192), io["gates_keep"][:, 0:8192]).then_inc(k.gates_in, 16)
            sy.wait_ge(yc_moved, 16)
            sy.dma_start(k.xT, io["xT"].rearrange("(t p) s -> p t s", p=P)).then_inc(k.x_again, 16)

        @block.tensor
        def _(pe):
            def score(t):
                h, c, i = tl[t]
                rows = slice(64 * (h % 2), 64 * (h % 2) + 64)
                if t >= 4:
                    pe.wait_ge(w_ready, t - 3)
                pe.matmul(k.bank(t % 4)[:, off[t]:HALF], kk[rows, h // 2, i * P:(i + 1) * P],
                          q[rows, h // 2, c * HALF + off[t]:(c + 1) * HALF], start=True, stop=True,
                          skip_group_check=True).then_inc(z_ready, 1)

            def exponent(t):
                pe.wait_ge(sp_ready, t + 1)
                if diag[t]:
                    pe.wait_ge(sp_masked, diags[t])
                if not first[t]:
                    if first[t - 1]:
                        later = sp[:, (t - 1) % 3]
                    else:
                        pe.wait_ge(sum_ready, summed[t - 1])
                        later = r[:, summed[t - 1] % 2]
                    pe.matmul(k.bank(t % 4)[:, off[t - 1]:HALF], negones, later[:, off[t - 1]:HALF],
                              start=False, stop=False, skip_group_check=True)
                pe.matmul(k.bank(t % 4)[:, off[t]:HALF], negtri, sp[:, t % 3, off[t]:HALF], start=False, stop=True,
                          skip_group_check=True).then_inc(expo_ready, 1)

            def values(t):
                h, c, i = tl[t]
                rows = slice(64 * (h % 2), 64 * (h % 2) + 64)
                pe.wait_ge(w_ready, t + 1)
                if diag[t]:
                    pe.wait_ge(w_masked, diags[t])
                if first[t] and group[t] >= 2:
                    pe.wait_ge(o_emptied, group[t] - 1)
                pe.matmul(k.bank(4 + group[t] % 2)[rows, off[t]:HALF], vv[:, i, h * HD:(h + 1) * HD],
                          w[:, t % 3, off[t]:HALF], start=first[t], stop=t == last_of[group[t]],
                          skip_group_check=True).then_inc(av_done, 1)

            pe.wait_ge(cp_in, 16)
            score(0)
            score(1)
            for t in range(T + 1):
                if t + 2 < T:
                    score(t + 2)
                if t < T:
                    exponent(t)
                if t >= 1:
                    values(t - 1)

        @block.vector
        def _(v):
            def negabs(t):
                v.wait_ge(z_ready, t + 1)
                tile = x[:, t % 3, off[t]:HALF]
                n = k.vec.inc(v.tensor_scalar(tile, k.bank(t % 4)[:, off[t]:HALF], 0.0, 2.0, ALU.min, ALU.mult))
                v.wait_ge(k.vec.sem, n)
                v.tensor_tensor(tile, tile, k.bank(t % 4)[:, off[t]:HALF], ALU.subtract).then_inc(x_ready, 1)

            def softplus(t):
                v.wait_ge(ln_done, t + 1)
                if t >= 3:
                    v.wait_ge(expo_ready, t - 1)
                    v.wait_ge(sum_ready, summed[t - 2])
                v.scalar_tensor_tensor(sp[:, t % 3, off[t]:HALF], k.bank(t % 4)[:, off[t]:HALF], 0.0,
                                       x[:, t % 3, off[t]:HALF], ALU.max, ALU.add).then_inc(sp_ready, 1)

            def keep_o(g):
                h, c = g // 2, g % 2
                rows = slice(64 * (h % 2), 64 * (h % 2) + 64)
                v.wait_ge(av_done, last_of[g] + 1)
                v.tensor_copy(o[rows, h // 2, c * HALF:(c + 1) * HALF], k.bank(4 + g % 2)[rows]).then_inc(o_emptied, 1)

            negabs(0)
            for t in range(T):
                if t + 1 < T:
                    negabs(t + 1)
                softplus(t)
                if t >= 3 and t - 3 == last_of[group[t - 3]]:
                    keep_o(group[t - 3])
            keep_o(15)

        @block.scalar
        def _(a):
            def log(t):
                tile = x[:, t % 3, off[t]:HALF]
                a.wait_ge(x_ready, t + 1)
                a.activation(tile, tile, ACT.Exp).then_inc(e_done, 1)
                a.wait_ge(e_done, t + 1)
                a.activation(tile, tile, ACT.Ln, bias=1.0).then_inc(ln_done, 1)

            a.preload_act_table_set("natural_log_exp_and_others")
            log(0)
            for t in range(T):
                if t + 1 < T:
                    log(t + 1)
                a.wait_ge(expo_ready, t + 1)
                if t >= 3:
                    a.wait_ge(av_done, t - 2)
                    if diags[t - 3]:
                        a.wait_ge(w_masked, diags[t - 3])
                a.activation(w[:, t % 3, off[t]:HALF], k.bank(t % 4)[:, off[t]:HALF], ACT.Exp).then_inc(w_ready, 1)

        @block.gpsimd
        def _(g):
            def mask(t, tile, done):
                g.affine_select(out=tile, in_=tile, compare_op=ALU.is_gt, fill=0.0, base=0, pattern=[[1, P]],
                                channel_multiplier=-1).then_inc(done, 1)

            for t in range(T + 1):
                if t < T:
                    g.wait_ge(sp_ready, t + 1)
                    if diag[t]:
                        mask(t, sp[:, t % 3, off[t]:off[t] + P], sp_masked)
                    if not first[t] and t != last_of[group[t]]:
                        n = summed[t]
                        if diag[t]:
                            g.wait_ge(sp_masked, diags[t])
                        if first[t - 1]:
                            before = sp[:, (t - 1) % 3]
                        else:
                            g.wait_ge(sum_ready, n - 1)
                            before = r[:, (n - 1) % 2]
                        if n >= 2:
                            g.wait_ge(expo_ready, t)
                        if off[t] < off[t - 1]:
                            g.tensor_copy(r[:, n % 2, off[t]:off[t - 1]], sp[:, t % 3, off[t]:off[t - 1]])
                        g.tensor_tensor(r[:, n % 2, off[t - 1]:HALF], before[:, off[t - 1]:HALF],
                                        sp[:, t % 3, off[t - 1]:HALF], ALU.add).then_inc(sum_ready, 1)
                if t >= 1 and diag[t - 1]:
                    g.wait_ge(w_ready, t)
                    mask(t - 1, w[:, (t - 1) % 3, off[t - 1]:off[t - 1] + P], w_masked)



def stream_phase(k):
    nc, io = k.nc, k.io
    mix, branches = k.data(0, 8, HALF), k.data_part(4096, 8, HALF)
    f = k.data(8192, 8, HALF)
    yc, o = k.data(12288, 4, S), k.data(16384, 4, S)
    yc_lo, o_lo = k.data_part(12288, 4, S), k.data_part(16384, 4, S)
    whole = (k.view(HT_AT, 16, HALF), k.data(12288, 16, HALF))
    H = (k.part(HT_AT, 16, HALF), k.data_part(12288, 16, HALF))
    sg = k.view(HT_AT, 2, 8, HALF)
    ff_whole = k.data(0, 16, HALF)
    ff = k.data_part(0, 16, HALF)
    p = (k.data(20480, 2, HALF), k.data(0, 2, HALF))
    pp_w = k.data(1024, 2, D)
    sgt, acc2 = k.data(3072, 3, HALF), k.data(7424, HALF)
    q2, kv2 = k.data(8192, 4, S), k.data(0, 4, S)
    gl = k.data(6144, 8, 24)
    sq, acc, root, rstd, tmp = norm_scratch(k)

    def cols(h):
        return slice(h * HALF, (h + 1) * HALF)

    parts = {
        "mix": [(s, m) for m in range(8) for s in ("ya", "yc")],
        "wo": [("wo", m) for m in range(8)],
        "mlp": [(s, 8 * c + m) for c in range(FF_PARTS) for s in ("up", "down") for m in range(8)],
        "gate": [("gate", 0), ("gate", 1)] + [x for m in range(6) for x in (("gate", m + 2), ("pp", m))]
                + [("pp", 6), ("pp", 7)],
        "in2": [(s, m) for s in ("q2", "kv2", "vsvw", "gl") for m in range(4)],
    }
    stages = [("mix", 0), ("wo", 0), ("mix", 1), ("wo", 1), ("mlp", 0), ("mlp", 1), ("gate", 0), ("gate", 1),
              ("in2", 0), ("in2", 1)]
    plan = [(st, h, i, s, m) for st, h in stages for i, (s, m) in enumerate(parts[st])]
    at = {(st, h, s, m): n for n, (st, h, _, s, m) in enumerate(plan)}

    sum_after = {("mix", 1, 1): acc, ("wo", 1, 0): acc, ("mlp", 0, 1): acc, ("mlp", 0, 9): acc, ("mlp", 1, 1): acc,
                 ("mlp", 1, 9): acc, ("gate", 0, 1): acc, ("gate", 0, 9): acc, ("gate", 1, 1): acc2,
                 ("in2", 0, 0): acc}
    residual_after, normed_after = {}, {}
    for t in range(KT):
        residual_after["mix", 1, 2 * t + 1] = (0, "g_post_mix", (t,))
        normed_after["wo", 1, t] = (0, "g_pre_mlp", (t,))
        residual_after["mlp", 0, t + 1] = (1, "g_post_mix", (t,))
        normed_after["mlp", 0, t + 9] = (1, "g_pre_mlp", (t,))
        residual_after["mlp", 1, t + 1] = (0, "g_post_mlp", (t,))
        normed_after["mlp", 1, t + 9] = (0, "g_ple", (t,))
        normed_after["in2", 0, t] = (1, "norm_g_2", (t,))
    for i in range(4):
        residual_after["gate", 0, 2 * i + 1] = (1, "g_post_mlp", (2 * i, 2 * i + 1))
        normed_after["gate", 1, 2 * i + 1] = (0, "norm_g_2", (2 * i, 2 * i + 1))
    for i, ts in ((9, (0, 1)), (11, (2, 3, 4)), (13, (5, 6, 7))):
        normed_after["gate", 0, i] = (1, "g_ple", ts)

    def reader(s, m):
        return "v" if s in ("ya", "yc", "pp") or s == "down" and m >= 8 else "a"

    tiles = Tiles(k, "st", [reader(s, m) for _, _, _, s, m in plan])

    def unit(st, h, s, m):
        base = START[st, h]
        if st == "mlp":
            return base + 8 * (m // 8) + (4 if s == "down" else 0) + m % 8 // 2
        if st == "in2":
            return base + {"q2": m // 2, "kv2": 2 + m // 2, "vsvw": 4, "gl": 5}[s]
        return None if s == "pp" else base + m // 2

    def split_of(st, h, s, m):
        if s in ("wo", "pp", "gl"):
            return []
        return [(unit(st, h, s, m), i) for i in ((0, 1) if s == "vsvw" else (m % 2,))]

    pieces = Pieces(k, tiles.filled, [split_of(st, h, s, m) for st, h, _, s, m in plan])
    for n, (st, h, _, s, m) in enumerate(plan):
        if s != "pp":
            k.used[unit(st, h, s, m)] = (tiles.filled, n + 1)
    ss_ready, ss_done = k.sem("st_ss_ready"), k.sem("st_ss_done")
    root_done, root_used = k.sem("st_root_done"), k.sem("st_root_used")
    h_ready, mix_ready, ff_ready = k.sem("st_h_ready"), k.sem("mix_ready"), k.sem("ff_ready")
    branch_ready, f_used = k.sem("branches_split"), k.sem("f_used")
    sgt_used, gates_in, p_in = k.sem("ple_gate_used"), k.gates_in, [k.sem("p_in0"), k.sem("p_in1")]
    pp_w_in, k.rstd_kept = k.sem("pp_w_in"), k.sem("rstd_kept")
    h_index = {("mlp", 0): 0, ("mlp", 1): 1, ("gate", 0): 2, ("gate", 1): 3, ("in2", 0): 4, ("in2", 1): 5}
    pT = io["pT"].rearrange("(t p) s -> p t s", p=P)

    with nc.Block() as block:

        @block.sync
        def _(sp):
            sp.dma_start(p[0], pT[:, :, cols(0)]).then_inc(p_in[0], 16)
            load_weights(k, sp, START["gate", 0] + 2)
            sp.wait_ge(tiles.filled, at["mlp", 1, "down", 31] + 1)
            sp.dma_start(pp_w, io["weights"][BLOCK_AT["pp", 0]].rearrange("p (t c) -> p t c", t=2)
                         ).then_inc(pp_w_in, 16)
            sp.dma_start(p[1], pT[:, :, cols(1)]).then_inc(p_in[1], 16)
            load_weights(k, sp, START["cmp"] + RING)
            sp.wait_ge(k.rstd_kept, 32)

        @block.gpsimd
        def _(g):
            pieces.lower(g)

        @block.tensor
        def _(pe):
            sums = 0
            for n, (st, h, i, s, m) in enumerate(plan):
                if i == 0 and st == "wo":
                    pe.wait_ge(mix_ready, 8 * (h + 1))
                if (s, m) == ("pp", 0):
                    pe.wait_ge(pp_w_in, 16)
                    pe.wait_ge(p_in[h], 16)
                tiles.may_fill(pe, n)
                width = {"vsvw": 256, "gl": 24}.get(s, HALF)
                if split_of(st, h, s, m):
                    pieces.ready(pe, n)
                    hi, lo = pieces.hi(pieces.of_tile[n][0]), pieces.lo(pieces.of_tile[n][0])
                    pairs = []
                    for t in range(4 if st == "mix" else KT):
                        wait = (h_ready, KT * h_index[st, h] + t + 1) if i == 0 and st != "mix" else None
                        x = (H[h][:, t], H[h][:, KT + t])
                        if st == "mix":
                            b = int(s == "yc")
                            x = branches[:, 4 * b + t], (o_lo, yc_lo)[b][:, t, cols(h)]
                            if m == 0:
                                wait = (branch_ready, 8 * h + 4 * b + t + 1)
                            w = slice((4 * b + t) * P, (4 * b + t + 1) * P)
                        elif s == "down":
                            x = (ff[:, t], ff[:, KT + t])
                            w = slice(t * P, (t + 1) * P)
                            if m % 8 == 0:
                                wait = (ff_ready, 32 * h + m + t + 1)
                        elif s == "vsvw":
                            q_ = pieces.of_tile[n][t // 4]
                            tok, w = slice(m * P, (m + 1) * P), slice((t % 4) * 256, (t % 4 + 1) * 256)
                            pairs.append(((x[0][:, tok], x[1][:, tok]), (pieces.hi(q_)[:, w], pieces.lo(q_)[:, w]),
                                          None))
                            continue
                        else:
                            w = slice(t * P, (t + 1) * P)
                        pairs.append(((hi[:, w], lo[:, w]), x, wait))
                    last = three_passes(pe, tiles.bank(n, width), pairs)
                else:
                    if s == "pp":
                        ops = [(pp_w[:, t, m * P:(m + 1) * P], p[h][:, t]) for t in range(2)]
                    else:
                        block_landed(k, pe, unit(st, h, s, m))
                        w = k.slot(unit(st, h, s, m))
                        if s == "wo":
                            w = w.rearrange("p (b t c) -> p b t c", b=2, t=KT)[:, m % 2]
                            ops = [(w[:, t], mix[:, t]) for t in range(KT)]
                        else:
                            w = w.rearrange("p (t c) -> p t c", t=KT)
                            ops = [(H[h][:, t, m * P:(m + 1) * P].bitcast(F32), w[:, t % KT, 0:width]) for t in range(2 * KT)]
                    for t, (lhs, rhs) in enumerate(ops):
                        last = pe.matmul(tiles.bank(n, width), lhs, rhs, start=t == 0, stop=t == len(ops) - 1)
                last.then_inc(tiles.filled, 1)
                if (st, h, i) in sum_after:
                    sums += 1
                    pe.wait_ge(ss_ready, sums)
                    pe.matmul(k.bank(4 + sums % 2), k.const("ones"), sum_after[st, h, i], start=True,
                              stop=True).then_inc(ss_done, 1)

        @block.scalar
        def _(a):
            sums, gates = 0, 0
            for n, (st, h, i, s, m) in enumerate(plan):
                tile = tiles.bank(n)
                if (st, h, i) == ("wo", 0, 0):
                    a.wait_ge(mix_ready, 8)
                    a.dma_start(sg, io["gates_keep"][:, 16 * HALF:32 * HALF].rearrange(
                        "p (b m c) -> p b m c", b=2, m=8)).then_inc(gates_in, 16)
                if tiles.readers[n] == "a":
                    tiles.may_read(a, n)
                if s == "wo" or s == "down" and m < 8:
                    if (st, h) != ("wo", 0):
                        a.wait_ge(f_used, {"wo": 0, "mlp": 8 * (h + 1)}[st] + m + 1)
                    tiles.read(a.copy(f[:, m], tile), n)
                elif s == "up":
                    tiles.read(a.activation(ff_whole[:, KT + m % 8], tile, ACT.Relu), n)
                elif s == "gate":
                    if gates >= 3:
                        a.wait_ge(sgt_used, gates - 2)
                    tiles.read(a.activation(sgt[:, gates % 3], tile, ACT.Sigmoid), n)
                    gates += 1
                elif s == "q2":
                    tiles.read(a.mul(q2[:, m, cols(h)], tile, HD ** -0.5), n)
                elif s == "kv2":
                    tiles.read(a.copy(kv2[:, m, cols(h)], tile), n)
                elif s == "vsvw":
                    both = k.data(4096, 2, 8, P)[:, :, 4 * h + m]
                    tiles.read(a.copy(both, tiles.bank(n, 256).rearrange("p (b c) -> p b c", b=2)), n)
                elif s == "gl":
                    tiles.read(a.activation(gl[:, 4 * h + m], tiles.bank(n, 24), ACT.Sigmoid), n)
                if (st, h, i) in sum_after:
                    sums += 1
                    a.wait_ge(ss_done, sums)
                    if sums > 1:
                        a.wait_ge(root_used, sums - 1)
                    a.activation(root, k.bank(4 + sums % 2), ACT.Sqrt, bias=k.eps, scale=1.0 / D).then_inc(root_done, 1)
                if (st, h, i) == ("in2", 1, 0):
                    a.wait_ge(h_ready, 6 * KT)
                    a.dma_start(io["rstd_keep"][:, 0:HALF], rstd).then_inc(k.rstd_kept, 16)
                    a.dma_start(io["rstd_keep"][:, HALF:S], tmp).then_inc(k.rstd_kept, 16)

        @block.vector
        def _(v):
            state = Shared(sums=0, gates=0)
            state.signals = state.f_used = 0

            def step(ins):
                v.wait_ge(k.vec.sem, k.vec.inc(ins))

            def signal():
                v.nop().then_inc(ss_ready, 1)
                state.signals += 1

            def finish_sum(out):
                state.sums += 1
                v.wait_ge(root_done, state.sums)
                v.reciprocal(out, root).then_inc(root_used, 1)
                v.wait_ge(root_used, state.sums)

            def add_square(i, tile, into):
                step(v.tensor_tensor(sq[i % 2], tile, tile, ALU.mult))
                if i == 0:
                    if state.signals:
                        v.wait_ge(ss_done, state.signals)
                    step(v.tensor_copy(into, sq[0]))
                else:
                    step(v.tensor_tensor(into, into, sq[i % 2], ALU.add))

            def add_to_x(t, h, term):
                step(v.tensor_tensor(k.xT[:, t, cols(h)], k.xT[:, t, cols(h)], term, ALU.add))

            def split_branches(h, t):
                at_ = (slice(None), t % 4, cols(h))
                split_tile(k, v, branches[:, t], (o_lo, yc_lo)[t // 4][at_], (o, yc)[t // 4][at_]).then_inc(branch_ready, 1)

            v.wait_ge(k.x_again, 16)
            pieces.split_ahead(v, 0)
            for t in range(8):
                split_branches(0, t)
            for n, (st, h, i, s, m) in enumerate(plan):
                pieces.split_ahead(v, n)
                tile = tiles.bank(n)
                if s in ("ya", "yc"):
                    tiles.may_read(v, n)
                    if m == 0:
                        v.wait_ge(gates_in, 16 * (h + 1))
                    g = sg[:, int(s == "yc"), m]
                    tiles.read(v.tensor_tensor(g, tile, g, ALU.mult), n)
                    if s == "yc":
                        v.wait_ge(tiles.emptied["v"], tiles.rank[n])
                        v.tensor_tensor(mix[:, m], sg[:, 0, m], g, ALU.add).then_inc(mix_ready, 1)
                elif s == "wo" or s == "down" and m < 8:
                    v.wait_ge(tiles.emptied["a"], tiles.rank[n])
                    if s == "wo":
                        add_square(m, f[:, m], acc)
                        if h == 0:
                            split_branches(1, m)
                elif s == "down":
                    tiles.may_read(v, n)
                    tiles.read(v.tensor_tensor(f[:, m % 8], f[:, m % 8], tile, ALU.add), n)
                    v.wait_ge(tiles.emptied["v"], tiles.rank[n])
                    if m >= 24:
                        add_square(m % 8, f[:, m % 8], acc)
                elif s == "up":
                    x = ff_whole[:, KT + m % 8]
                    v.wait_ge(tiles.emptied["a"], tiles.rank[n])
                    step(v.tensor_tensor(x, x, x, ALU.mult))
                    split_tile(k, v, ff[:, m % 8], ff[:, KT + m % 8], x).then_inc(ff_ready, 1)
                elif s == "pp":
                    g = sgt[:, state.gates % 3]
                    v.wait_ge(tiles.emptied["a"], tiles.rank[at[st, h, "gate", m]])
                    tiles.may_read(v, n)
                    tiles.read(v.tensor_tensor(g, tile, g, ALU.mult), n)
                    v.wait_ge(tiles.emptied["v"], tiles.rank[n])
                    v.tensor_tensor(k.xT[:, m, cols(h)], k.xT[:, m, cols(h)], g, ALU.add).then_inc(sgt_used, 1)
                    state.gates += 1
                    v.wait_ge(sgt_used, state.gates)
                    add_square(m, k.xT[:, m, cols(h)], acc if h else acc2)
                if i == len(parts[st]) - 1 and st in ("wo", "mlp", "gate"):
                    signal()
                second = (st, h, i) == ("in2", 0, 0)
                if (st, h, i) in sum_after:
                    finish_sum(tmp if second else rstd)
                if (st, h, i) in residual_after:
                    half, gain, ts = residual_after[st, h, i]
                    for t in ts:
                        v.scalar_tensor_tensor(tmp, f[:, t], k.const(gain)[:, t:t + 1], rstd, ALU.mult,
                                               ALU.mult).then_inc(f_used, 1)
                        state.f_used += 1
                        v.wait_ge(f_used, state.f_used)
                        add_to_x(t, half, tmp)
                        add_square(t, k.xT[:, t, cols(half)], acc)
                    if ts[-1] == KT - 1:
                        signal()
                if (st, h, i) in normed_after:
                    half, gain, ts = normed_after[st, h, i]
                    for t in ts:
                        x = whole[half][:, KT + t]
                        step(v.scalar_tensor_tensor(x, k.xT[:, t, cols(half)], k.const(gain)[:, t:t + 1],
                                                    tmp if st == "in2" else rstd, ALU.mult, ALU.mult))
                        split_tile(k, v, H[half][:, t], H[half][:, KT + t], x).then_inc(h_ready, 1)

CC = {}
_at = 0
for _name, _n in (("causal", 128), ("window", 640), ("cmp_add", 512), ("cmp_keep", 512), ("imp_add", 64),
                  ("imp_keep", 64), ("overlap", 64), ("earlier", 256), ("swap", 128)):
    CC[_name] = (_at, _n)
    _at += _n
CC_N = _at
assert CC_N <= 3072


def nsa_phase(k):
    nc, io = k.nc, k.io
    nt = S // P
    q2 = k.data(8192, 4, S)
    kc_vc, kskw = k.data(0, 2, S), k.data(2048, 2, S)
    vsvw, gl = k.data(4096, 2, nt, P), k.data(6144, nt, 3, 8)
    rope = k.data(16640, 2, S)
    acc, mixn = k.data(18688, nt, 512), k.data(12544, 4, S)
    kcmp, vcmp = k.data(6400, 64), k.data(6464, 64)
    st_max, st_sum, st_inv = k.data(6528, nt, 8), k.data(6592, nt, 8), k.data(6656, nt, 8)
    pg, pw, imp = k.data(6720, 2, 64), k.data(6848, 2, 64), k.data(6976, 8, 16)
    neg_max, sums = k.data(7104, 2 * 64), k.data(7232, 2 * 64)
    coef, rank, sel = k.data(7360, 16, 8), k.data(7488, 8, 16), k.data(7616, 8, 16)
    cs, pc, ptc = k.data(22784, 2, 512), k.data(23808, 2, 512), k.data(24832, 2, 512)
    rt = k.data(25856, 512)
    greater = k.data(22784, 8, 256)
    hv = lambda at, *shape: k.view(HT_AT + at, *shape)
    shifted, win_in = hv(0, 2, S), hv(2048, 16, P)
    hid, sig = hv(4096, 2, P), hv(4352, 2, P)
    ss, pp, pts = hv(0, 2, 1024), hv(2048, 2, 1024), hv(4096, 4, 512)
    equal = hv(6144, 8, 256)
    bias_at = (k.data(0, 2, 1024), k.data(16640, 2, 1024))
    o_tmp = rt

    def cst(name, *shape):
        return k.view(CP_AT + CC[name][0], *(shape or (CC[name][1],)))

    causal, window = cst("causal"), cst("window")

    def rows(g):
        return slice(64 * g, 64 * g + 64)

    passes = [(b, t, j, g) for b in (2, 1) for t in range(nt) for j in range(4) for g in range(2)]
    N = len(passes)

    def span(n):
        b, t, _, _ = passes[n]
        first = max(0, t - 4) if b == 2 else 0
        return first, t + 1 - first

    chunks = [(n, c) for n in range(N) for c in range((span(n)[1] + 3) // 4)]
    chunk_at = {nc_: i for i, nc_ in enumerate(chunks)}
    copier = ["a" if i % 2 else "v" for i in range(len(chunks))]
    copied_rank = [copier[:i + 1].count(copier[i]) for i in range(len(chunks))]

    def of(n):
        return [min(4, span(n)[1] - 4 * c) for c in range((span(n)[1] + 3) // 4)]

    sem = k.sem
    rope_in = sem("rope_in")
    k.spilled = sem("spilled")
    swapped, swap_read, roped, scaled = sem("swapped"), sem("swap_read"), sem("roped"), sem("cos_scaled")
    sh_ready, wi_ready, hid_mm, sig_ready, hid_ready = (sem("shifted_ready"), sem("windows_ready"), sem("hidden_done"),
                                                        sem("sigmoid_ready"), sem("hidden_ready"))
    cmp_mm, cmp_ready = sem("cmp_done"), sem("cmp_ready")
    cs_mm, cs_ready, ce_ready, pc_ready = sem("cmp_scores"), sem("cmp_shifted"), sem("cmp_exp"), sem("cmp_probs")
    ct_mm, ct_ready, co_mm, co_read = sem("cmp_turned"), sem("cmp_turned_copied"), sem("cmp_out"), sem("cmp_out_read")
    s_mm, s_read, e_ready = sem("scores"), sem("scores_read"), sem("probs_ready")
    t_mm, t_copied = sem("turned"), {"a": sem("turned_copied_a"), "v": sem("turned_copied_v")}
    av_mm, o_mm, o_read = sem("attended"), sem("attended_tile"), sem("attended_read")
    bias_ready, sel_ready = sem("bias_ready"), sem("selection_ready")
    m_mm, m_read = sem("mix_turned"), sem("mix_copied")
    swaps = [(kskw, i, h) for i in range(2) for h in range(2)] + [(q2, j, h) for j in range(4) for h in range(2)]

    with nc.Block() as block:

        def copy_turned(eng, n, who):
            for c, w in enumerate(of(n)):
                i = chunk_at[n, c]
                if copier[i] != who:
                    continue
                eng.wait_ge(t_mm, i + 1)
                if i >= 4:
                    eng.wait_ge(av_mm, chunks[i - 4][0] + 1)
                copy = eng.copy if who == "a" else eng.tensor_copy
                copy(pts[:, i % 4, 0:w * P], k.bank(4 + i % 2, w * P)).then_inc(t_copied[who], 1)

        @block.sync
        def _(sp):
            sp.dma_start(k.view(CP_AT, CC_N), io["consts_c"]).then_inc(k.cp_in, 16)
            sp.dma_start(rope, io["rope"].rearrange("p (b s) -> p b s", b=2)).then_inc(rope_in, 16)
            sp.dma_start(io["x_keep"], k.view(XT_AT, 8192)).then_inc(k.spilled, 16)
            for i, unit in enumerate(range(START["cmp"], START["in3", 0])):
                k.used[unit] = (hid_mm, i + 1)
            load_weights(k, sp, START["in3", 0] + RING)

        @block.tensor
        def _(pe):
            pe.wait_ge(k.cp_in, 32)
            ident = k.const("ident")

            def swap(i):
                x, j, h = swaps[i]
                if i >= 2:
                    pe.wait_ge(swap_read, i - 1)
                pe.matmul(k.bank(6 + i % 2), cst("swap"), x[:, j, h * HALF:(h + 1) * HALF], start=True,
                          stop=True).then_inc(swapped, 1)

            for i in range(4):
                swap(i)
            for x in range(2):
                pe.wait_ge(wi_ready, 4 * (x + 1))
                for b in range(2):
                    unit = START["cmp"] + 2 * x + b
                    block_landed(k, pe, unit)
                    w = k.slot(unit).rearrange("p (l c) -> p l c", l=8)
                    for ht in range(2):
                        for l in range(8):
                            last = pe.matmul(k.bank(2 * x + ht, P), w[:, l, ht * P:(ht + 1) * P], win_in[:, 8 * b + l],
                                             start=b == 0 and l == 0, stop=b == 1 and l == 7)
                    last.then_inc(hid_mm, 1)
                pe.wait_ge(hid_ready, 2 * (x + 1))
                w2 = k.const("w2k" if x == 0 else "w2v").rearrange("p (t c) -> p t c", t=2)
                for g in range(2):
                    for ht in range(2):
                        a_, b_ = (w2[:, ht], hid[:, ht, rows(g)]) if x == 0 else (hid[:, ht, rows(g)], w2[:, ht])
                        last = pe.matmul(k.bank(4 + x, 64)[rows(g)], a_, b_, start=ht == 0, stop=ht == 1)
                last.then_inc(cmp_mm, 1)
            pe.wait_ge(cmp_ready, 2)
            for t in range(nt + 2):
                if t < nt:
                    if t >= 2:
                        pe.wait_ge(cs_ready, 2 * (t - 2) + 1)
                    for j in range(4):
                        for g in range(2):
                            last = pe.matmul(k.bank(2 * (t % 2) + g)[:, j * 64:(j + 1) * 64],
                                             q2[rows(g), j, t * P:(t + 1) * P], kcmp[rows(g)], start=True, stop=True)
                    last.then_inc(cs_mm, 1)
                if t >= 2:
                    u = t - 2
                    pe.wait_ge(pc_ready, u + 1)
                    if u >= 2:
                        pe.wait_ge(ct_ready, u - 1)
                    for j in range(4):
                        last = pe.transpose(k.bank(4 + u % 2)[:, j * P:(j + 1) * P], pc[:, u % 2, j * P:(j + 1) * P], ident)
                    last.then_inc(ct_mm, 1)
                    pe.wait_ge(ct_ready, u + 1)
                    if u >= 1:
                        pe.wait_ge(co_read, u)
                    for j in range(4):
                        for g in range(2):
                            last = pe.matmul(k.bank(6 + g)[:, j * 64:(j + 1) * 64], ptc[rows(g), u % 2, j * P:(j + 1) * P],
                                             vcmp[rows(g)], start=True, stop=True)
                    last.then_inc(co_mm, 1)
            pe.wait_ge(co_read, nt)
            for i in range(4, len(swaps)):
                swap(i)

            def score(n):
                b, t, j, g = passes[n]
                first, width = span(n)
                if n >= 2:
                    pe.wait_ge(s_read, n - 1)
                keys = kskw[rows(g), 0 if b == 1 else 1]
                for c in range(0, width, 4):
                    w = min(4, width - c)
                    last = pe.matmul(k.bank(2 * (n % 2) + c // 4, w * P), q2[rows(g), j, t * P:(t + 1) * P],
                                     keys[:, (first + c) * P:(first + c + w) * P], start=True, stop=True)
                last.then_inc(s_mm, 1)

            def turn(n):
                pe.wait_ge(e_ready, n + 1)
                for c, w in enumerate(of(n)):
                    i = chunk_at[n, c]
                    if i >= 2:
                        pe.wait_ge(t_copied[copier[i - 2]], copied_rank[i - 2])
                    for x in range(w):
                        at = (4 * c + x) * P
                        last = pe.transpose(k.bank(4 + i % 2)[:, x * P:(x + 1) * P], pp[:, n % 2, at:at + P], ident)
                    last.then_inc(t_mm, 1)

            def attend(n):
                b, t, j, g = passes[n]
                first, width = span(n)
                tile = n // 8
                if n % 8 == 0 and tile >= 2:
                    pe.wait_ge(o_read, tile - 1)
                for c, w in enumerate(of(n)):
                    i = chunk_at[n, c]
                    pe.wait_ge(t_copied[copier[i]], copied_rank[i])
                    for x in range(w):
                        kt = first + 4 * c + x
                        last = pe.matmul(k.bank(6 + tile % 2)[:, (n % 8) * 64:(n % 8) * 64 + 64],
                                         pts[:, i % 4, x * P:(x + 1) * P], vsvw[:, 0 if b == 1 else 1, kt, rows(g)],
                                         start=4 * c + x == 0, stop=4 * c + x == width - 1)
                last.then_inc(av_mm, 1)

            pe.wait_ge(roped, len(swaps))
            score(0)
            for n in range(N + 1):
                if n + 1 < N:
                    score(n + 1)
                if n < N:
                    turn(n)
                if n >= 1:
                    attend(n - 1)
            pe.wait_ge(o_read, N // 8)
            for i in range(8):
                j, h = i // 2, i % 2
                if i >= 2:
                    pe.wait_ge(m_read, i - 1)
                for x in range(4):
                    last = pe.transpose(k.bank(i % 2)[:, x * P:(x + 1) * P], acc[:, 4 * h + x, j * P:(j + 1) * P], ident)
                last.then_inc(m_mm, 1)

        @block.scalar
        def _(a):
            for x in range(2):
                if x == 1:
                    a.wait_ge(wi_ready, 4)
                for g in range(2):
                    a.copy(shifted[0:64, g], kc_vc[rows(g), x]).then_inc(sh_ready, 1)
                    a.copy(shifted[64:128, g, 0:S - 1], kc_vc[rows(g), x, 1:S]).then_inc(sh_ready, 1)
                a.wait_ge(hid_mm, 2 * (x + 1))
                if x == 1:
                    a.wait_ge(hid_ready, 2)
                for ht in range(2):
                    a.activation(sig[:, ht], k.bank(2 * x + ht, P), ACT.Sigmoid).then_inc(sig_ready, 1)
            for t in range(nt + 2):
                if t < nt:
                    a.wait_ge(cs_ready, 2 * t + 2)
                    a.activation(cs[:, t % 2], cs[:, t % 2], ACT.Exp).then_inc(ce_ready, 1)
                if t >= 2:
                    u = t - 2
                    a.wait_ge(ct_mm, u + 1)
                    if u >= 2:
                        a.wait_ge(co_mm, u - 1)
                    a.copy(ptc[:, u % 2], k.bank(4 + u % 2)).then_inc(ct_ready, 1)

            def probs(n):
                width = span(n)[1] * P
                a.wait_ge(s_read, n + 1)
                if n >= 2:
                    a.wait_ge(t_mm, chunk_at[n - 1, 0])
                a.activation(pp[:, n % 2, 0:width], ss[:, n % 2, 0:width], ACT.Exp, bias=neg_max[:, n:n + 1],
                             scale=-1.0, accum_out=sums[:, n:n + 1]).then_inc(e_ready, 1)

            probs(0)
            for n in range(N):
                if n + 1 < N:
                    probs(n + 1)
                copy_turned(a, n, "a")
            for i in range(8):
                j, h = i // 2, i % 2
                a.wait_ge(m_mm, i + 1)
                a.copy(mixn[:, j, h * HALF:(h + 1) * HALF], k.bank(i % 2)).then_inc(m_read, 1)

        @block.vector
        def _(v):
            v.wait_ge(k.cp_in, 32)
            v.wait_ge(rope_in, 16)

            def rotate(i):
                x, j, h = swaps[i]
                tile = x[:, j, h * HALF:(h + 1) * HALF]
                v.wait_ge(swapped, i + 1)
                if i >= 1:
                    v.wait_ge(roped, i)
                v.tensor_tensor(rt, k.bank(6 + i % 2), rope[:, 1, h * HALF:(h + 1) * HALF], ALU.mult).then_inc(swap_read, 1)
                v.wait_ge(swap_read, i + 1)
                v.wait_ge(scaled, i + 1)
                v.tensor_tensor(tile, tile, rt, ALU.add).then_inc(roped, 1)

            n = k.vec.inc(v.memset(win_in.rearrange("p l (g c) -> p l g c", g=2)[:, :, :, CMP_N:CMP_PAD], 0.0))
            for i in range(4):
                rotate(i)
            for x in range(2):
                pos = k.const("pos_k" if x == 0 else "pos_v")
                if x == 1:
                    v.wait_ge(hid_mm, 2)
                for g in range(2):
                    v.wait_ge(sh_ready, 4 * x + 2 * g + 2)
                    src = shifted[:, g].rearrange("p (c l two) -> p l c two", l=8, two=2)[:, :, :, 0]
                    for b in range(2):
                        out = win_in.rearrange("p l (g c) -> p l g c", g=2)[:, 8 * b:8 * b + 8, g, 0:CMP_N]
                        v.tensor_tensor(out, src[:, :, b:b + CMP_N],
                                        pos[:, 8 * b:8 * b + 8].unsqueeze(2).to_broadcast((P, 8, CMP_N)),
                                        ALU.add).then_inc(wi_ready, 1)
                for ht in range(2):
                    v.wait_ge(sig_ready, 2 * x + ht + 1)
                    if x == 1:
                        v.wait_ge(cmp_mm, 1)
                    v.tensor_tensor(hid[:, ht], k.bank(2 * x + ht, P), sig[:, ht], ALU.mult).then_inc(hid_ready, 1)
                v.wait_ge(cmp_mm, x + 1)
                v.tensor_copy(kcmp if x == 0 else vcmp, k.bank(4 + x, 64)).then_inc(cmp_ready, 1)
            add = cst("cmp_add", nt, 64)
            keep = cst("cmp_keep", nt, 64)

            def per_head(tile):
                return tile.rearrange("p (h c) -> p h c", h=8)

            def by_group(tile):
                return tile.rearrange("p (j g c) -> p g j c", j=4, g=2)

            def two_banks(b):
                return k.ps[:, b * 512:(b + 2) * 512].rearrange("p (g j c) -> p g j c", g=2, c=64)[:, :, 0:4]

            def wide(cols, w=64):
                return cols.unsqueeze(2).to_broadcast((P, 8, w))

            def step(ins):
                v.wait_ge(k.vec.sem, k.vec.inc(ins))

            def cmp_scores(t):
                v.wait_ge(cs_mm, t + 1)
                tile = per_head(cs[:, t % 2])
                v.tensor_tensor(by_group(cs[:, t % 2]), two_banks(2 * (t % 2)),
                                add[:, t].unsqueeze(1).unsqueeze(1).to_broadcast((P, 2, 4, 64)),
                                ALU.add).then_inc(cs_ready, 1)
                v.wait_ge(cs_ready, 2 * t + 1)
                step(v.tensor_reduce(st_max[:, t], tile, AX, ALU.max))
                v.tensor_tensor(tile, tile, wide(st_max[:, t]), ALU.subtract).then_inc(cs_ready, 1)

            def cmp_probs(t):
                tile, out = per_head(cs[:, t % 2]), per_head(pc[:, t % 2])
                v.wait_ge(ce_ready, t + 1)
                step(v.tensor_reduce(st_sum[:, t], tile, AX, ALU.add))
                step(v.reciprocal(st_inv[:, t], st_sum[:, t]))
                if t >= 2:
                    v.wait_ge(ct_mm, t - 1)
                step(v.tensor_tensor(out, tile, keep[:, t].unsqueeze(1).to_broadcast((P, 8, 64)), ALU.mult))
                v.tensor_tensor(out, out, wide(st_inv[:, t]), ALU.mult).then_inc(pc_ready, 1)
                if t < 4:
                    return
                v.wait_ge(pc_ready, t + 1)
                step(v.tensor_reduce(pg, pc[:, t % 2].rearrange("p (j g c) -> p g c j", j=4, g=2), AX, ALU.add))
                step(v.tensor_tensor(pw, pg, cst("overlap").unsqueeze(1).to_broadcast((P, 2, 64)), ALU.mult))
                im = imp[:, 2 * (t - 4):2 * (t - 3)]
                four = pw.rearrange("p g (b f) -> p g b f", f=4)
                step(v.tensor_reduce(im, four, AX, ALU.add))
                step(v.tensor_tensor(im[:, :, 1:16], im[:, :, 1:16], four[:, :, 0:15, 3], ALU.add))
                step(v.tensor_tensor(im, im, cst("imp_keep", 4, 16)[:, t - 4].unsqueeze(1).to_broadcast((P, 2, 16)),
                                     ALU.mult))
                step(v.tensor_tensor(im, im, cst("imp_add", 4, 16)[:, t - 4].unsqueeze(1).to_broadcast((P, 2, 16)),
                                     ALU.add))

            def cmp_out(t):
                v.wait_ge(co_mm, t + 1)
                v.tensor_tensor(by_group(acc[:, t]), two_banks(6),
                                gl[:, t, 0].rearrange("p (j g) -> p g j", g=2).unsqueeze(3).to_broadcast((P, 2, 4, 64)),
                                ALU.mult).then_inc(co_read, 1)

            for t in range(nt + 3):
                if t >= 3:
                    cmp_out(t - 3)
                if t < nt:
                    cmp_scores(t)
                if 1 <= t <= nt:
                    cmp_probs(t - 1)
            for i in range(4, len(swaps)):
                rotate(i)
            bj, bi = imp.unsqueeze(3).to_broadcast((P, 8, 16, 16)), imp.unsqueeze(2).to_broadcast((P, 8, 16, 16))
            four_d = lambda x: x.rearrange("p a (j i) -> p a j i", j=16)
            v.wait_ge(ct_ready, nt)

            def select(i):
                if i == 0:
                    step(v.tensor_tensor(four_d(greater), bi, bj, ALU.is_gt))
                elif i == 1:
                    step(v.tensor_tensor(four_d(equal), bi, bj, ALU.is_equal))
                elif i == 2:
                    step(v.tensor_tensor(equal, equal, cst("earlier").unsqueeze(1).to_broadcast((P, 8, 256)), ALU.mult))
                elif i == 3:
                    step(v.tensor_tensor(greater, greater, equal, ALU.add))
                elif i == 4:
                    step(v.tensor_reduce(rank, four_d(greater), AX, ALU.add))
                    v.tensor_scalar(sel, rank, 7.5, NEG, ALU.is_gt, ALU.mult).then_inc(sel_ready, 1)

            def mask_scores(n):
                b, t, j, g = passes[n]
                width = span(n)[1] * P
                v.wait_ge(s_mm, n + 1)
                if n >= 2:
                    v.wait_ge(e_ready, n - 1)
                if b == 2:
                    bias = window[:, 640 - width:640]
                else:
                    v.wait_ge(bias_ready, t + 1)
                    bias = bias_at[t % 2][:, g, 0:width]
                v.tensor_tensor_reduce(ss[:, n % 2, 0:width], k.ps[:, 1024 * (n % 2):1024 * (n % 2) + width], bias,
                                       -1.0, 3e38, ALU.add, ALU.min, neg_max[:, n:n + 1]).then_inc(s_read, 1)

            def gather(tile):
                b, t = passes[8 * tile][:2]
                v.wait_ge(e_ready, 8 * tile + 8)
                step(v.reciprocal(coef[:, tile], sums[:, 8 * tile:8 * tile + 8]))
                step(v.tensor_tensor(coef[:, tile], coef[:, tile], gl[:, t, b], ALU.mult))
                v.wait_ge(av_mm, 8 * tile + 8)
                step(v.tensor_tensor(per_head(o_tmp), per_head(k.bank(6 + tile % 2)), wide(coef[:, tile]), ALU.mult))
                step(v.tensor_tensor(acc[:, t], acc[:, t], o_tmp, ALU.add))
                v.nop().then_inc(o_read, 1)

            mask_scores(0)
            for n in range(N):
                if n + 1 < N:
                    mask_scores(n + 1)
                if n % 8 == 1 and n > 8:
                    gather(n // 8 - 1)
                copy_turned(v, n, "v")
                if n in (10, 14, 18, 22, 26):
                    select((n - 10) // 4)
            gather(N // 8 - 1)

        @block.gpsimd
        def _(g_):
            g_.wait_ge(rope_in, 16)
            g_.wait_ge(k.cp_in, 32)
            for i, (x, j, h) in enumerate(swaps):
                tile = x[:, j, h * HALF:(h + 1) * HALF]
                g_.wait_ge(swapped, i + 1)
                if i >= 4:
                    g_.wait_ge(cs_mm, nt)
                g_.tensor_tensor(tile, tile, rope[:, 0, h * HALF:(h + 1) * HALF], ALU.mult).then_inc(scaled, 1)
            for t in range(nt):
                if t >= 2:
                    g_.wait_ge(s_read, 64 + 8 * (t - 1))
                else:
                    g_.wait_ge(roped, len(swaps))
                    g_.wait_ge(sh_ready, 8)
                for g in range(2):
                    tile = bias_at[t % 2][:, g, 0:(t + 1) * P]
                    if t < 4:
                        n = k.pool.inc(g_.memset(tile, 0.0))
                    else:
                        g_.wait_ge(sel_ready, 1)
                        n = k.pool.inc(g_.tensor_copy(
                            tile.rearrange("p (b c) -> p b c", c=64),
                            sel[:, 2 * (t - 4) + g, 0:2 * (t + 1)].unsqueeze(2).to_broadcast((P, 2 * (t + 1), 64))))
                    g_.wait_ge(k.pool.sem, n)
                    last = g_.tensor_tensor(tile[:, t * P:], tile[:, t * P:], causal, ALU.add)
                    if g == 0:
                        k.pool.inc(last)
                last.then_inc(bias_ready, 1)


CHUNK = 64
NCHUNK = S // CHUNK
LEVELS = 6
GN_EPS = 64e-5
DECAY = float(np.exp(-0.5))
CD = {}
_at = 0
for _name, _n in (("mask", 128), ("level", LEVELS * CHUNK), ("eye", CHUNK), ("up", 512), ("resets", 1024)):
    CD[_name] = (_at, _n)
    _at += _n
CD_N = _at - 1024
assert _at <= 3072


def gates_phase(k):
    nc, io = k.nc, k.io
    mixn, wdad, gr = k.data(12544, 4, S), k.data(16640, 1, S), k.data(17664, 4, S)
    sg = (view_cp(k, 2560), k.data(21760, HALF))
    rstd = view_cp(k, 0, S)
    x_part = k.part(XT_AT, KT, S)
    H = ([k.part(HT_AT, 16, HALF)[:, t] for t in range(16)],
         [x_part[:, t, 0:HALF] for t in range(KT)] + [x_part[:, t, HALF:S] for t in range(KT)])
    whole = ([k.view(HT_AT + 8 * HALF, 8, HALF)[:, t] for t in range(KT)], [k.xT[:, t, HALF:S] for t in range(KT)])
    count = {"gnsa": 4, "grwkv": 4, "r3": 4, "k3": 4, "v3": 4, "wdad": 1}
    first = {"gnsa": 0, "grwkv": 2, "r3": 4, "k3": 6, "v3": 8, "wdad": 10}
    dest = {"r3": k.data(0, 4, S), "k3": k.data(4096, 4, S), "v3": k.data(8192, 4, S), "wdad": wdad}
    plan = [(h, s, m) for h in range(2) for s in count for m in range(count[s])]
    tiles = Tiles(k, "g", ["v" if s in ("gnsa", "grwkv") else "a" for _, s, _ in plan])
    units = [START["in3", h] + first[s] + m // 2 for h, s, m in plan]
    pieces = Pieces(k, tiles.filled, [[(unit, m % 2)] for unit, (_, _, m) in zip(units, plan)])
    for n, unit in enumerate(units):
        k.used[unit] = (tiles.filled, n + 1)
    h_ready, rstd_in = k.sem("g_h_ready"), k.sem("rstd_in")
    sg_ready, gated = k.sem("sigmoid_gate_ready"), k.sem("gate_used")

    with nc.Block() as block:

        @block.sync
        def _(sp):
            sp.dma_start(rstd, io["rstd_keep"]).then_inc(rstd_in, 16)
            load_weights(k, sp, START["wout", 0] + RING)
            sp.wait_ge(gated, 16)
            sp.dma_start(io["mix_keep"], k.data(12544, 4096)).then_inc(k.spilled, 16)
            sp.dma_start(io["gate_keep"], k.data(17664, 4096)).then_inc(k.spilled, 16)

        @block.gpsimd
        def _(g):
            pieces.lower(g)

        @block.tensor
        def _(pe):
            for n, (h, s, m) in enumerate(plan):
                tiles.may_fill(pe, n)
                pieces.ready(pe, n)
                p = pieces.of_tile[n][0]
                pairs = [((pieces.hi(p)[:, t * P:(t + 1) * P], pieces.lo(p)[:, t * P:(t + 1) * P]),
                          (H[h][t], H[h][KT + t]), (h_ready, KT * h + t + 1) if (s, m) == ("gnsa", 0) else None)
                         for t in range(KT)]
                three_passes(pe, tiles.bank(n), pairs).then_inc(tiles.filled, 1)

        @block.scalar
        def _(a):
            gates = 0
            for n, (h, s, m) in enumerate(plan):
                tiles.may_read(a, n)
                if s in ("gnsa", "grwkv"):
                    if gates >= 2:
                        a.wait_ge(gated, gates - 1)
                    a.activation(sg[gates % 2], tiles.bank(n), ACT.Sigmoid).then_inc(sg_ready, 1)
                    gates += 1
                else:
                    tiles.read(a.copy(dest[s][:, m, h * HALF:(h + 1) * HALF], tiles.bank(n)), n)

        @block.vector
        def _(v):
            def normed(h, t):
                v.wait_ge(k.vec.sem, k.vec.inc(v.scalar_tensor_tensor(
                    whole[h][t], k.xT[:, t, h * HALF:(h + 1) * HALF], k.const("norm_g_2")[:, t:t + 1],
                    rstd[:, h * HALF:(h + 1) * HALF], ALU.mult, ALU.mult)))
                split_tile(k, v, H[h][t], H[h][KT + t], whole[h][t]).then_inc(h_ready, 1)

            v.wait_ge(rstd_in, 16)
            for t in range(KT):
                normed(0, t)
                if t == 1:
                    pieces.split_ahead(v, 0)
            v.wait_ge(k.spilled, 16)
            gates = 0
            for n, (h, s, m) in enumerate(plan):
                pieces.split_ahead(v, n)
                cols = slice(h * HALF, (h + 1) * HALF)
                if s in ("gnsa", "grwkv"):
                    v.wait_ge(sg_ready, gates + 1)
                    x = sg[gates % 2]
                    tiles.read(v.tensor_tensor(x, tiles.bank(n), x, ALU.mult), n)
                    v.wait_ge(tiles.emptied["v"], tiles.rank[n])
                    if s == "gnsa":
                        v.tensor_tensor(mixn[:, m, cols], mixn[:, m, cols], x, ALU.mult).then_inc(gated, 1)
                    else:
                        v.tensor_copy(gr[:, m, cols], x).then_inc(gated, 1)
                    gates += 1
                elif h == 0 and s in ("r3", "k3"):
                    v.wait_ge(tiles.filled, n)
                    normed(1, m + (4 if s == "k3" else 0))


def rwkv_phase(k):
    nc, io = k.nc, k.io
    r3, k3, v3 = k.data(0, 4, S), k.data(4096, 4, S), k.data(8192, 4, S)
    wdad = k.data(16640, S)
    low = lambda at, *shape: k.view(XT_AT + at, *shape)
    L, A, KK = low(0, 4, S), low(4096, 4, S), low(8192, 4, S)
    dd, t0, t1, t2, t3 = low(12288, 2, S), low(14336, HALF), low(14848, HALF), low(15360, HALF), low(15872, HALF)
    mask, level = k.view(CP_AT + CD["mask"][0], P), k.view(CP_AT + CD["level"][0], LEVELS, CHUNK)
    eye, up = k.view(CP_AT + CD["eye"][0], CHUNK), k.view(CP_AT + CD["up"][0], 512)
    resets = k.view(CP_AT + CD["resets"][0], S)
    place = [12544]

    def buf(*shape):
        at = place[0]
        place[0] += int(np.prod(shape))
        assert place[0] <= DA
        if len(shape) == 4:
            return k.data(at, shape[0] * shape[1], shape[2] * shape[3]).rearrange(
                "p (a b) (c d) -> p a b c d", a=shape[0], c=shape[2])
        return k.data(at, *shape)

    ra, bk = buf(2, 4, P), buf(2, 4, P)
    er, ek = buf(2, 4, CHUNK), buf(2, 4, CHUNK)
    mm = buf(2, 2, 4, P)
    mab = buf(2, 4, CHUNK)
    off = buf(2, LEVELS, 4, CHUNK)
    tt, gg = buf(1, 4, CHUNK), buf(2, 4, CHUNK)
    xx = buf(2, 4, CHUNK)
    bkt, uv = buf(2, 4, P), buf(2, 4, P)
    zv, zz, st = buf(2, 4, CHUNK), buf(1, 4, CHUNK), buf(1, 4, CHUNK)
    sem = k.sem
    shifts = [k3[:, m] for m in range(4)] + [wdad] + [x[:, m] for x in (r3, v3) for m in range(4)]
    mu_at = [4, 5, 6, 7, 12, 0, 1, 2, 3, 8, 9, 10, 11]
    mt = [(m, h) for m in range(4) for h in range(2)]

    diff_ready, shifted = sem("token_diff"), sem("token_shifted")
    tanh_done, wa_mm, wa_read = sem("tanh_done"), sem("decay_iclr_mm"), sem("decay_iclr_read")
    kq_ready, kn_mm, kn_root, kn_read = sem("kk_squares"), sem("kk_norm_mm"), sem("kk_norm_root"), sem("kk_norm_read")
    prep_done, resets_ready, iclr_read = sem("prep_done"), sem("resets_ready"), sem("iclr_read")

    def rows(e):
        return slice(64 * e, 64 * e + 64)

    with nc.Block() as block:

        @block.sync
        def _(sp):
            sp.dma_start(k.view(CP_AT, CD_N), io["consts_d"]).then_inc(k.cp_in, 16)
            sp.wait_ge(k.spilled, 48)

        @block.gpsimd
        def _(g):
            n = k.pool.inc(g.memset(resets, 1.0))
            g.wait_ge(k.pool.sem, n)
            g.memset(resets.rearrange("p (c t) -> p c t", t=CHUNK)[:, :, 0:1], 0.0).then_inc(resets_ready, 1)
            for i, x in enumerate(shifts):
                if i >= 2:
                    g.wait_ge(shifted, i - 1)
                d = dd[:, i % 2]
                g.tensor_tensor(d[:, 1:S], x[:, 0:S - 1], x[:, 1:S], ALU.subtract)
                g.tensor_scalar(d[:, 0:1], x[:, 0:1], -1.0, None, ALU.mult).then_inc(diff_ready, 1)
            g.wait_ge(kn_read, 8)
            for i, (m, h) in enumerate(mt):
                cols = slice(h * HALF, (h + 1) * HALF)
                g.wait_ge(iclr_read, i + 1)
                g.tensor_tensor(A[:, m, cols], A[:, m, cols], KK[:, m, cols], ALU.mult)

        @block.tensor
        def _(pe):
            for i in range(8):
                pe.wait_ge(kq_ready, i + 1)
                if i >= 2:
                    pe.wait_ge(kn_root, i - 1)
                pe.matmul(k.bank(4 + i % 2), k.const("bones"), (t0, t1)[i % 2], start=True, stop=True).then_inc(kn_mm, 1)
            pe.wait_ge(k.cp_in, 48)
            pe.wait_ge(tanh_done, 1)
            for i, (m, h) in enumerate(mt):
                cols = slice(h * HALF, (h + 1) * HALF)
                if i >= 2:
                    pe.wait_ge(wa_read, 2 * i - 2)
                pe.matmul(k.bank(2 * (i % 2)), up[0:64, m * P:(m + 1) * P], wdad[0:64, cols], start=True, stop=True)
                pe.matmul(k.bank(2 * (i % 2) + 1), up[64:128, m * P:(m + 1) * P], wdad[64:128, cols], start=True,
                          stop=True).then_inc(wa_mm, 1)

        @block.scalar
        def _(a):
            for i, (m, h) in enumerate(mt):
                a.wait_ge(kn_mm, i + 1)
                a.activation(L[:, m, h * HALF:(h + 1) * HALF], k.bank(4 + i % 2), ACT.Sqrt).then_inc(kn_root, 1)
            a.wait_ge(shifted, 5)
            a.activation(wdad[0:64], wdad[0:64], ACT.Tanh).then_inc(tanh_done, 1)
            w0, a0 = k.const("decay_w0_2"), k.const("iclr_a0_2")
            for i, (m, h) in enumerate(mt):
                cols = slice(h * HALF, (h + 1) * HALF)
                a.wait_ge(wa_mm, i + 1)
                a.activation(A[:, m, cols], k.bank(2 * (i % 2) + 1), ACT.Sigmoid,
                             bias=a0[:, m:m + 1]).then_inc(wa_read, 1)
                a.wait_ge(kn_read, i + 1)
                a.activation(L[:, m, cols], k.bank(2 * (i % 2)), ACT.Sigmoid, bias=w0[:, m:m + 1]).then_inc(wa_read, 1)

        @block.vector
        def _(v):
            def step(ins):
                v.wait_ge(k.vec.sem, k.vec.inc(ins))

            mu, kk_, ka = k.const("shift_mu_2"), k.const("k_k_2"), k.const("k_a_2")

            def shift(i):
                x = shifts[i]
                v.wait_ge(diff_ready, i + 1)
                v.scalar_tensor_tensor(x, dd[:, i % 2], mu[:, mu_at[i]:mu_at[i] + 1], x, ALU.mult,
                                       ALU.add).then_inc(shifted, 1)

            def square(i):
                m, h = mt[i]
                cols = slice(h * HALF, (h + 1) * HALF)
                v.wait_ge(shifted, m + 1)
                step(v.tensor_scalar(KK[:, m, cols], k3[:, m, cols], kk_[:, m:m + 1], None, ALU.mult))
                if i >= 2:
                    v.wait_ge(kn_mm, i - 1)
                v.tensor_tensor((t0, t1)[i % 2], KK[:, m, cols], KK[:, m, cols], ALU.mult).then_inc(kq_ready, 1)

            def normalise(i):
                m, h = mt[i]
                cols = slice(h * HALF, (h + 1) * HALF)
                v.wait_ge(kn_root, i + 1)
                root = L[:, m, cols]
                step(v.tensor_scalar(root, root, 1e-12, None, ALU.max))
                step(v.reciprocal(root, root))
                v.tensor_tensor(KK[:, m, cols], KK[:, m, cols], root, ALU.mult).then_inc(kn_read, 1)

            for i in range(4):
                shift(i)
                square(2 * i)
                square(2 * i + 1)
            shift(4)
            for i in range(8):
                normalise(i)
                shift(5 + i)
            v.wait_ge(resets_ready, 1)
            for m in range(4):
                v.wait_ge(wa_read, 4 * m + 4)
                v.tensor_tensor_scan(L[:, m], resets, L[:, m], 0.0, ALU.mult, ALU.add).then_inc(prep_done, 1)
                for h in range(2):
                    cols = slice(h * HALF, (h + 1) * HALF)
                    v.tensor_scalar((t2, t3)[h], A[:, m, cols], 1.0, ka[:, m:m + 1], ALU.subtract,
                                    ALU.mult).then_inc(iclr_read, 1)
                    v.wait_ge(iclr_read, 2 * m + h + 1)
                    step(v.scalar_tensor_tensor(k3[:, m, cols], (t2, t3)[h], 1.0, k3[:, m, cols], ALU.add, ALU.mult))
            v.nop().then_inc(prep_done, 1)

    exp_ready, ops_ready, raw_mm, mm_ready, mab_ready = (sem("chunk_exp"), sem("chunk_operands"), sem("chunk_raw"),
                                                         sem("chunk_masked"), sem("chunk_mab"))
    off_ready, turn_mm, turn_read, zv_mm, zv_ready = (sem("chunk_levels"), sem("chunk_turned"), sem("chunk_turned_read"),
                                                      sem("chunk_zv_mm"), sem("chunk_zv"))
    x_mm, x_ready, w_mm, t_ready, g_ready = ([sem(f"{name}{i}") for i in range(2)] for name in (
        "inv_x_mm", "inv_x", "inv_w_mm", "inv_t", "inv_g"))
    x_bank, w_bank, G = (2, 4), (3, 7), (slice(0, 2), slice(2, 4))
    zs_mm, z_ready, u_mm, u_ready, y_mm, y_read, s_mm, s_ready = (
        sem("chunk_zs_mm"), sem("chunk_z"), sem("chunk_u_mm"), sem("chunk_u"), sem("chunk_y_mm"), sem("chunk_y"),
        sem("chunk_s_mm"), sem("chunk_state"))
    C = NCHUNK

    def at(c):
        return slice(c * CHUNK, (c + 1) * CHUNK)

    def four(b, width=CHUNK):
        return k.bank(b, 4 * width).rearrange("p (m c) -> p m c", m=4)

    def half(b, at):
        return k.bank(b)[:, at:at + 2 * CHUNK].rearrange("p (m c) -> p m c", m=2)

    def bc(x, n=4):
        return x.unsqueeze(1).to_broadcast((x.shape[0], n, x.shape[1]))

    with nc.Block() as block:

        @block.tensor
        def _(pe):
            ident = k.const("ident")

            def pairs(bank, lhs, rhs):
                for m in range(4):
                    for e in range(2):
                        last = pe.matmul(four(bank)[rows(e), m], lhs(m, e), rhs(m, e), start=True, stop=True)
                return last

            def group_pairs(i, bank, at, lhs, rhs):
                out = k.bank(bank)[:, at:at + 2 * CHUNK].rearrange("p (m c) -> p m c", m=2)
                for m in range(2):
                    for e in range(2):
                        last = pe.matmul(out[rows(e), m], lhs(2 * i + m, e), rhs(2 * i + m, e), start=True, stop=True)
                return last

            def raw(c):
                pe.wait_ge(ops_ready, c + 1)
                if c >= 1:
                    pe.wait_ge(zv_ready, c)
                    pe.wait_ge(turn_read, 2 * c)
                for e in range(2):
                    for m in range(4):
                        last = pe.matmul(four(e, P)[:, m], bk[rows(e), c % 2, m], ra[rows(e), c % 2, m], start=True,
                                         stop=True)
                last.then_inc(raw_mm, 1)

            def turn(c):
                pe.wait_ge(mm_ready, 2 * c + 2)
                for m in range(4):
                    last = pe.transpose(four(0, P)[:, m], bk[:, c % 2, m], ident)
                last.then_inc(turn_mm, 1)
                for m in range(4):
                    vt = k.data(8192 + m * S + c * CHUNK - CHUNK, P)
                    last = pe.transpose(four(1, P)[:, m], vt, ident)
                last.then_inc(turn_mm, 1)

            def value_part(c):
                pe.wait_ge(turn_read, 2 * c + 2)
                pairs(0, lambda m, e: mm[64:128, c % 2, e, m, 64:128],
                      lambda m, e: uv[64:128, c % 2, m, 64 * e:64 * e + 64]).then_inc(zv_mm, 1)

            def inv_x(c, l):
                pe.wait_ge(off_ready, LEVELS * c + l + 1)
                for i in range(2):
                    if l == 0:
                        last = group_pairs(i, x_bank[i], 0, lambda m, e: off[rows(e), c % 2, 0, m],
                                           lambda m, e: eye[rows(e)])
                    else:
                        pe.wait_ge(t_ready[i], (LEVELS - 1) * c + l)
                        last = group_pairs(i, x_bank[i], 0, lambda m, e: off[rows(e), c % 2, l, m],
                                           lambda m, e: tt[rows(e), 0, m])
                    last.then_inc(x_mm[i], 1)

            def inv_w(c, l):
                for i in range(2):
                    pe.wait_ge(x_ready[i], (LEVELS - 1) * c + l)
                    pe.wait_ge(g_ready[i], LEVELS * c + l)
                    if l < LEVELS - 1:
                        group_pairs(i, w_bank[i], 0, lambda m, e: gg[rows(e), c % 2, m],
                                    lambda m, e: xx[rows(e), l % 2, m])
                    group_pairs(i, w_bank[i], 2 * CHUNK, lambda m, e: xx[rows(e), l % 2, m],
                                lambda m, e: gg[rows(e), c % 2, m]).then_inc(w_mm[i], 1)

            def state_part(c):
                if c >= 1:
                    pe.wait_ge(s_ready, c)
                pairs(5, lambda m, e: ra[rows(e), c % 2, m, 64:128], lambda m, e: st[rows(e), 0, m]).then_inc(zs_mm, 1)

            def solve(c):
                pe.wait_ge(z_ready, c + 1)
                for i in range(2):
                    pe.wait_ge(g_ready[i], LEVELS * (c + 1))
                if c >= 1:
                    pe.wait_ge(y_read, c)
                pairs(6, lambda m, e: gg[rows(e), c % 2, m], lambda m, e: zz[rows(e), 0, m]).then_inc(u_mm, 1)

            def outputs(c):
                pe.wait_ge(u_ready, 2 * c + 2)
                for m in range(4):
                    for e in range(2):
                        last = pe.matmul(four(5)[rows(e), m], bkt[:, c % 2, m, rows(e)], uv[:, c % 2, m, rows(e)],
                                         start=True, stop=True)
                last.then_inc(s_mm, 1)
                for m in range(4):
                    for e in range(2):
                        pe.matmul(four(6)[rows(e), m], st[rows(e), 0, m], ra[rows(e), c % 2, m, 0:64], start=True,
                                  stop=False)
                        last = pe.matmul(four(6)[rows(e), m], uv[:, c % 2, m, rows(e)], mm[:, c % 2, e, m, 0:64],
                                         start=False, stop=True)
                last.then_inc(y_mm, 1)

            raw(0)
            for c in range(C + 1):
                if c >= 1:
                    state_part(c - 1)
                if c < C:
                    inv_x(c, 0)
                    turn(c)
                if c >= 1:
                    solve(c - 1)
                if c < C:
                    inv_x(c, 1)
                    value_part(c)
                    inv_w(c, 1)
                if c >= 1:
                    outputs(c - 1)
                if c < C:
                    for l in range(2, LEVELS):
                        inv_x(c, l)
                        inv_w(c, l)
                        if l == 3 and c + 1 < C:
                            raw(c + 1)

        @block.scalar
        def _(a):
            a.wait_ge(prep_done, 5)

            def exps(c):
                if c >= 2:
                    a.wait_ge(ops_ready, c - 1)
                    a.wait_ge(s_ready, c - 1)
                a.activation(er[:, c % 2], L[:, :, at(c)], ACT.Exp, scale=-DECAY)
                a.activation(ek[:, c % 2], L[:, :, at(c)], ACT.Exp, scale=DECAY).then_inc(exp_ready, 1)

            def both_heads(c):
                a.wait_ge(mm_ready, 2 * c + 2)
                if c >= 2:
                    a.wait_ge(off_ready, LEVELS * (c - 1))
                a.copy(mab[0:64, c % 2], mm[0:64, c % 2, 0, :, 64:128])
                a.copy(mab[64:128, c % 2], mm[0:64, c % 2, 1, :, 64:128]).then_inc(mab_ready, 1)

            exps(0)
            both_heads(0)
            for c in range(C + 1):
                if c < C:
                    a.wait_ge(turn_mm, 2 * c + 1)
                    if c >= 2:
                        a.wait_ge(y_mm, c - 1)
                    a.copy(bkt[:, c % 2], four(0, P)).then_inc(turn_read, 1)
                    a.wait_ge(turn_mm, 2 * c + 2)
                    a.copy(uv[64:128, c % 2], four(1, P)[64:128]).then_inc(turn_read, 1)
                if c >= 1:
                    a.wait_ge(u_mm, c)
                    for e in range(2):
                        a.copy(uv[0:64, (c - 1) % 2, :, rows(e)], four(6)[rows(e)]).then_inc(u_ready, 1)
                if c < C:
                    for l in range(1, LEVELS):
                        n = (LEVELS - 1) * c + l
                        for i in range(2):
                            a.wait_ge(x_mm[i], LEVELS * c + l + 1)
                            if n > 2:
                                a.wait_ge(w_mm[i], n - 2)
                            a.copy(xx[:, l % 2, G[i]], half(x_bank[i], 0)).then_inc(x_ready[i], 1)
                        if l == 2 and c >= 1:
                            a.wait_ge(y_mm, c)
                            a.copy(A[:, :, at(c - 1)], four(6)).then_inc(y_read, 1)
                        if l == 2 and c + 1 < C:
                            exps(c + 1)
                        if l == 4 and c + 1 < C:
                            both_heads(c + 1)
                else:
                    a.wait_ge(y_mm, c)
                    a.copy(A[:, :, at(c - 1)], four(6)).then_inc(y_read, 1)

        @block.vector
        def _(v):
            def step(ins):
                v.wait_ge(k.vec.sem, k.vec.inc(ins))

            step(v.memset(st, 0.0))

            def combine(c):
                v.wait_ge(zs_mm, c + 1)
                v.wait_ge(zv_ready, c + 1)
                if c >= 1:
                    v.wait_ge(u_mm, c)
                v.tensor_tensor(zz[:, 0], four(5), zv[:, c % 2], ALU.add).then_inc(z_ready, 1)

            def next_state(c):
                v.wait_ge(s_mm, c + 1)
                v.wait_ge(y_mm, c + 1)
                step(v.tensor_tensor(st[:, 0], st[:, 0], four(5), ALU.add))
                v.tensor_tensor(st[:, 0], st[:, 0], er[:, c % 2, :, CHUNK - 1:CHUNK].to_broadcast((P, 4, CHUNK)),
                                ALU.mult).then_inc(s_ready, 1)

            def masked(c):
                v.wait_ge(raw_mm, c + 1)
                if c >= 2:
                    v.wait_ge(y_mm, c - 1)
                for e in range(2):
                    v.tensor_tensor(mm[:, c % 2, e], four(e, P), bc(mask), ALU.mult).then_inc(mm_ready, 1)

            masked(0)
            for c in range(C + 1):
                if c >= 1:
                    combine(c - 1)
                if c < C:
                    v.wait_ge(off_ready, LEVELS * c + 1)
                    for i in range(2):
                        v.tensor_tensor(gg[:, c % 2, G[i]], off[:, c % 2, 0, G[i]], bc(eye, 2),
                                        ALU.add).then_inc(g_ready[i], 1)
                    for i in range(2):
                        v.wait_ge(x_mm[i], LEVELS * c + 1)
                        v.tensor_tensor(tt[:, 0, G[i]], half(x_bank[i], 0), bc(eye, 2), ALU.add).then_inc(t_ready[i], 1)
                    v.wait_ge(zv_mm, c + 1)
                    v.tensor_copy(zv[:, c % 2], four(0)).then_inc(zv_ready, 1)
                    for l in range(1, LEVELS):
                        for i in range(2):
                            v.wait_ge(w_mm[i], (LEVELS - 1) * c + l)
                            if l < LEVELS - 1:
                                v.wait_ge(t_ready[i], (LEVELS - 1) * c + l)
                                v.tensor_tensor(tt[:, 0, G[i]], tt[:, 0, G[i]], half(w_bank[i], 0),
                                                ALU.add).then_inc(t_ready[i], 1)
                            v.wait_ge(g_ready[i], LEVELS * c + l)
                            v.tensor_tensor(gg[:, c % 2, G[i]], gg[:, c % 2, G[i]], half(w_bank[i], 2 * CHUNK),
                                            ALU.add).then_inc(g_ready[i], 1)
                        if l == 1 and c >= 1:
                            next_state(c - 1)
                        if l == 3 and c + 1 < C:
                            masked(c + 1)
                else:
                    next_state(c - 1)

        @block.gpsimd
        def _(g):
            def operands(c):
                g.wait_ge(exp_ready, c + 1)
                if c >= 2:
                    g.wait_ge(y_mm, c - 1)
                    g.wait_ge(turn_read, 2 * c - 3)
                o = ra[:, c % 2]
                g.tensor_tensor(o[:, :, 0:64], r3[:, :, at(c)], er[:, c % 2], ALU.mult)
                g.tensor_scalar(o[:, :, 64:65], KK[:, :, c * CHUNK:c * CHUNK + 1], -1.0, None, ALU.mult)
                n = k.pool.inc(g.tensor_scalar(er_neg, er[:, c % 2], -1.0, None, ALU.mult))
                g.wait_ge(k.pool.sem, n)
                k.pool.inc(g.tensor_tensor(o[:, :, 65:128], KK[:, :, c * CHUNK + 1:(c + 1) * CHUNK],
                                           er_neg[:, :, 0:63], ALU.mult))
                o = bk[:, c % 2]
                g.tensor_tensor(o[:, :, 0:64], A[:, :, at(c)], ek[:, c % 2], ALU.mult)
                g.tensor_tensor(o[:, :, 64:128], k3[:, :, at(c)], ek[:, c % 2], ALU.mult).then_inc(ops_ready, 1)
                g.wait_ge(k.pool.sem, k.pool.n)

            er_neg = low(12288, 4, CHUNK)
            operands(0)
            for c in range(C):
                g.wait_ge(mab_ready, c + 1)
                for l in range(LEVELS):
                    if c >= 2:
                        g.wait_ge(x_mm[1], LEVELS * (c - 1))
                    g.tensor_tensor(off[:, c % 2, l], mab[:, c % 2], bc(level[:, l]), ALU.mult).then_inc(off_ready, 1)
                if c + 1 < C:
                    operands(c + 1)

    gate_in, k.mix_in = sem("gate_in"), sem("mix_in")
    q1_ready, mean_mm, d_ready, q2_ready, var_mm, root2 = (sem("y_mean_in"), sem("y_mean_mm"), sem("y_centred"),
                                                           sem("y_var_in"), sem("y_var_mm"), sem("y_root"))
    bo_in, bo_mm, done = sem("bonus_in"), sem("bonus_mm"), sem("recurrent_done")
    gr, sq2, bon = k.data(12544, 4, S), k.data(16640, 2, HALF), k.data(17664, 2, HALF)
    rr, cc = k.data(18688, 2, HALF), k.data(19712, 2, HALF)

    with nc.Block() as block:

        @block.sync
        def _(sp):
            sp.dma_start(k.data(12544, 4096), io["gate_keep"]).then_inc(gate_in, 16)
            sp.dma_start(k.view(HT_AT, 4096), io["mix_keep"]).then_inc(k.mix_in, 16)

        @block.tensor
        def _(pe):
            def mean(i):
                m, h = mt[i]
                if i >= 2:
                    pe.wait_ge(d_ready, i - 1)
                pe.matmul(k.bank(i % 2), k.const("bones"), A[:, m, h * HALF:(h + 1) * HALF], start=True,
                          stop=True).then_inc(mean_mm, 1)

            mean(0)
            for i in range(8):
                if i + 1 < 8:
                    mean(i + 1)
                pe.wait_ge(q2_ready, i + 1)
                if i >= 2:
                    pe.wait_ge(root2, i - 1)
                pe.matmul(k.bank(2 + i % 2), k.const("bones"), sq2[:, i % 2], start=True, stop=True).then_inc(var_mm, 1)
                pe.wait_ge(bo_in, i + 1)
                if i >= 2:
                    pe.wait_ge(done, i - 1)
                pe.matmul(k.bank(4 + i % 2), k.const("bones"), bon[:, i % 2], start=True, stop=True).then_inc(bo_mm, 1)

        @block.scalar
        def _(a):
            for i in range(8):
                a.wait_ge(var_mm, i + 1)
                if i >= 2:
                    a.wait_ge(done, i - 1)
                a.activation(rr[:, i % 2], k.bank(2 + i % 2), ACT.Sqrt, bias=k.gn_eps, scale=1.0 / HD).then_inc(root2, 1)

        @block.gpsimd
        def _(g):
            rk = k.const("r_k_2")
            for i, (m, h) in enumerate(mt):
                cols = slice(h * HALF, (h + 1) * HALF)
                if i >= 2:
                    g.wait_ge(bo_mm, i - 1)
                n = k.pool.inc(g.tensor_tensor(bon[:, i % 2], r3[:, m, cols], k3[:, m, cols], ALU.mult))
                g.wait_ge(k.pool.sem, n)
                g.tensor_scalar(bon[:, i % 2], bon[:, i % 2], rk[:, m:m + 1], None, ALU.mult).then_inc(bo_in, 1)
                g.wait_ge(d_ready, i + 1)
                if i >= 2:
                    g.wait_ge(var_mm, i - 1)
                g.wait_ge(bo_in, i + 1)
                g.tensor_tensor(sq2[:, i % 2], cc[:, i % 2], cc[:, i % 2], ALU.mult).then_inc(q2_ready, 1)

        @block.vector
        def _(v):
            def step(ins):
                v.wait_ge(k.vec.sem, k.vec.inc(ins))

            gw, gb = k.const("gn_w_2"), k.const("gn_b_2")

            def centre(i):
                m, h = mt[i]
                v.wait_ge(mean_mm, i + 1)
                if i >= 2:
                    v.wait_ge(done, i - 1)
                    v.wait_ge(q2_ready, i - 1)
                v.scalar_tensor_tensor(cc[:, i % 2], k.bank(i % 2), -1.0 / HD, A[:, m, h * HALF:(h + 1) * HALF],
                                       ALU.mult, ALU.add).then_inc(d_ready, 1)

            centre(0)
            v.wait_ge(gate_in, 16)
            for i, (m, h) in enumerate(mt):
                cols = slice(h * HALF, (h + 1) * HALF)
                if i + 1 < 8:
                    centre(i + 1)
                v.wait_ge(root2, i + 1)
                x, c_ = rr[:, i % 2], cc[:, i % 2]
                step(v.reciprocal(x, x))
                step(v.tensor_tensor(c_, c_, x, ALU.mult))
                step(v.tensor_scalar(c_, c_, gw[:, m:m + 1], gb[:, m:m + 1], ALU.mult, ALU.add))
                v.wait_ge(bo_mm, i + 1)
                step(v.tensor_tensor(x, k.bank(4 + i % 2), v3[:, m, cols], ALU.mult))
                step(v.tensor_tensor(c_, c_, x, ALU.add))
                v.tensor_tensor(gr[:, m, cols], gr[:, m, cols], c_, ALU.mult).then_inc(done, 1)


def output_phase(k):
    nc, io = k.nc, k.io
    mixr, mixn, hi = k.data(12544, 4, S), k.view(HT_AT, 4, S), k.data_part(4096, 8, S)
    mixr_lo, mixn_lo = k.data_part(12544, 4, S), k.part(HT_AT, 4, S)
    sq, acc, root, rstd, _ = norm_scratch(k)
    plan = [(h, m) for h in range(2) for m in range(8)]
    tiles = Tiles(k, "out", ["v"] * 16)
    units = [START["wout", h] + m // 2 for h, m in plan]
    pieces = Pieces(k, tiles.filled, [[(unit, m % 2)] for unit, (_, m) in zip(units, plan)])
    for n, unit in enumerate(units):
        k.used[unit] = (tiles.filled, n + 1)
    ss_ready, ss_done, root_done = k.sem("out_ss_ready"), k.sem("out_ss_done"), k.sem("out_root_done")
    mix_in, x_in, out_ready, stored = k.mix_in, k.sem("x_back"), k.sem("out_ready"), k.sem("stored")
    mix_split = k.sem("mixes_split")

    with nc.Block() as block:

        @block.sync
        def _(sp):
            sp.dma_start(k.view(XT_AT, 8192), io["x_keep"]).then_inc(x_in, 16)
            load_weights(k, sp, START["end"])
            for i in range(16):
                h, m = i // 8, i % 8
                sp.wait_ge(out_ready, i + 1)
                sp.dma_start(io["out"].rearrange("(t p) s -> p t s", p=P)[:, m, h * HALF:(h + 1) * HALF],
                             k.xT[:, m, h * HALF:(h + 1) * HALF]).then_inc(stored, 16)
            sp.wait_ge(stored, 16 * 16)

        @block.gpsimd
        def _(g):
            pieces.lower(g)

        @block.tensor
        def _(pe):
            order = list(range(4, 8)) + list(range(4))
            for n, (h, m) in enumerate(plan):
                tiles.may_fill(pe, n)
                pieces.ready(pe, n)
                p = pieces.of_tile[n][0]
                pairs = []
                for i, t in enumerate(order):
                    x = (mixn_lo if t < 4 else mixr_lo)[:, t % 4, h * HALF:(h + 1) * HALF]
                    pairs.append(((pieces.hi(p)[:, t * P:(t + 1) * P], pieces.lo(p)[:, t * P:(t + 1) * P]),
                                  (hi[:, t, h * HALF:(h + 1) * HALF], x), (mix_split, 8 * h + i + 1) if m == 0 else None))
                three_passes(pe, tiles.bank(n), pairs).then_inc(tiles.filled, 1)
                if n in (9, 15):
                    pe.wait_ge(ss_ready, 1 if n == 9 else 2)
                    pe.matmul(k.bank(5), k.const("ones"), acc, start=True, stop=True).then_inc(ss_done, 1)

        @block.scalar
        def _(a):
            for h in range(2):
                a.wait_ge(ss_done, h + 1)
                if h:
                    a.wait_ge(out_ready, 1)
                a.activation(root, k.bank(5), ACT.Sqrt, bias=k.eps, scale=1.0 / D).then_inc(root_done, 1)

        @block.vector
        def _(v):
            g = k.const("final_g_2")

            def split(h, i):
                t = (i + 4) % 8
                if t == 0:
                    v.wait_ge(mix_in, 16)
                at_ = (slice(None), t % 4, slice(h * HALF, (h + 1) * HALF))
                lo, x = ((mixn_lo, mixn) if t < 4 else (mixr_lo, mixr))
                split_tile(k, v, hi[:, t, h * HALF:(h + 1) * HALF], lo[at_], x[at_]).then_inc(mix_split, 1)

            pieces.split_ahead(v, 0)
            for i in range(8):
                split(0, i)
            v.wait_ge(x_in, 16)
            for n, (h, m) in enumerate(plan):
                pieces.split_ahead(v, n)
                if h == 0:
                    split(1, m)
                cols = slice(h * HALF, (h + 1) * HALF)
                x = k.xT[:, m, cols]
                tiles.may_read(v, n)
                tiles.read(v.tensor_tensor(x, x, tiles.bank(n), ALU.add), n)
                v.wait_ge(tiles.emptied["v"], n + 1)
                last = k.vec.inc(v.tensor_tensor(sq[m % 2], x, x, ALU.mult))
                v.wait_ge(k.vec.sem, last)
                if m == 0:
                    if h:
                        v.wait_ge(ss_done, 1)
                    last = k.vec.inc(v.tensor_copy(acc, sq[0]))
                else:
                    last = k.vec.inc(v.tensor_tensor(acc, acc, sq[m % 2], ALU.add))
                v.wait_ge(k.vec.sem, last)
                if m == 7:
                    v.nop().then_inc(ss_ready, 1)
                if n in (9, 15):
                    half = slice(0, HALF) if n == 9 else slice(HALF, S)
                    v.wait_ge(root_done, 1 if n == 9 else 2)
                    v.wait_ge(k.vec.sem, k.vec.inc(v.reciprocal(rstd, root)))
                    for t in range(KT):
                        v.scalar_tensor_tensor(k.xT[:, t, half], k.xT[:, t, half], g[:, t:t + 1], rstd, ALU.mult,
                                               ALU.mult).then_inc(out_ready, 1)


KEPT = {"x_keep": 8192, "mix_keep": 4096, "gate_keep": 4096, "gates_keep": 16384, "rstd_keep": 1024}

def pack(inputs):
    f = {n: np.asarray(a) for n, a in inputs.items()}
    z = np.float32

    def cols(w, c0, n=256):
        b = np.zeros((w.shape[0], 256), z)
        b[:, :n] = w[:, c0:c0 + n]
        return b.reshape(-1, P, 256).transpose(1, 0, 2).reshape(P, -1)

    def tiles(w, c0, n=256):
        return cols(w, c0, n).reshape(P, -1, 2, P).transpose(0, 2, 1, 3).reshape(P, -1)

    w = f["w_in"][0]
    blocks = {}
    for i, part in enumerate(("q", "k", "v", "cb", "cc", "cu")):
        for j in range(2):
            blocks[part, j] = (cols if part == "v" else tiles)(w, i * 512 + j * 256)
    for j in range(4):
        blocks["ga", j] = tiles(w, 3072 + j * 256)
        blocks["gc", j] = tiles(w, 4096 + j * 256)
        both = np.concatenate([f["w_attn_out"][0], f["w_conv_out"][0]], 0)
        blocks["aoco", j] = tiles(both, j * 256)
        blocks["wo", j] = tiles(f["w_o"][0], j * 256)
        blocks["gate", j] = tiles(f["w_ple_gate"][0], j * 256)
    for j in range(16):
        blocks["up", j] = tiles(f["w_up"][0], j * 256)
        part = D * (j // 4)
        blocks["down", j] = tiles(f["w_down"][0][part:part + D], (j % 4) * 256)
    blocks["pp", 0] = f["w_ple_proj"][0].reshape(2, P, D).transpose(1, 0, 2).reshape(P, -1)

    order = np.concatenate([np.r_[j * 64:(j + 1) * 64, (4 + j) * 64:(5 + j) * 64] for j in range(4)])
    w = f["w_in_2"][0]
    w2 = {"q": w[:, 0:512][:, order], "kc": w[:, 512:640], "vc": w[:, 640:768], "ks": w[:, 768:896],
          "vs": w[:, 896:1024], "kw": w[:, 1024:1152], "vw": w[:, 1152:1280], "gl": w[:, 1280:1304],
          "gnsa": w[:, 1304:1816][:, order], "r": w[:, 1816:2328], "k": w[:, 2328:2840], "v": w[:, 2840:3352],
          "wdad": w[:, 3352:3480], "grwkv": w[:, 3480:3992]}
    for j in range(2):
        blocks["q2", j] = tiles(w2["q"], j * 256)
        blocks["gnsa", j] = tiles(w2["gnsa"], j * 256)
        blocks["grwkv", j] = tiles(w2["grwkv"], j * 256)
        for part in "rkv":
            blocks[part + "3", j] = tiles(w2[part], j * 256)
    blocks["kcvc", 0] = tiles(np.concatenate([w2["kc"], w2["vc"]], 1), 0)
    blocks["kskw", 0] = tiles(np.concatenate([w2["ks"], w2["kw"]], 1), 0)
    blocks["vsvw", 0] = cols(np.concatenate([w2["vs"], w2["vw"]], 1), 0)
    gl = w2["gl"].reshape(D, 2, 4, 3).transpose(0, 3, 2, 1).reshape(D, 24)
    blocks["gl", 0] = cols(gl, 0, 24)
    blocks["wdad", 0] = tiles(w2["wdad"], 0, 128)
    for name in "kv":
        w1 = f[f"cmp_w1_{name}_2"][0].reshape(16, P, 256)
        for j in range(2):
            blocks["w1" + name, j] = w1[8 * j:8 * j + 8].transpose(1, 0, 2).reshape(P, -1)
    wout = f["w_out_2"][0]
    wout = np.concatenate([wout[:512][order], wout[512:]], 0)
    for j in range(4):
        blocks["wout", j] = tiles(wout, j * 256)
    weights = np.stack([blocks[n] for n in BLOCKS])

    def col(a):
        return np.asarray(a).reshape(-1, P).T

    c = np.zeros((P, CA_N), z)

    def put(name, a):
        at, n = CA[name]
        c[:, at:at + n] = a

    put("ident", np.eye(P, dtype=z))
    put("ones", np.ones((P, P), z))
    put("bones", np.kron(np.eye(2, dtype=z), np.ones((64, 64), z)))
    for name in ("g_pre_mix", "b_gate", "g_post_mix", "g_pre_mlp", "g_post_mlp", "g_ple", "norm_g_2", "shift_mu_2",
                 "decay_w0_2", "iclr_a0_2", "k_k_2", "k_a_2", "r_k_2", "gn_w_2", "gn_b_2"):
        put(name, col(f[name][0]))
    put("final_g_2", col(f["final_g_2"]))
    put("w_conv", f["w_conv"][0].reshape(3, 4, P).transpose(2, 0, 1).reshape(P, 12))
    for name in "kv":
        put("pos_" + name, f[f"cmp_pos_{name}_2"][0].reshape(16, P).T)
        put("w2" + name, f[f"cmp_w2_{name}_2"][0].reshape(2, P, 64).transpose(1, 0, 2).reshape(P, 128))
    tri = np.zeros((P, CB_N), z)
    tri[:, :P] = -np.tril(np.ones((P, P), z))
    tri[:, P:] = -1.0
    pos, blk = np.arange(S), np.arange(16)
    cc = np.zeros((P, CC_N), z)

    def put_c(name, a):
        at, n = CC[name]
        cc[:, at:at + n] = np.asarray(a, z).reshape(-1, n)

    qi, ki = np.arange(P)[:, None], np.arange(P)[None, :]
    put_c("causal", np.where(ki <= qi, 0.0, NEG))
    wk = np.arange(640)[None, :] - 512
    put_c("window", np.where((qi - wk >= 0) & (qi - wk < 512), 0.0, NEG))
    ends = np.r_[np.arange(CMP_N) * 16 + 31, 1 << 20]
    keep = (ends[None, None, :] <= pos.reshape(8, P).T[:, :, None])
    put_c("cmp_add", np.where(keep, 0.0, NEG))
    put_c("cmp_keep", keep)
    tb = (pos // 64).reshape(8, P).T[:, 4:, None]
    forced = (blk == 0) | (blk == tb) | (blk == tb - 1)
    put_c("imp_keep", blk <= tb)
    put_c("imp_add", np.where(blk <= tb, 1e3 * forced, -1.0))
    put_c("overlap", np.tile(np.array([1, 1, 1, 0.5]), 16))
    put_c("earlier", (blk[None, :] < blk[:, None]).reshape(1, 256))
    swap = np.zeros((P, P), z)
    for base in (0, 64):
        for i in range(8):
            swap[base + i + 8, base + i] = swap[base + i, base + i + 8] = 1.0
    put_c("swap", swap)
    inv = np.float32(500000.0) ** (-np.arange(8, dtype=z) / np.float32(8))
    ang = pos.astype(z)[None, :] * inv.astype(z)[:, None]
    cos, sin = np.ones((64, S), z), np.zeros((64, S), z)
    cos[0:8] = cos[8:16] = np.cos(ang)
    sin[0:8], sin[8:16] = -np.sin(ang), np.sin(ang)
    rope = np.concatenate([np.tile(cos, (2, 1)), np.tile(sin, (2, 1))], 1)
    cd = np.zeros((P, CD_N), z)
    j, t = np.arange(64)[:, None], np.arange(64)[None, :]
    cd[:, :P] = np.tile(np.concatenate([t >= j, t > j], 1), (2, 1))
    at = CD["level"][0]
    for lv in range(LEVELS):
        s2 = 2 << lv
        here = (j // s2 == t // s2) & (j % s2 < s2 // 2) & (t % s2 >= s2 // 2)
        cd[:, at + lv * 64:at + (lv + 1) * 64] = np.tile(here, (2, 1))
    cd[:, CD["eye"][0]:CD["eye"][0] + 64] = np.tile(np.eye(64), (2, 1))
    cd[:, CD["up"][0]:CD["up"][0] + 512] = np.concatenate([f["decay_up_2"][0], f["iclr_up_2"][0]], 0)
    return {
        "consts_d": cd, "consts_c": cc, "rope": rope, "weights": weights, "consts": c, "consts_b": tri,
        "xT": np.ascontiguousarray(f["x"][0].T), "pT": np.ascontiguousarray(f["p"][0, 0].T),
    }


def kernel(**inputs):
    import concourse.bacc as bacc
    from concourse.bass_utils import run_bass_kernel_spmd

    nc = bacc.Bacc("TRN2", target_bir_lowering=False, num_devices=1)
    arrays = {"in_" + name: a for name, a in pack(inputs).items()}
    io = {name[3:]: nc.dram_tensor(name, a.shape, F32, kind="ExternalInput").ap() for name, a in arrays.items()}
    for name, n in KEPT.items():
        io[name] = nc.dram_tensor(name, (P, n), F32, kind="Internal").ap()
    io["out"] = nc.dram_tensor("out_T", (D, S), F32, kind="ExternalOutput").ap()
    build(nc, io)
    result = run_bass_kernel_spmd(nc, [arrays], core_ids=[0])
    return np.ascontiguousarray(result.results[0]["out_T"].T)[None]
```
